# Optimizing a Trainium2 kernel written in Bass

```python
import jax, jax.numpy as jnp
from jax import lax
import numpy as np
import math

D_MODEL = 1024
BATCH = 1
SEQ = 512
DEPTH = 1

HEAD_DIM = 64
HEADS_PER_GROUP = 4
DILATED_GROUPS = ((128, 1), (512, 4), (2048, 16))
N_GROUPS = len(DILATED_GROUPS)
N_ATTN_HEADS = N_GROUPS * HEADS_PER_GROUP
ATTN_WIDTH = N_ATTN_HEADS * HEAD_DIM
ATTN_OUT_WIDTH = HEADS_PER_GROUP * HEAD_DIM
ROT_DIM = HEAD_DIM // 4
ROPE_THETA = 500000.0
BLOCK = 128
POOL_WINDOWS = (2, 4, 8, 16)
POOL_GROUP_WIDTH = 128
POOL_WIDTH = len(POOL_WINDOWS) * POOL_GROUP_WIDTH
N_BRANCHES = 2
IN_WIDTH = 3 * ATTN_WIDTH + POOL_WIDTH + N_BRANCHES * D_MODEL
D_FF = 2816
RMS_EPS = 1e-6


def rms_norm(x, g):
    xf = x.astype(jnp.float32)
    y = xf * lax.rsqrt(jnp.mean(xf * xf, axis=-1, keepdims=True) + RMS_EPS)
    return (y * g.astype(jnp.float32)).astype(x.dtype)

def swiglu(x, w1, w3, w2):
    return (jax.nn.silu(x @ w1) * (x @ w3)) @ w2

def rope_tables(seq):
    pos = jnp.arange(seq, dtype=jnp.float32)
    inv = ROPE_THETA ** (-jnp.arange(0, ROT_DIM, 2, dtype=jnp.float32) / ROT_DIM)
    ang = pos[:, None] * inv[None, :]
    return jnp.cos(ang), jnp.sin(ang)

def apply_partial_rope(x, cos, sin):
    xf = x.astype(jnp.float32)
    half = ROT_DIM // 2
    x1, x2 = xf[..., :half], xf[..., half:ROT_DIM]
    c, s = cos[None, :, None, :], sin[None, :, None, :]
    out = jnp.concatenate([x1 * c - x2 * s, x2 * c + x1 * s, xf[..., ROT_DIM:]], axis=-1)
    return out.astype(x.dtype)

def dilated_window_attention(q, k, v, window, dilation):
    B, S, H, Dh = q.shape
    r = dilation
    L = S // r
    n_back = window // r
    nb = -(-L // BLOCK)
    Lp = nb * BLOCK

    def to_blocks(t):
        t = t.reshape(B, L, r, H, Dh).transpose(0, 2, 1, 3, 4)
        t = jnp.pad(t, ((0, 0), (0, 0), (0, Lp - L), (0, 0), (0, 0)))
        return t.reshape(B, r, nb, BLOCK, H, Dh)

    def band(t):
        prev = jnp.pad(t[:, :, :-1], ((0, 0), (0, 0), (1, 0), (0, 0), (0, 0), (0, 0)))
        return jnp.concatenate([prev, t], axis=3)

    qb = to_blocks(q)
    kk = band(to_blocks(k))
    vv = band(to_blocks(v))
    s = jnp.einsum('brnqhd,brnkhd->brnhqk', qb, kk).astype(jnp.float32) * (Dh ** -0.5)
    qi = jnp.arange(BLOCK)[:, None]
    kj = jnp.arange(2 * BLOCK)[None, :]
    dist = qi + BLOCK - kj
    key_pos = (jnp.arange(nb)[:, None, None] - 1) * BLOCK + kj[None]
    allowed = (dist >= 0)[None] & (dist <= n_back)[None] & (key_pos >= 0)
    s = jnp.where(allowed[None, None, :, None], s, -jnp.inf)
    m = jnp.max(s, axis=-1, keepdims=True)
    p = jnp.exp(s - m)
    l = jnp.sum(p, axis=-1, keepdims=True)
    o = jnp.einsum('brnhqk,brnkhd->brnqhd', p, vv.astype(jnp.float32)) / jnp.swapaxes(l, 3, 4)
    lse = (m + jnp.log(l))[..., 0]
    o = o.reshape(B, r, Lp, H, Dh)[:, :, :L].transpose(0, 2, 1, 3, 4).reshape(B, S, H, Dh)
    lse = lse.transpose(0, 1, 2, 4, 3).reshape(B, r, Lp, H)[:, :, :L].transpose(0, 2, 1, 3).reshape(B, S, H)
    return o, lse

def dilated_mixture_attention(q, k, v):
    B, S = q.shape[:2]
    cos, sin = rope_tables(S)
    q = apply_partial_rope(q, cos, sin)
    k = apply_partial_rope(k, cos, sin)
    outs, lses = [], []
    for g, (window, dilation) in enumerate(DILATED_GROUPS):
        hs = slice(g * HEADS_PER_GROUP, (g + 1) * HEADS_PER_GROUP)
        o, lse = dilated_window_attention(q[:, :, hs], k[:, :, hs], v[:, :, hs], window, dilation)
        outs.append(o)
        lses.append(lse)
    alpha = jax.nn.softmax(jnp.stack(lses, axis=0), axis=0)
    o = jnp.sum(alpha[..., None] * jnp.stack(outs, axis=0), axis=0)
    return o.reshape(B, S, ATTN_OUT_WIDTH).astype(v.dtype)

def multiscale_pool(p, w_pool, pool_scale):
    B, S, C = p.shape
    pf = p.astype(jnp.float32)
    cs0 = jnp.concatenate([jnp.zeros((B, 1, C), jnp.float32), jnp.cumsum(pf, axis=1)], axis=1)
    outs = []
    for gi, win in enumerate(POOL_WINDOWS):
        cs = slice(gi * POOL_GROUP_WIDTH, (gi + 1) * POOL_GROUP_WIDTH)
        c = cs0[..., cs]
        lagged = jnp.pad(c[:, :S - win + 1], ((0, 0), (win - 1, 0), (0, 0)))
        cnt = jnp.minimum(jnp.arange(1, S + 1), win).astype(jnp.float32)[None, :, None]
        outs.append((c[:, 1:] - lagged) / cnt - pf[..., cs])
    d = jnp.stack(outs, axis=2).astype(p.dtype)
    y = jnp.einsum('bsgc,gcd->bsgd', d, w_pool).reshape(B, S, C)
    return y * pool_scale

def first_inputs(seed: int = 0) -> dict:
    key = jax.random.key(seed)
    ks = jax.random.split(key, 20)
    f32 = jnp.float32

    def nrm(k, shape, fan_in):
        return jax.random.normal(k, shape, f32) * (fan_in ** -0.5)

    def gain(k, shape):
        return 1.0 + 0.02 * jax.random.normal(k, shape, f32)

    L = DEPTH
    return {
        "x": jax.random.normal(ks[0], (BATCH, SEQ, D_MODEL), f32),
        "ffn1_norm": gain(ks[1], (L, D_MODEL)),
        "ffn1_w1": nrm(ks[2], (L, D_MODEL, D_FF), D_MODEL),
        "ffn1_w3": nrm(ks[3], (L, D_MODEL, D_FF), D_MODEL),
        "ffn1_w2": nrm(ks[4], (L, D_FF, D_MODEL), D_FF),
        "mix_norm": gain(ks[5], (L, D_MODEL)),
        "w_in": nrm(ks[6], (L, D_MODEL, IN_WIDTH), D_MODEL),
        "w_branch_attn": nrm(ks[7], (L, ATTN_OUT_WIDTH, D_MODEL), ATTN_OUT_WIDTH),
        "w_branch_pool": nrm(ks[8], (L, POOL_WIDTH, D_MODEL), POOL_WIDTH),
        "pool_w": nrm(ks[9], (L, len(POOL_WINDOWS), POOL_GROUP_WIDTH, POOL_GROUP_WIDTH), POOL_GROUP_WIDTH),
        "pool_scale": gain(ks[10], (L, POOL_WIDTH)),
        "w_out": nrm(ks[11], (L, D_MODEL, D_MODEL), D_MODEL),
        "ffn2_norm": gain(ks[12], (L, D_MODEL)),
        "ffn2_w1": nrm(ks[13], (L, D_MODEL, D_FF), D_MODEL),
        "ffn2_w3": nrm(ks[14], (L, D_MODEL, D_FF), D_MODEL),
        "ffn2_w2": nrm(ks[15], (L, D_FF, D_MODEL), D_FF),
        "final_norm": gain(ks[16], (D_MODEL,)),
    }

def first_block(x, ffn1_norm, ffn1_w1, ffn1_w3, ffn1_w2, mix_norm, w_in, w_branch_attn, w_branch_pool,
              pool_w, pool_scale, w_out, ffn2_norm, ffn2_w1, ffn2_w3, ffn2_w2, final_norm):
    B, S, D = x.shape
    h = x
    for l in range(DEPTH):
        h = h + 0.5 * swiglu(rms_norm(h, ffn1_norm[l]), ffn1_w1[l], ffn1_w3[l], ffn1_w2[l])
        u = rms_norm(h, mix_norm[l])
        proj = u @ w_in[l]
        o = 0
        q = proj[..., o:o + ATTN_WIDTH].reshape(B, S, N_ATTN_HEADS, HEAD_DIM); o += ATTN_WIDTH
        k = proj[..., o:o + ATTN_WIDTH].reshape(B, S, N_ATTN_HEADS, HEAD_DIM); o += ATTN_WIDTH
        v = proj[..., o:o + ATTN_WIDTH].reshape(B, S, N_ATTN_HEADS, HEAD_DIM); o += ATTN_WIDTH
        pz = proj[..., o:o + POOL_WIDTH]; o += POOL_WIDTH
        gates = jax.nn.sigmoid(proj[..., o:o + N_BRANCHES * D_MODEL].reshape(B, S, N_BRANCHES, D_MODEL))
        y_attn = dilated_mixture_attention(q, k, v) @ w_branch_attn[l]
        y_pool = multiscale_pool(pz, pool_w[l], pool_scale[l]) @ w_branch_pool[l]
        merged = gates[:, :, 0] * y_attn + gates[:, :, 1] * y_pool
        h = h + merged @ w_out[l]
        h = h + 0.5 * swiglu(rms_norm(h, ffn2_norm[l]), ffn2_w1[l], ffn2_w3[l], ffn2_w2[l])
    return rms_norm(h, final_norm)


DEPTH_2 = 2

N_A_LAYERS = DEPTH_2 // 2
N_B_LAYERS = DEPTH_2 - N_A_LAYERS

RET_HEADS = 4
RET_QK_DIM = 256
RET_V_DIM = 512
RET_WIDTH = RET_HEADS * RET_V_DIM
RET_QK_WIDTH = RET_HEADS * RET_QK_DIM
RET_CHUNK = 128
ROPE_BASE = 10000.0

SB_HEADS = 8
SB_QK_DIM = 128
SB_V_DIM = 256
SB_QK_WIDTH = SB_HEADS * SB_QK_DIM
SB_WIDTH = SB_HEADS * SB_V_DIM
SB_BLOCK = 128

EPS = 1e-6


def rms_norm_2(x, g):
    xf = x.astype(jnp.float32)
    y = xf * lax.rsqrt(jnp.mean(xf * xf, axis=-1, keepdims=True) + EPS)
    return (y * g.astype(jnp.float32)).astype(x.dtype)

def split_heads(t, n_heads):
    b, s, w = t.shape
    return t.reshape(b, s, n_heads, w // n_heads).transpose(0, 2, 1, 3)

def merge_heads(t):
    b, h, s, d = t.shape
    return t.transpose(0, 2, 1, 3).reshape(b, s, h * d)

def rope(x, pos):
    half = x.shape[-1] // 2
    inv_freq = 1.0 / (ROPE_BASE ** (jnp.arange(half, dtype=jnp.float32) / half))
    ang = pos[:, None] * inv_freq[None, :]
    cos, sin = jnp.cos(ang), jnp.sin(ang)
    x1, x2 = x[..., :half], x[..., half:]
    return jnp.concatenate([x1 * cos - x2 * sin, x1 * sin + x2 * cos], axis=-1)

def retention_chunkwise(q, k, v):
    b, h, t, dk = q.shape
    dv = v.shape[-1]
    c = RET_CHUNK
    nc = t // c
    log_gamma = jnp.log1p(-jnp.exp2(-5.0 - jnp.arange(h, dtype=jnp.float32)))
    idx = jnp.arange(c, dtype=jnp.float32)
    diff = idx[:, None] - idx[None, :]
    intra_decay = jnp.where(diff >= 0, jnp.exp(log_gamma[:, None, None] * diff), 0.0)
    q_decay = jnp.exp(log_gamma[:, None] * (idx[None, :] + 1.0))
    k_decay = jnp.exp(log_gamma[:, None] * (c - 1.0 - idx[None, :]))
    chunk_decay = jnp.exp(log_gamma * c)

    def to_chunks(a):
        return a.reshape(b, h, nc, c, a.shape[-1]).transpose(2, 0, 1, 3, 4)

    def step(state, inp):
        qc, kc, vc = inp
        scores = jnp.einsum('bhid,bhjd->bhij', qc, kc) * intra_decay
        o = jnp.einsum('bhij,bhje->bhie', scores, vc)
        o = o + jnp.einsum('bhid,bhde->bhie', qc * q_decay[None, :, :, None], state)
        state = state * chunk_decay[None, :, None, None] + jnp.einsum(
            'bhjd,bhje->bhde', kc * k_decay[None, :, :, None], vc)
        return state, o

    state0 = jnp.zeros((b, h, dk, dv), jnp.float32)
    _, out = lax.scan(step, state0, (to_chunks(q), to_chunks(k), to_chunks(v)))
    return out.transpose(1, 2, 0, 3, 4).reshape(b, h, t, dv)

def stick_breaking_attention(q, k, v):
    b, h, t, dk = q.shape
    nb = t // SB_BLOCK
    scale = 1.0 / math.sqrt(dk)
    key_idx = jnp.arange(t)
    q_blocks = q.reshape(b, h, nb, SB_BLOCK, dk).transpose(2, 0, 1, 3, 4)

    def block(args):
        qb, blk = args
        t_idx = blk * SB_BLOCK + jnp.arange(SB_BLOCK)
        z = jnp.einsum('bhqd,bhkd->bhqk', qb, k) * scale
        causal = key_idx[None, :] < t_idx[:, None]
        log_not = jnp.where(causal, jax.nn.log_sigmoid(-z), 0.0)
        suffix = lax.cumsum(log_not, axis=3, reverse=True) - log_not
        weights = jnp.where(causal, jnp.exp(jax.nn.log_sigmoid(z) + suffix), 0.0)
        return jnp.einsum('bhqk,bhke->bhqe', weights, v)

    out = lax.map(block, (q_blocks, jnp.arange(nb)))
    return out.transpose(1, 2, 0, 3, 4).reshape(b, h, t, v.shape[-1])

def second_inputs(seed: int = 0) -> dict:
    key = jax.random.key(seed)
    ks = jax.random.split(key, 12)
    d = D_MODEL
    ret_in_cols = 2 * RET_QK_WIDTH + 2 * RET_WIDTH
    sb_in_cols = SB_QK_WIDTH + SB_WIDTH
    kv_cols = SB_QK_WIDTH + SB_WIDTH

    def gain(k, shape):
        return 1.0 + 0.02 * jax.random.normal(k, shape, jnp.float32)

    def dense(k, shape, fan_in):
        return jax.random.normal(k, shape, jnp.float32) * (fan_in ** -0.5)

    return {
        "x": jax.random.normal(ks[0], (BATCH, SEQ, d), jnp.float32),
        "ret_norm_pre": gain(ks[1], (N_A_LAYERS, d)),
        "ret_w_in": dense(ks[2], (N_A_LAYERS, d, ret_in_cols), d),
        "ret_w_out": dense(ks[3], (N_A_LAYERS, RET_WIDTH, d), RET_WIDTH),
        "ret_norm_post": gain(ks[4], (N_A_LAYERS, d)),
        "kv_norm": gain(ks[5], (d,)),
        "w_kv": dense(ks[6], (d, kv_cols), d),
        "sb_norm_pre": gain(ks[7], (N_B_LAYERS, d)),
        "sb_w_in": dense(ks[8], (N_B_LAYERS, d, sb_in_cols), d),
        "sb_w_out": dense(ks[9], (N_B_LAYERS, SB_WIDTH, d), SB_WIDTH),
        "sb_norm_post": gain(ks[10], (N_B_LAYERS, d)),
    }

def second_block(x, ret_norm_pre, ret_w_in, ret_w_out, ret_norm_post, kv_norm, w_kv,
              sb_norm_pre, sb_w_in, sb_w_out, sb_norm_post):
    b, t, _ = x.shape
    pos = jnp.arange(t, dtype=jnp.float32)
    h = x
    k_shared = None
    v_shared = None
    for i in range(DEPTH_2):
        if i < N_A_LAYERS:
            u = rms_norm_2(h, ret_norm_pre[i])
            proj = u @ ret_w_in[i]
            q, k, v, g = jnp.split(
                proj, [RET_QK_WIDTH, 2 * RET_QK_WIDTH, 2 * RET_QK_WIDTH + RET_WIDTH], axis=-1)
            q = rope(split_heads(q, RET_HEADS).astype(jnp.float32), pos)
            k = rope(split_heads(k, RET_HEADS).astype(jnp.float32), pos) * (RET_QK_DIM ** -0.5)
            v = split_heads(v, RET_HEADS).astype(jnp.float32)
            o = retention_chunkwise(q, k, v)
            mu = jnp.mean(o, axis=-1, keepdims=True)
            var = jnp.mean(jnp.square(o - mu), axis=-1, keepdims=True)
            o = (o - mu) * lax.rsqrt(var + EPS)
            o = merge_heads(o).astype(h.dtype) * jax.nn.silu(g)
            y = o @ ret_w_out[i]
            h = h + rms_norm_2(y, ret_norm_post[i])
            if i == N_A_LAYERS - 1:
                kv = rms_norm_2(h, kv_norm) @ w_kv
                k_sh, v_sh = jnp.split(kv, [SB_QK_WIDTH], axis=-1)
                k_shared = split_heads(k_sh, SB_HEADS).astype(jnp.float32)
                v_shared = split_heads(v_sh, SB_HEADS).astype(jnp.float32)
        else:
            j = i - N_A_LAYERS
            u = rms_norm_2(h, sb_norm_pre[j])
            proj = u @ sb_w_in[j]
            q, g = jnp.split(proj, [SB_QK_WIDTH], axis=-1)
            q = split_heads(q, SB_HEADS).astype(jnp.float32)
            o = stick_breaking_attention(q, k_shared, v_shared)
            o = merge_heads(o).astype(h.dtype) * jax.nn.silu(g)
            y = o @ sb_w_out[j]
            h = h + rms_norm_2(y, sb_norm_post[j])
    return h


def setup_inputs(seed=0):
    out = dict(first_inputs(seed))
    for name, value in second_inputs(seed + 1).items():
        if name != "x":
            out[name + "_2"] = value
    return out


def reference(
    x, ffn1_norm, ffn1_w1, ffn1_w3, ffn1_w2, mix_norm, w_in, w_branch_attn, w_branch_pool,
    pool_w, pool_scale, w_out, ffn2_norm, ffn2_w1, ffn2_w3, ffn2_w2, final_norm, ret_norm_pre_2,
    ret_w_in_2, ret_w_out_2, ret_norm_post_2, kv_norm_2, w_kv_2, sb_norm_pre_2, sb_w_in_2,
    sb_w_out_2, sb_norm_post_2,
):
    x = first_block(
        x, ffn1_norm, ffn1_w1, ffn1_w3, ffn1_w2, mix_norm, w_in, w_branch_attn, w_branch_pool,
        pool_w, pool_scale, w_out, ffn2_norm, ffn2_w1, ffn2_w3, ffn2_w2, final_norm,
    )
    return second_block(
        x, ret_norm_pre_2, ret_w_in_2, ret_w_out_2, ret_norm_post_2, kv_norm_2, w_kv_2,
        sb_norm_pre_2, sb_w_in_2, sb_w_out_2, sb_norm_post_2,
    )


_drawn_inputs = setup_inputs


def setup_inputs(seed=0):
    import zlib

    import numpy as np

    out = dict(_drawn_inputs(seed))
    spreads = {}
    factors = {'ffn1_norm': 3.145,
     'mix_norm': 2.907,
     'pool_scale': 3.282,
     'ffn2_norm': 4.103,
     'ret_norm_post_2': 3.319,
     'kv_norm_2': 4.507,
     'sb_norm_pre_2': 4.259,
     'sb_norm_post_2': 4.973}
    for name, (base, spread) in spreads.items():
        noise = np.random.default_rng([zlib.crc32(name.encode()), seed]).standard_normal(out[name].shape)
        drawn = base * np.exp(spread * noise) if base else spread * noise
        out[name] = __import__('jax').numpy.asarray(drawn.astype(out[name].dtype))
    for name, factor in factors.items():
        out[name] = (out[name] * factor).astype(out[name].dtype)
    return out
```

```python
from contextlib import ExitStack, contextmanager

import numpy as np

import concourse.bass as bass
from concourse import mybir

F32 = mybir.dt.float32
F32R = mybir.dt.float32r
ALU = mybir.AluOpType
ACT = mybir.ActivationFunctionType
AX_X = mybir.AxisListType.X

P = 128
TOK = 512
D = 1024
DC = D // P
FF = 2816
FC = FF // P
BLK = P * P // P
SLAB = 16 * BLK
RING = 2
BANKS = 4
EPS = 1e-6
NEG = -1e30

N_GROUPS, GROUP_HEADS, HEAD = 3, 4, 64
DIL = 4
POOL_WINDOWS = (2, 4, 8, 16)
PAD = max(POOL_WINDOWS)
RET_HEADS, RET_KC, RET_VC = 4, 2, 4
SB_HEADS, SB_VC = 8, 2
TB = TOK // P
TRI = [TOK - P * m for m in range(TB)]
TRI_AT = [sum(TRI[:m]) for m in range(TB)]
TRI_COLS = sum(TRI)
RET_SKIP = -(TB + RET_VC + 2) % BANKS
RET_BANKS = TB + RET_VC + 2 + RET_SKIP

GAINS = ["ffn1_norm", "mix_norm", "ffn2_norm", "final_norm", "ret_norm_pre_2", "ret_norm_post_2",
         "kv_norm_2", "sb_norm_pre_2", "sb_norm_post_2"]


class Count:

    def __init__(self):
        self.k, self.turn, self.per = 0, None, 0

    def at(self, extra=0):
        return self.k + extra if self.turn is None else self.turn * self.per + (self.k + extra)

    def landed(self):
        first = 16 * (self.k // RING + 1)
        return first if self.turn is None else self.turn * (16 * self.per // RING) + first

    def next(self, by=1):
        self.k += by
        return self.at()


@contextmanager
def loop(eng, times, *steps):
    with eng.Fori(0, times) as i:
        begin = [c.k for c, _ in steps]
        for c, per in steps:
            c.turn, c.per = i, per
        yield i
        for (c, per), k in zip(steps, begin):
            assert c.k == k + per, (c.k - k, per)
            c.turn, c.k = None, k + per * times


def block_kernel(nc, dram, out):
    with ExitStack() as ctx:
        def sb(name, shape, dt=F32, scope=ctx):
            return scope.enter_context(nc.sbuf_tensor(name, shape, dt))

        def sem(name):
            return ctx.enter_context(nc.semaphore(name))

        h = sb("h", [P, DC, TOK])
        raw = sb("raw", [P, RING, SLAB])
        w_hi = sb("w_hi", [P, RING, SLAB], F32R)
        w_lo = sb("w_lo", [P, RING, SLAB], F32R)
        x_hi = sb("x_hi", [P, DC, TOK], F32R)
        x_lo = sb("x_lo", [P, DC, TOK], F32R)
        tmp = sb("tmp", [P, 6 * TOK])
        ssq = sb("ssq", [P, TOK])
        rstd = sb("rstd", [P, TOK])
        gains = sb("gains", [P, len(GAINS), DC])
        pool_scale = sb("pool_scale", [P, len(POOL_WINDOWS)])
        ident = sb("ident", [P, P])
        mean_d = sb("mean_d", [P, P])
        mean_v = sb("mean_v", [P, P])
        diag_neg = sb("diag_neg", [P, P])
        signs = sb("signs", [P, 3, P])
        rot_r = sb("rot_r", [P, P], F32R)
        tri_r = sb("tri_r", [P, P], F32R)
        ones_r = sb("ones_r", [P, P], F32R)
        eps = sb("eps", [P, 1])

        def t(i, width=TOK):
            return tmp[:, i * TOK:i * TOK + width]

        with ExitStack() as scope:
            g_hi = sb("g_hi", [P, FC, TOK], F32R, scope)
            g_lo = sb("g_lo", [P, FC, TOK], F32R, scope)
        with ExitStack() as scope:
            o_hi = sb("o_hi", [P, 2, TOK], F32R, scope)
            o_lo = sb("o_lo", [P, 2, TOK], F32R, scope)
            pool_hi = sb("pool_hi", [P, 4, TOK], F32R, scope)
            pool_lo = sb("pool_lo", [P, 4, TOK], F32R, scope)
            with ExitStack() as inner:
                qk_hi = sb("qk_hi", [P, 2, N_GROUPS, TOK], F32R, inner)
                qk_lo = sb("qk_lo", [P, 2, N_GROUPS, TOK], F32R, inner)
                va_hi = sb("va_hi", [P, TB, N_GROUPS, 256], F32R, inner)
                va_lo = sb("va_lo", [P, TB, N_GROUPS, 256], F32R, inner)
                stage_hi = sb("stage_hi", [P, 2 * TOK], F32R, inner)
                stage_lo = sb("stage_lo", [P, 2 * TOK], F32R, inner)
                rope_a = sb("rope_a", [P, 2, TOK], F32, inner)
                band = sb("band", [P, DIL, TOK], mybir.dt.bfloat16, inner)
                classes = sb("classes", [P, 2, P], F32, inner)
                neg_max = sb("neg_max", [P, 2], F32, inner)
                den = sb("den", [P, 2], F32, inner)
                rden = sb("rden", [P, 2], F32, inner)
                o_tok = sb("o_tok", [P, 2, HEAD], F32, inner)
                rcount = sb("rcount", [P, 4, PAD], F32, inner)
            with ExitStack() as inner:
                m_hi = sb("m_hi", [P, DC, TOK], F32R, inner)
                m_lo = sb("m_lo", [P, DC, TOK], F32R, inner)
        with ExitStack() as scope:
            y_ret = sb("y_ret", [P, DC, TOK], F32, scope)
            rqk_hi = sb("rqk_hi", [P, 2, RET_KC, TOK], F32R, scope)
            rqk_lo = sb("rqk_lo", [P, 2, RET_KC, TOK], F32R, scope)
            rv_hi = sb("rv_hi", [P, TB, TOK], F32R, scope)
            rv_lo = sb("rv_lo", [P, TB, TOK], F32R, scope)
            rs_hi = sb("rs_hi", [P, TRI_COLS], F32R, scope)
            rs_lo = sb("rs_lo", [P, TRI_COLS], F32R, scope)
            r_gate = sb("r_gate", [P, RET_VC, TOK], F32, scope)
            r_out = sb("r_out", [P, RET_VC, TOK], F32, scope)
            rope_b = sb("rope_b", [P, 2, TOK], F32, scope)
            decay = sb("decay", [P, RET_HEADS, TOK], F32, scope)
        with ExitStack() as scope:
            y_sb = sb("y_sb", [P, DC, TOK], F32, scope)
            kv_hi = sb("kv_hi", [P, DC, TOK], F32R, scope)
            kv_lo = sb("kv_lo", [P, DC, TOK], F32R, scope)
            skq_hi = sb("skq_hi", [P, 2, TOK], F32R, scope)
            skq_lo = sb("skq_lo", [P, 2, TOK], F32R, scope)
            sv_hi = sb("sv_hi", [P, TB, 256], F32R, scope)
            sv_lo = sb("sv_lo", [P, TB, 256], F32R, scope)
            sp_hi = sb("sp_hi", [P, TRI_COLS], F32R, scope)
            sp_lo = sb("sp_lo", [P, TRI_COLS], F32R, scope)
            s_gate = sb("s_gate", [P, SB_VC, TOK], F32, scope)
            so_hi = sb("so_hi", [P, SB_VC, TOK], F32R, scope)
            so_lo = sb("so_lo", [P, SB_VC, TOK], F32R, scope)

        acc = ctx.enter_context(nc.psum_tensor("acc", [P, BANKS, TOK], F32))
        att = ctx.enter_context(nc.psum_tensor("att", [P, BANKS, TOK], F32))

        raw_landed = [sem(f"raw_landed{i}") for i in range(RING)]
        const_landed = sem("const_landed")
        x_landed = sem("x_landed")
        mix_landed = sem("mix_landed")
        ret_landed = sem("ret_landed")
        out_landed = sem("out_landed")
        const_ready = sem("const_ready")
        w_hi_ready = sem("w_hi_ready")
        w_ready = sem("w_ready")
        seg_done = sem("seg_done")
        acc_free = sem("acc_free")
        att_full = sem("att_full")
        att_free = sem("att_free")
        fn_ready = sem("fn_ready")
        prob_ready = sem("prob_ready")
        val_ready = sem("val_ready")
        hi_ready = sem("hi_ready")
        op_ready = sem("op_ready")
        ssq_ready = sem("ssq_ready")
        dve_step = sem("dve_step")
        h_ready = sem("h_ready")

        block = ctx.enter_context(nc.Block())

        @block.sync
        def _(sp):
            n = Count()

            def fetch(src, cols=SLAB):
                sp.wait_ge(w_ready, n.at(1))
                slot = n.k % RING
                sp.dma_start(raw[:, slot, 0:cols], src).then_inc(raw_landed[slot], 16)
                n.next()

            def ffn(name):
                with loop(sp, FC // 2, (n, 2)) as i:
                    for j in range(2):
                        fetch(dram[name + "_up"][2 * i + j])
                with loop(sp, DC, (n, 2)) as i:
                    for j in range(2):
                        fetch(dram[name + "_down"][2 * i + j], FC // 2 * BLK)

            for c in range(DC):
                sp.dma_start(h[:, c, :], dram["x"][:, c, :]).then_inc(x_landed, 16)
            ffn("ffn1")
            for g in range(N_GROUPS):
                fetch(dram["mix_v"][g])
            for g in range(N_GROUPS):
                fetch(dram["mix_qk"][0, g])
            for i in range(2):
                fetch(dram["mix_pool"][i])
            fetch(dram["pool_w"], 4 * BLK)
            for g in range(N_GROUPS):
                fetch(dram["mix_qk"][1, g])
            with loop(sp, DC, (n, 2)) as i:
                fetch(dram["mix_branch"][i], 6 * BLK)
                fetch(dram["mix_gate"][i])
            with loop(sp, DC // 4, (n, 2)) as i:
                for j in range(2):
                    fetch(dram["mix_out"][2 * i + j])
            ffn("ffn2")
            for j in range(2):
                fetch(dram["ret_head"][0, j])
            with loop(sp, RET_HEADS - 1, (n, 8)) as i:
                for j in range(2, 6):
                    fetch(dram["ret_head"][i, j])
                for j in range(2):
                    fetch(dram["ret_head"][i + 1, j])
                for j in range(2):
                    fetch(dram["ret_out"][i, j])
            for j in range(2, 6):
                fetch(dram["ret_head"][RET_HEADS - 1, j])
            for j in range(2):
                fetch(dram["ret_out"][RET_HEADS - 1, j])
            fetch(dram["sb_kq"][0])
            fetch(dram["sb_v"][0])
            fetch(dram["sb_g"][0])
            fetch(dram["sb_kq"][1])
            fetch(dram["sb_v"][1])
            with loop(sp, SB_HEADS // 2 - 1, (n, 8)) as i:
                for j in range(2):
                    fetch(dram["sb_g"][2 * i + (j + 1)])
                    fetch(dram["sb_out"][2 * i + j])
                    fetch(dram["sb_kq"][2 * i + (j + 2)])
                    fetch(dram["sb_v"][2 * i + (j + 2)])
            fetch(dram["sb_g"][SB_HEADS - 1])
            fetch(dram["sb_out"][SB_HEADS - 2])
            fetch(dram["sb_out"][SB_HEADS - 1])
            for c in range(DC):
                sp.wait_ge(h_ready, c + 1)
                sp.dma_start(out[:, c, :], h[:, c, :]).then_inc(out_landed, 16)
            sp.wait_ge(out_landed, 16 * DC)

        FFN_SEGS = FC * 2 + DC * 2
        MIX_SEGS = 3 * 2 + 3 * 2 + 2 * 2 + 4 + 3 * 2 + DC * 4 + DC

        @block.gpsimd
        def _(pool):
            for dst, name in ((gains, "gains"), (pool_scale, "pool_scale"), (ident, "ident"), (mean_d, "mean_d"),
                              (mean_v, "mean_v"), (diag_neg, "diag_neg"), (signs, "signs")):
                pool.dma_start(dst[:], dram[name]).then_inc(const_landed, 16)
            pool.wait_ge(seg_done, FFN_SEGS)
            for dst, name in ((rope_a, "rope_a"), (band, "band"), (classes, "classes"), (rcount, "rcount")):
                pool.dma_start(dst[:], dram[name]).then_inc(mix_landed, 16)
            pool.wait_ge(seg_done, 2 * FFN_SEGS + MIX_SEGS)
            for dst, name in ((rope_b, "rope_b"), (decay, "decay")):
                pool.dma_start(dst[:], dram[name]).then_inc(ret_landed, 16)

        @block.scalar
        def _(act):
            n, s, u, b = Count(), Count(), Count(), Count()
            val = Count()

            def prep():
                slot = n.k % RING
                act.wait_ge(raw_landed[slot], n.landed())
                if s.k:
                    act.wait_ge(seg_done, s.at())
                nc.scalar.activation(w_hi[:, slot, :], raw[:, slot, :], ACT.Copy).then_inc(w_hi_ready, 1)
                n.next()

            def split_val(dst, src):
                act.wait_ge(val_ready, val.next())
                nc.scalar.activation(dst, src, ACT.Copy).then_inc(hi_ready, 1)

            def split_acc(dst, src, seg):
                act.wait_ge(seg_done, s.at(seg))
                nc.scalar.activation(dst, src, ACT.Copy).then_inc(hi_ready, 1)

            def std_of(skip=0):
                bank = b.k % BANKS
                act.wait_ge(att_full, b.next(1 + skip))
                nc.scalar.activation(t(5), att[:, bank, :], ACT.Sqrt, bias=eps[:]).then_inc(fn_ready, 1)

            def norm(dst):
                std_of()
                for c in range(DC):
                    split_val(dst[:, c, :], t(c % 4))

            def ffn():
                norm(x_hi)
                with loop(act, FC // 2, (n, 2), (s, 4), (u, 4)) as i:
                    for j in range(2):
                        prep()
                        act.wait_ge(seg_done, s.at(1))
                        nc.scalar.activation(t(j), acc[:, u.k % BANKS, :], ACT.Silu).then_inc(fn_ready, 1)
                        act.wait_ge(acc_free, u.at(BANKS + 2))
                        nc.scalar.activation(g_hi[:, 2 * i + j, :], t(2 + j), ACT.Copy).then_inc(hi_ready, 1)
                        s.next(2)
                        u.next(2)
                with loop(act, DC // 4, (n, 8), (s, 8), (u, 4)):
                    for j in range(8):
                        prep()
                        s.next()
                    u.next(4)

            act.wait_ge(const_ready, 1)
            prep()
            ffn()

            norm(x_hi)
            for g in range(N_GROUPS):
                prep()
                for o in range(2):
                    split_acc(va_hi[:, 2 * o:2 * o + 2, g, :],
                              acc[:, u.k % BANKS, :].rearrange("p (k c) -> p k c", k=2), 1)
                    s.next()
                    u.next()

            def rope_split(o):
                split_acc(stage_hi[:, o * TOK:(o + 1) * TOK], acc[:, u.k % BANKS, :], 1)
                s.next()
                u.next()

            def rope_done(g, o):
                b.next()
                split_val(qk_hi[:, o, g, :], t(o))

            def qk(last):
                for g in range(N_GROUPS):
                    for o in range(2):
                        if o == 0:
                            prep()
                        rope_split(o)
                        if (g, o) != (0, 0):
                            rope_done(g - 1 + o, 1 - o)
                if last:
                    rope_done(N_GROUPS - 1, 1)

            def attend(a):
                def exps(k):
                    b.next(2)
                    act.wait_ge(val_ready, val.next())
                    nc.scalar.activation(tmp[:, 768 * (k % 2):768 * (k % 2 + 1)],
                                         tmp[:, 768 * (k % 2):768 * (k % 2 + 1)], ACT.Exp,
                                         bias=neg_max[:, k % 2:k % 2 + 1],
                                         accum_out=den[:, k % 2:k % 2 + 1]).then_inc(prob_ready, 1)
                exps(0)
                for k in range(2 * DIL):
                    if k + 1 < 2 * DIL:
                        exps(k + 1)
                    act.wait_ge(att_full, b.next(2))
                    nc.scalar.activation(stage_hi[:, 0:TOK], att[:, (b.k - 2) % BANKS, :], ACT.Copy)
                    nc.scalar.activation(stage_hi[:, TOK:768], att[:, (b.k - 1) % BANKS, 0:256],
                                         ACT.Copy).then_inc(hi_ready, 1)
                    b.next()
                    if k % 2:
                        act.wait_ge(att_full, b.next())
                        nc.scalar.activation(o_hi[:, a, k // 2::DIL], att[:, (b.k - 1) % BANKS, 0:P],
                                             ACT.Copy).then_inc(hi_ready, 1)

            qk(False)
            for i in range(4):
                if i % 2 == 0:
                    prep()
                s.next()
                u.next()
                if i == 0:
                    rope_done(N_GROUPS - 1, 1)
                split_val(pool_hi[:, i, :], tmp[:, 1584:1584 + TOK])
            prep()
            for i in range(4):
                s.next()
                act.wait_ge(acc_free, u.next() + BANKS)
                nc.scalar.activation(pool_hi[:, i, :], t(i), ACT.Copy).then_inc(hi_ready, 1)
            attend(0)
            qk(True)
            attend(1)
            with loop(act, DC, (n, 2), (s, 4), (u, 4), (val, 1)) as i:
                prep()
                s.next(2)
                prep()
                for o in range(2):
                    act.wait_ge(seg_done, s.at(o + 1))
                    nc.scalar.activation(t(o), acc[:, (u.k + 2 + o) % BANKS, :], ACT.Sigmoid).then_inc(fn_ready, 1)
                s.next(2)
                u.next(4)
                split_val(m_hi[:, i, :], t(4))
            with loop(act, DC // 4, (n, 2), (s, 4), (u, 4)):
                for j in range(2):
                    prep()
                    s.next(2)
                u.next(4)

            ffn()

            std_of()
            norm(x_hi)

            def ret_rope(o):
                prep()
                for c in range(RET_KC):
                    split_val(rqk_hi[:, o, c, :], t(2 * c))
                s.next(2)
                u.next(2)

            def ret_v(j):
                prep()
                for o in range(2):
                    split_acc(rv_hi[:, 2 * o:2 * o + 2, 256 * j:256 * j + 256],
                              acc[:, u.k % BANKS, :].rearrange("p (k c) -> p k c", k=2), 1)
                    s.next()
                    u.next()

            def gate(dst):
                prep()
                for o in range(2):
                    act.wait_ge(acc_free, u.next() + BANKS)
                    nc.scalar.activation(dst[:, o, :], dst[:, o, :], ACT.Silu).then_inc(fn_ready, 1)
                    s.next()

            def ret_body(last):
                ret_v(0)
                for m in range(TB):
                    act.wait_ge(att_free, b.next() + BANKS)
                    nc.scalar.activation(rs_hi[:, TRI_AT[m]:TRI_AT[m] + TRI[m]], t(m, TRI[m]),
                                         ACT.Copy).then_inc(hi_ready, 1)
                ret_v(1)
                gate(r_gate[:, 0:2, :])
                b.next(RET_VC)
                gate(r_gate[:, 2:4, :])
                b.next()
                if not last:
                    ret_rope(0)
                std_of(RET_SKIP)
                for c in range(RET_VC):
                    split_val(rv_hi[:, c, :], r_out[:, c, :])
                if not last:
                    ret_rope(1)
                for j in range(2):
                    prep()
                    s.next(4)
                    u.next(4)

            for o in range(2):
                ret_rope(o)
            with loop(act, RET_HEADS - 1, (n, 8), (s, 20), (u, 20), (b, RET_BANKS), (val, 2 * RET_KC + RET_VC)):
                ret_body(False)
            ret_body(True)
            std_of()

            std_of()
            for c in range(DC):
                split_val(x_hi[:, c, :], t(2 * (c % 2)))
                split_val(kv_hi[:, c, :], t(2 * (c % 2) + 1))

            def sb_kq():
                prep()
                for o in range(2):
                    split_acc(skq_hi[:, o, :], acc[:, u.k % BANKS, :], 1)
                    s.next()
                    u.next()

            def sb_v():
                prep()
                for o in range(2):
                    split_acc(sv_hi[:, 2 * o:2 * o + 2, :],
                              acc[:, u.k % BANKS, :].rearrange("p (k c) -> p k c", k=2), 1)
                    s.next()
                    u.next()

            def sb_out():
                prep()
                s.next(8)
                u.next(8)

            def sb_soft():
                for m in range(TB):
                    z = tmp[:, TRI_AT[m]:TRI_AT[m] + TRI[m]]
                    e = tmp[:, TRI_COLS + TRI_AT[m]:TRI_COLS + TRI_AT[m] + TRI[m]]
                    act.wait_ge(att_free, b.next() + BANKS)
                    nc.scalar.activation(e, z, ACT.Abs).then_inc(act_step, 1)
                    act.wait_ge(act_step, step.next())
                    nc.scalar.activation(e, e, ACT.Exp, scale=-1.0).then_inc(act_step, 1)
                    act.wait_ge(act_step, step.next())
                    nc.scalar.activation(e, e, ACT.Ln, bias=1.0).then_inc(fn_ready, 1)
                for m in range(TB):
                    split_val(sp_hi[:, TRI_AT[m]:TRI_AT[m] + TRI[m]],
                              tmp[:, TRI_COLS + TRI_AT[m]:TRI_COLS + TRI_AT[m] + TRI[m]])

            def sb_weights():
                for m in range(TB):
                    z = tmp[:, TRI_AT[m]:TRI_AT[m] + TRI[m]]
                    e = tmp[:, TRI_COLS + TRI_AT[m]:TRI_COLS + TRI_AT[m] + TRI[m]]
                    act.wait_ge(att_free, b.next() + BANKS)
                    nc.scalar.activation(e, z, ACT.Exp).then_inc(act_step, 1)
                    act.wait_ge(act_step, step.next())
                    nc.scalar.activation(sp_hi[:, TRI_AT[m]:TRI_AT[m] + TRI[m]], e, ACT.Copy).then_inc(hi_ready, 1)

            def sb_gated():
                for d in range(SB_VC):
                    act.wait_ge(att_free, b.next() + BANKS)
                    nc.scalar.activation(so_hi[:, d, :], s_gate[:, d, :], ACT.Copy).then_inc(hi_ready, 1)

            def sb_body(first, last):
                prep()
                sb_soft()
                for o in range(2):
                    act.wait_ge(acc_free, u.next() + BANKS)
                    nc.scalar.activation(s_gate[:, o, :], s_gate[:, o, :], ACT.Silu).then_inc(fn_ready, 1)
                    s.next()
                if not first:
                    sb_out()
                sb_weights()
                if not last:
                    sb_kq()
                sb_gated()
                if not last:
                    sb_v()

            act_step, step = sem("act_step"), Count()
            sb_kq()
            sb_v()
            sb_body(True, False)
            with loop(act, SB_HEADS // 2 - 1, (n, 8), (s, 28), (u, 28), (b, 2 * (2 * TB + SB_VC)),
                      (val, 2 * TB), (step, 6 * TB)):
                for j in range(2):
                    sb_body(False, False)
            sb_body(False, True)
            std_of()

        @block.vector
        def _(dve):
            n, s, u, b = Count(), Count(), Count(), Count()
            fn, hi, step, sq, prob, op = (Count() for _ in range(6))
            tt = nc.vector.tensor_tensor
            stt = nc.vector.scalar_tensor_tensor

            def prep():
                slot = n.k % RING
                dve.wait_ge(w_hi_ready, n.at(1))
                tt(w_lo[:, slot, :], raw[:, slot, :], w_hi[:, slot, :].bitcast(F32), ALU.subtract).then_inc(w_ready, 1)
                n.next()

            def link(ins):
                ins.then_inc(dve_step, 1)
                dve.wait_ge(dve_step, step.next())

            def low(dst, src, hi_part, done=op_ready):
                dve.wait_ge(hi_ready, hi.next())
                tt(dst, src, hi_part.bitcast(F32), ALU.subtract).then_inc(done, 1)
                if done is op_ready:
                    op.next()

            def settle():
                dve.wait_ge(op_ready, op.at())

            def add_square(src, first):
                if first:
                    tt(ssq[:], src, src, ALU.mult).then_inc(ssq_ready, 1)
                else:
                    dve.wait_ge(ssq_ready, sq.at())
                    link(tt(t(4), src, src, ALU.mult))
                    tt(ssq[:], ssq[:], t(4), ALU.add).then_inc(ssq_ready, 1)
                sq.next()

            def rstd_of(skip=0):
                dve.wait_ge(fn_ready, fn.next())
                nc.vector.reciprocal(rstd[:], t(5)).then_inc(att_free, 1 + skip)
                dve.wait_ge(att_free, b.next(1 + skip) + BANKS)

            def norm(gain, dst_hi, dst_lo):
                rstd_of()
                for c in range(DC + 1):
                    if c < DC:
                        stt(t(c % 4), h[:, c, :], gains[:, gain, c:c + 1], rstd[:], ALU.mult, ALU.mult).then_inc(val_ready, 1)
                    if c:
                        low(dst_lo[:, c - 1, :], t((c - 1) % 4), dst_hi[:, c - 1, :])

            def ffn(gain):
                norm(gain, x_hi, x_lo)
                with loop(dve, FC // 2, (n, 2), (s, 4), (u, 4), (fn, 2), (hi, 2), (op, 2)) as i:
                    for j in range(2):
                        prep()
                        dve.wait_ge(fn_ready, fn.next())
                        dve.wait_ge(seg_done, s.next(2))
                        tt(t(2 + j), t(j), acc[:, (u.k + 1) % BANKS, :], ALU.mult).then_inc(acc_free, 2)
                        u.next(2)
                        low(g_lo[:, 2 * i + j, :], t(2 + j), g_hi[:, 2 * i + j, :])
                nc.vector.memset(ssq[:], 0.0).then_inc(ssq_ready, 1)
                sq.next()
                with loop(dve, DC // 4, (n, 8), (s, 8), (u, 4), (step, 4), (sq, 4)) as i:
                    for j in range(4):
                        prep()
                        prep()
                        dve.wait_ge(seg_done, s.next(2))
                        stt(h[:, 4 * i + j, :], acc[:, u.k % BANKS, :], 0.5, h[:, 4 * i + j, :],
                            ALU.mult, ALU.add).then_inc(acc_free, 1)
                        dve.wait_ge(acc_free, u.next() + BANKS)
                        add_square(h[:, 4 * i + j, :], False)

            nc.vector.memset(eps[:], EPS).then_inc(w_ready, RING)
            dve.wait_ge(const_landed, 7 * 16)
            nc.vector.tensor_copy(rot_r[:], signs[:, 0, :]).then_inc(acc_free, BANKS)
            nc.vector.tensor_copy(tri_r[:], signs[:, 1, :]).then_inc(att_free, BANKS)
            nc.vector.tensor_copy(ones_r[:], signs[:, 2, :]).then_inc(const_ready, 1)
            dve.wait_ge(const_ready, 1)
            dve.wait_ge(x_landed, 16 * DC)
            for c in range(DC):
                add_square(h[:, c, :], c == 0)
            prep()
            ffn(0)

            norm(1, x_hi, x_lo)
            for g in range(N_GROUPS):
                prep()
                for o in range(2):
                    low(va_lo[:, 2 * o:2 * o + 2, g, :], acc[:, u.k % BANKS, :].rearrange("p (k c) -> p k c", k=2),
                        va_hi[:, 2 * o:2 * o + 2, g, :], acc_free)
                    s.next()
                    u.next()
            dve.wait_ge(mix_landed, 4 * 16)

            def rope_split(o):
                cols = slice(o * TOK, (o + 1) * TOK)
                settle()
                low(stage_lo[:, cols], acc[:, u.k % BANKS, :], stage_hi[:, cols])
                tt(t(o), acc[:, u.k % BANKS, :], rope_a[:, 0, :], ALU.mult).then_inc(acc_free, 1)
                s.next()
                u.next()

            def rope_done(g, o, split_after):
                dve.wait_ge(att_full, b.next())
                tt(t(2 + o), att[:, (b.k - 1) % BANKS, :], rope_a[:, 1, :], ALU.mult).then_inc(att_free, 1)
                dve.wait_ge(att_free, b.at(BANKS))
                dve.wait_ge(acc_free, u.at(BANKS - split_after))
                tt(t(o), t(o), t(2 + o), ALU.add).then_inc(val_ready, 1)
                low(qk_lo[:, o, g, :], t(o), qk_hi[:, o, g, :])

            def qk(last):
                for g in range(N_GROUPS):
                    for o in range(2):
                        if o == 0:
                            prep()
                        rope_split(o)
                        if (g, o) != (0, 0):
                            rope_done(g - 1 + o, 1 - o, 1)
                if last:
                    rope_done(N_GROUPS - 1, 1, 0)

            def attend(a):
                def scores(k):
                    at = 768 * (k % 2)
                    dve.wait_ge(att_full, b.next(2))
                    stt(tmp[:, at:at + TOK], att[:, (b.k - 2) % BANKS, :], HEAD ** -0.5, band[:, k // 2, :],
                        ALU.mult, ALU.add)
                    stt(tmp[:, at + TOK:at + 768], att[:, (b.k - 1) % BANKS, 0:256], HEAD ** -0.5,
                        classes[:].rearrange("p g c -> p (g c)"), ALU.mult, ALU.add).then_inc(att_free, 2)
                    dve.wait_ge(att_free, b.at(BANKS))
                    nc.vector.tensor_reduce(neg_max[:, k % 2:k % 2 + 1], tmp[:, at:at + 768], AX_X, ALU.max,
                                            negate=True).then_inc(val_ready, 1)
                settle()
                scores(0)
                for k in range(2 * DIL):
                    if k + 1 < 2 * DIL:
                        scores(k + 1)
                    dve.wait_ge(prob_ready, prob.next())
                    nc.vector.reciprocal(rden[:, k % 2:k % 2 + 1], den[:, k % 2:k % 2 + 1]).then_inc(dve_step, 1)
                    step.next()
                    dve.wait_ge(hi_ready, hi.next())
                    b.next(2)
                    tt(stage_lo[:, 0:TOK], att[:, (b.k - 2) % BANKS, :], stage_hi[:, 0:TOK].bitcast(F32), ALU.subtract)
                    tt(stage_lo[:, TOK:768], att[:, (b.k - 1) % BANKS, 0:256], stage_hi[:, TOK:768].bitcast(F32),
                       ALU.subtract).then_inc(att_free, 2)
                    dve.wait_ge(att_full, b.next())
                    dve.wait_ge(dve_step, step.at())
                    nc.vector.tensor_scalar(o_tok[:, k % 2, :], att[:, (b.k - 1) % BANKS, 0:HEAD],
                                            rden[:, k % 2:k % 2 + 1], None, ALU.mult).then_inc(att_free, 1)
                    if k % 2:
                        b.next()
                        low(o_lo[:, a, k // 2::DIL], att[:, (b.k - 1) % BANKS, 0:P], o_hi[:, a, k // 2::DIL], att_free)

            qk(False)
            for i, window in enumerate(POOL_WINDOWS):
                if i % 2 == 0:
                    prep()
                if i == 0:
                    rope_done(N_GROUPS - 1, 1, 0)
                width = PAD + TOK
                rows = [tmp[:, k * width:(k + 1) * width] for k in range(3)]
                settle()
                link(nc.vector.memset(tmp[:, 0:3 * width].rearrange("p (k c) -> p k c", k=3)[:, :, 0:PAD], 0.0))
                dve.wait_ge(seg_done, s.next())
                nc.vector.tensor_copy(rows[0][:, PAD:], acc[:, u.k % BANKS, :]).then_inc(acc_free, 1)
                dve.wait_ge(acc_free, u.next() + BANKS)
                src, reach = rows[0], 1
                while reach < window:
                    dst = rows[2] if src is rows[1] else rows[1]
                    link(tt(dst[:, PAD:], src[:, PAD:], src[:, PAD - reach:width - reach], ALU.add))
                    src, reach = dst, 2 * reach
                diff = tmp[:, 3 * width:3 * width + TOK]
                link(stt(diff, src[:, PAD:], 1.0 / window, rows[0][:, PAD:], ALU.mult, ALU.subtract))
                link(tt(diff[:, 0:PAD], src[:, PAD:2 * PAD], rcount[:, i, :], ALU.mult))
                tt(diff[:, 0:PAD], diff[:, 0:PAD], rows[0][:, PAD:2 * PAD], ALU.subtract).then_inc(val_ready, 1)
                low(pool_lo[:, i, :], diff, pool_hi[:, i, :])
            prep()
            settle()
            for i in range(4):
                dve.wait_ge(seg_done, s.next())
                nc.vector.tensor_scalar(t(i), acc[:, u.k % BANKS, :], pool_scale[:, i:i + 1], None,
                                        ALU.mult).then_inc(acc_free, 1)
                u.next()
                low(pool_lo[:, i, :], t(i), pool_hi[:, i, :])
            attend(0)
            qk(True)
            attend(1)
            with loop(dve, DC, (n, 2), (s, 4), (u, 4), (fn, 2), (hi, 1), (op, 1)) as i:
                prep()
                for o in range(2):
                    dve.wait_ge(seg_done, s.next())
                    nc.vector.tensor_copy(t(2 + o), acc[:, u.k % BANKS, :]).then_inc(acc_free, 1)
                    u.next()
                prep()
                s.next(2)
                dve.wait_ge(acc_free, u.at(BANKS))
                for o in range(2):
                    dve.wait_ge(fn_ready, fn.next())
                    tt(t(2 + o), t(o), t(2 + o), ALU.mult).then_inc(acc_free, 1)
                    u.next()
                dve.wait_ge(acc_free, u.at(BANKS))
                tt(t(4), t(2), t(3), ALU.add).then_inc(val_ready, 1)
                low(m_lo[:, i, :], t(4), m_hi[:, i, :])
            nc.vector.memset(ssq[:], 0.0).then_inc(ssq_ready, 1)
            sq.next()
            with loop(dve, DC // 4, (n, 2), (s, 4), (u, 4), (step, 4), (sq, 4)) as i:
                for j in range(2):
                    prep()
                    for o in range(2):
                        c = 4 * i + (2 * j + o)
                        dve.wait_ge(seg_done, s.next())
                        tt(h[:, c, :], acc[:, u.k % BANKS, :], h[:, c, :], ALU.add).then_inc(acc_free, 1)
                        dve.wait_ge(acc_free, u.next() + BANKS)
                        add_square(h[:, c, :], False)

            ffn(2)

            rstd_of()
            for c in range(DC):
                link(stt(h[:, c, :], h[:, c, :], gains[:, 3, c:c + 1], rstd[:], ALU.mult, ALU.mult))
                add_square(h[:, c, :], c == 0)

            norm(4, x_hi, x_lo)
            dve.wait_ge(ret_landed, 2 * 16)

            def ret_rope(o):
                prep()
                dve.wait_ge(seg_done, s.next(2))
                settle()
                x1, x2 = acc[:, u.k % BANKS, :], acc[:, (u.k + 1) % BANKS, :]
                u.next(2)
                cos, sin = rope_b[:, 0, :], rope_b[:, 1, :]
                tt(t(0), x1, cos, ALU.mult)
                tt(t(1), x2, sin, ALU.mult)
                tt(t(2), x1, sin, ALU.mult)
                tt(t(3), x2, cos, ALU.mult).then_inc(acc_free, 2)
                dve.wait_ge(acc_free, u.at(BANKS))
                tt(t(0), t(0), t(1), ALU.subtract).then_inc(val_ready, 1)
                tt(t(2), t(2), t(3), ALU.add).then_inc(val_ready, 1)
                for c in range(RET_KC):
                    low(rqk_lo[:, o, c, :], t(2 * c), rqk_hi[:, o, c, :])

            def ret_v(j):
                prep()
                for o in range(2):
                    dst = slice(256 * j, 256 * j + 256)
                    low(rv_lo[:, 2 * o:2 * o + 2, dst], acc[:, u.k % BANKS, :].rearrange("p (k c) -> p k c", k=2),
                        rv_hi[:, 2 * o:2 * o + 2, dst], acc_free)
                    s.next()
                    u.next()

            def gate(dst):
                prep()
                for o in range(2):
                    dve.wait_ge(seg_done, s.next())
                    nc.vector.tensor_copy(dst[:, o, :], acc[:, u.k % BANKS, :]).then_inc(acc_free, 1)
                    u.next()

            def ret_body(head, last):
                ret_v(0)
                settle()
                for m in range(TB):
                    dve.wait_ge(att_full, b.next())
                    tt(t(m, TRI[m]), att[:, (b.k - 1) % BANKS, 0:TRI[m]], decay[:, head, 0:TRI[m]],
                       ALU.mult).then_inc(att_free, 1)
                for m in range(TB):
                    cols = slice(TRI_AT[m], TRI_AT[m] + TRI[m])
                    low(rs_lo[:, cols], t(m, TRI[m]), rs_hi[:, cols])
                ret_v(1)
                gate(r_gate[:, 0:2, :])
                for c in range(RET_VC):
                    dve.wait_ge(att_full, b.next())
                    nc.vector.tensor_copy(r_out[:, c, :], att[:, (b.k - 1) % BANKS, :]).then_inc(att_free, 1)
                dve.wait_ge(att_free, b.at(BANKS))
                link(tt(t(4), r_out[:, 0, :], r_out[:, 1, :], ALU.add))
                link(tt(t(4), t(4), r_out[:, 2, :], ALU.add))
                tt(t(4), t(4), r_out[:, 3, :], ALU.add).then_inc(op_ready, 1)
                op.next()
                gate(r_gate[:, 2:4, :])
                dve.wait_ge(att_full, b.next())
                for c in range(RET_VC):
                    ins = tt(r_out[:, c, :], r_out[:, c, :], att[:, (b.k - 1) % BANKS, :], ALU.subtract)
                ins.then_inc(att_free, 1)
                dve.wait_ge(att_free, b.at(BANKS))
                for c in range(RET_VC):
                    add_square(r_out[:, c, :], c == 0)
                if not last:
                    ret_rope(0)
                fn.next(RET_VC)
                rstd_of(RET_SKIP)
                for c in range(RET_VC):
                    link(tt(r_out[:, c, :], r_out[:, c, :], rstd[:], ALU.mult))
                    tt(r_out[:, c, :], r_out[:, c, :], r_gate[:, c, :], ALU.mult).then_inc(val_ready, 1)
                for c in range(RET_VC):
                    low(rv_lo[:, c, :], r_out[:, c, :], rv_hi[:, c, :])
                if not last:
                    ret_rope(1)
                for j in range(2):
                    prep()
                    for o in range(4):
                        c = 4 * j + o
                        dve.wait_ge(seg_done, s.next())
                        tt(y_ret[:, c, :], acc[:, u.k % BANKS, :], y_ret[:, c, :], ALU.add).then_inc(acc_free, 1)
                        u.next()

            link(nc.vector.memset(y_ret[:], 0.0))
            for o in range(2):
                ret_rope(o)
            with loop(dve, RET_HEADS - 1, (n, 8), (s, 20), (u, 20), (b, RET_BANKS), (fn, RET_VC + 1),
                      (hi, 4 + TB + RET_VC + 2 * RET_KC), (step, 2 + 3 + 4), (sq, RET_VC),
                      (op, TB + 1 + RET_VC + 2 * RET_KC)) as head:
                ret_body(head, False)
            ret_body(RET_HEADS - 1, True)

            def post_norm(y, gain, final):
                dve.wait_ge(acc_free, u.at(BANKS))
                for c in range(DC):
                    add_square(y[:, c, :], c == 0)
                rstd_of()
                for c in range(DC):
                    link(stt(t(c % 4), y[:, c, :], gains[:, gain, c:c + 1], rstd[:], ALU.mult, ALU.mult))
                    if final:
                        tt(h[:, c, :], h[:, c, :], t(c % 4), ALU.add).then_inc(h_ready, 1)
                    else:
                        link(tt(h[:, c, :], h[:, c, :], t(c % 4), ALU.add))
                        add_square(h[:, c, :], c == 0)

            post_norm(y_ret, 5, False)

            rstd_of()
            for c in range(DC + 1):
                if c < DC:
                    settle()
                    for k, gain in enumerate((7, 6)):
                        stt(t(2 * (c % 2) + k), h[:, c, :], gains[:, gain, c:c + 1], rstd[:], ALU.mult,
                            ALU.mult).then_inc(val_ready, 1)
                if c:
                    low(x_lo[:, c - 1, :], t(2 * ((c - 1) % 2)), x_hi[:, c - 1, :])
                    low(kv_lo[:, c - 1, :], t(2 * ((c - 1) % 2) + 1), kv_hi[:, c - 1, :])
            link(nc.vector.memset(y_sb[:], 0.0))

            def sb_kq():
                prep()
                for o in range(2):
                    low(skq_lo[:, o, :], acc[:, u.k % BANKS, :], skq_hi[:, o, :], acc_free)
                    s.next()
                    u.next()

            def sb_v():
                prep()
                for o in range(2):
                    low(sv_lo[:, 2 * o:2 * o + 2, :], acc[:, u.k % BANKS, :].rearrange("p (k c) -> p k c", k=2),
                        sv_hi[:, 2 * o:2 * o + 2, :], acc_free)
                    s.next()
                    u.next()

            def sb_out(more):
                if more:
                    prep()
                for c in range(DC):
                    dve.wait_ge(seg_done, s.next())
                    tt(y_sb[:, c, :], acc[:, u.k % BANKS, :], y_sb[:, c, :], ALU.add).then_inc(acc_free, 1)
                    u.next()

            SCALE = float(P) ** -0.5

            def sb_body(first, last):
                prep()
                settle()
                for m in range(TB):
                    at, bank = TRI_AT[m], b.k % BANKS
                    dve.wait_ge(att_full, b.next())
                    if TRI[m] > P:
                        nc.vector.tensor_scalar(tmp[:, at + P:at + TRI[m]], att[:, bank, P:TRI[m]], SCALE, None, ALU.mult)
                    stt(tmp[:, at:at + P], att[:, bank, 0:P], SCALE, diag_neg[:], ALU.mult, ALU.add).then_inc(att_free, 1)
                for m in range(TB):
                    z = tmp[:, TRI_AT[m]:TRI_AT[m] + TRI[m]]
                    e = tmp[:, TRI_COLS + TRI_AT[m]:TRI_COLS + TRI_AT[m] + TRI[m]]
                    dve.wait_ge(fn_ready, fn.next())
                    stt(e, z, 0.0, e, ALU.max, ALU.add).then_inc(val_ready, 1)
                for m in range(TB):
                    cols = slice(TRI_AT[m], TRI_AT[m] + TRI[m])
                    low(sp_lo[:, cols], tmp[:, TRI_COLS + TRI_AT[m]:TRI_COLS + TRI_AT[m] + TRI[m]], sp_hi[:, cols])
                for o in range(2):
                    dve.wait_ge(seg_done, s.next())
                    nc.vector.tensor_copy(s_gate[:, o, :], acc[:, u.k % BANKS, :]).then_inc(acc_free, 1)
                    u.next()
                if not first:
                    sb_out(True)
                settle()
                for m in range(TB):
                    z = tmp[:, TRI_AT[m]:TRI_AT[m] + TRI[m]]
                    dve.wait_ge(att_full, b.next())
                    tt(z, z, att[:, (b.k - 1) % BANKS, 0:TRI[m]], ALU.subtract).then_inc(att_free, 1)
                for m in range(TB):
                    cols = slice(TRI_AT[m], TRI_AT[m] + TRI[m])
                    low(sp_lo[:, cols], tmp[:, TRI_COLS + TRI_AT[m]:TRI_COLS + TRI_AT[m] + TRI[m]], sp_hi[:, cols])
                if not last:
                    sb_kq()
                for d in range(SB_VC):
                    dve.wait_ge(att_full, b.next())
                    dve.wait_ge(fn_ready, fn.next())
                    tt(s_gate[:, d, :], s_gate[:, d, :], att[:, (b.k - 1) % BANKS, :], ALU.mult).then_inc(att_free, 1)
                for d in range(SB_VC):
                    low(so_lo[:, d, :], s_gate[:, d, :], so_hi[:, d, :])
                if not last:
                    sb_v()

            sb_kq()
            sb_v()
            sb_body(True, False)
            with loop(dve, SB_HEADS // 2 - 1, (n, 8), (s, 28), (u, 28), (b, 2 * (2 * TB + SB_VC)),
                      (fn, 2 * (TB + SB_VC)), (hi, 2 * (2 * TB + SB_VC + 4)), (op, 2 * (2 * TB + SB_VC))):
                for j in range(2):
                    sb_body(False, False)
            sb_body(False, True)
            sb_out(False)
            post_norm(y_sb, 8, True)

        @block.tensor
        def _(pe):
            n, u, b = Count(), Count(), Count()
            op, sq, prob = Count(), Count(), Count()
            mm = nc.tensor.matmul

            def slab():
                pe.wait_ge(w_ready, n.at(RING + 1))
                slot = n.k % RING
                n.next()
                return lambda i, width=BLK: (w_hi[:, slot, i * width:(i + 1) * width],
                                             w_lo[:, slot, i * width:(i + 1) * width])

            def bank():
                pe.wait_ge(acc_free, u.at(1))
                u.next()
                return acc[:, (u.k - 1) % BANKS, :]

            def side_bank():
                pe.wait_ge(att_free, b.at(1))
                b.next()
                return att[:, (b.k - 1) % BANKS, :]

            def passes(dst, still, move, first, last):
                mm(dst, still[0], move[0], start=first, stop=False)
                mm(dst, still[0], move[1], start=False, stop=False)
                return mm(dst, still[1], move[0], start=False, stop=last)

            def project(w, first_block, x, chunks=DC, wait=None):
                dst = bank()
                for c in range(chunks):
                    if wait is not None:
                        pe.wait_ge(op_ready, wait + c + 1)
                    last = passes(dst, w(first_block + c), (x[0][:, c, :], x[1][:, c, :]), c == 0, c == chunks - 1)
                last.then_inc(seg_done, 1)

            def values(x, blocks):
                w = slab()
                for k in range(TB):
                    if k % 2 == 0:
                        dst = bank()
                    for c in range(DC):
                        last = passes(dst[:, 256 * (k % 2):256 * (k % 2) + 256],
                                      (x[0][:, c, blocks[k]], x[1][:, c, blocks[k]]), w(c, 256), c == 0, c == DC - 1)
                    if k % 2:
                        last.then_inc(seg_done, 1)

            def mean_square(skip=0, mean=mean_d):
                pe.wait_ge(ssq_ready, sq.at())
                dst = side_bank()
                b.next(skip)
                mm(dst, mean[:], ssq[:], start=True, stop=True).then_inc(att_full, 1 + skip)

            x = (x_hi, x_lo)

            def ffn(adds):
                sq.next(adds)
                mean_square()
                at = op.k
                op.next(DC)
                with loop(pe, FC // 2, (n, 2), (u, 4), (op, 2)):
                    for j in range(2):
                        w = slab()
                        project(w, 0, x, wait=at if j == 0 else None)
                        project(w, DC, x)
                    op.next(2)
                with loop(pe, DC // 4, (n, 8), (u, 4)):
                    for j in range(4):
                        dst = bank()
                        for half in range(2):
                            w = slab()
                            k0 = half * FC // 2
                            if j == 0:
                                pe.wait_ge(op_ready, op.at(k0 + FC // 2 - FC))
                            for k in range(FC // 2):
                                last = passes(dst, w(k), (g_hi[:, k0 + k, :], g_lo[:, k0 + k, :]),
                                              k0 + k == 0, k0 + k == FC - 1)
                            last.then_inc(seg_done, 1)

            pe.wait_ge(const_ready, 1)
            ffn(DC)

            plain = [slice(P * k, P * k + P) for k in range(TB)]
            strided = [slice(r, None, DIL) for r in range(DIL)]
            sq.next(1 + DC)
            mean_square()
            op.next(DC)
            pe.wait_ge(op_ready, op.at())
            for g in range(N_GROUPS):
                values(x, plain if g == 0 else strided)
            v_at = u.k

            def rotate(o):
                dst = side_bank()
                cols = slice(o * TOK, (o + 1) * TOK)
                mm(dst, rot_r[:], stage_hi[:, cols], start=True, stop=False)
                mm(dst, rot_r[:], stage_lo[:, cols], start=False, stop=True).then_inc(att_full, 1)

            def qk(last):
                for g in range(N_GROUPS):
                    w = slab()
                    for o in range(2):
                        project(w, o * DC, x)
                        if (g, o) != (0, 0):
                            pe.wait_ge(op_ready, op.next())
                            rotate(1 - o)
                            op.next()
                if last:
                    pe.wait_ge(op_ready, op.next())
                    rotate(1)
                    op.next()

            def attend(a):
                def scores(k):
                    r, rows = k // 2, slice(HEAD * (k % 2), HEAD * (k % 2) + HEAD)
                    for g in range(N_GROUPS):
                        if g < 2:
                            dst = side_bank()
                        keys = slice(None) if g == 0 else strided[r]
                        width = TOK if g == 0 else P
                        at = P if g == 2 else 0
                        last = passes(dst[:, at:at + width],
                                      (qk_hi[rows, 0, g, strided[r]], qk_lo[rows, 0, g, strided[r]]),
                                      (qk_hi[rows, 1, g, keys], qk_lo[rows, 1, g, keys]), True, True)
                    last.then_inc(att_full, 2)

                scores(0)
                for k in range(2 * DIL):
                    r, hh = k // 2, k % 2
                    if k + 1 < 2 * DIL:
                        scores(k + 1)
                    pe.wait_ge(prob_ready, prob.next())
                    for i in range(6):
                        if i % 4 == 0:
                            dst = side_bank()
                        at = 768 * (k % 2) + P * i
                        last = nc.tensor.transpose(dst[:, P * (i % 4):P * (i % 4) + P], tmp[:, at:at + P], ident[:])
                    last.then_inc(att_full, 2)
                    pe.wait_ge(att_free, b.at(BANKS))
                    dst = side_bank()
                    head = slice(HEAD * (2 * a + hh), HEAD * (2 * a + hh) + HEAD)
                    for i in range(6):
                        g, k_blk = (0, i) if i < 4 else (i - 3, r)
                        last = passes(dst[:, 0:HEAD], (stage_hi[:, P * i:P * i + P], stage_lo[:, P * i:P * i + P]),
                                      (va_hi[:, k_blk, g, head], va_lo[:, k_blk, g, head]), i == 0, i == 5)
                    last.then_inc(att_full, 1)
                    if hh:
                        pe.wait_ge(att_free, b.at(BANKS))
                        dst = side_bank()
                        nc.tensor.transpose(dst[:, 0:P], o_tok[:].rearrange("p k d -> p (k d)"),
                                            ident[:]).then_inc(att_full, 1)

            qk(False)
            for i in range(4):
                if i % 2 == 0:
                    w = slab()
                project(w, DC * (i % 2), x)
                if i == 0:
                    pe.wait_ge(op_ready, op.next())
                    rotate(1)
                    op.next()
            w = slab()
            for i in range(4):
                pe.wait_ge(op_ready, op.next())
                passes(bank(), w(i), (pool_hi[:, i, :], pool_lo[:, i, :]), True, True).then_inc(seg_done, 1)
            op.next(4)
            pe.wait_ge(acc_free, v_at + BANKS)
            attend(0)
            qk(True)
            pe.wait_ge(op_ready, op.at())
            attend(1)
            pe.wait_ge(att_free, b.at(BANKS))
            with loop(pe, DC, (n, 2), (u, 4)):
                w = slab()
                project(w, 0, (o_hi, o_lo), 2)
                project(w, 2, (pool_hi, pool_lo), 4)
                w = slab()
                project(w, 0, x)
                project(w, DC, x)
            at = op.k
            op.next(DC)
            with loop(pe, DC // 4, (n, 2), (u, 4)):
                for j in range(2):
                    w = slab()
                    project(w, 0, (m_hi, m_lo), wait=at if j == 0 else None)
                    project(w, DC, (m_hi, m_lo))

            ffn(1 + DC)

            sq.next(1 + DC)
            mean_square()

            sq.next(DC)
            mean_square()
            op.next(DC)
            pe.wait_ge(op_ready, op.at())

            def pair():
                w = slab()
                project(w, 0, x)
                project(w, DC, x)

            def ret_body(last):
                values(x, plain)
                for m in range(TB):
                    dst = side_bank()
                    for c in range(RET_KC):
                        ins = passes(dst[:, 0:TRI[m]], (rqk_hi[:, 1, c, plain[m]], rqk_lo[:, 1, c, plain[m]]),
                                     (rqk_hi[:, 0, c, P * m:], rqk_lo[:, 0, c, P * m:]), c == 0, c == RET_KC - 1)
                    ins.then_inc(att_full, 1)
                values(x, plain)
                pair()
                op.next(TB)
                pe.wait_ge(op_ready, op.at())
                pe.wait_ge(acc_free, u.at(BANKS - 2))
                for c in range(RET_VC):
                    dst = side_bank()
                    for m in range(TB):
                        cols = slice(TRI_AT[m], TRI_AT[m] + TRI[m])
                        ins = passes(dst[:, P * m:], (rv_hi[:, m, P * c:P * c + P], rv_lo[:, m, P * c:P * c + P]),
                                     (rs_hi[:, cols], rs_lo[:, cols]), m == 0, m == TB - 1)
                    ins.then_inc(att_full, 1)
                pair()
                pe.wait_ge(op_ready, op.next())
                mm(side_bank(), mean_v[:], t(4), start=True, stop=True).then_inc(att_full, 1)
                if not last:
                    pair()
                sq.next(RET_VC)
                mean_square(RET_SKIP, mean_v)
                if not last:
                    pair()
                op.next(RET_VC + (0 if last else RET_KC))
                at = op.at(-RET_KC) if not last else op.at()
                if not last:
                    op.next(RET_KC)
                pe.wait_ge(op_ready, at)
                for j in range(2):
                    w = slab()
                    for o in range(4):
                        project(w, 4 * o, (rv_hi, rv_lo), 4)

            for o in range(2):
                pair()
                op.next(RET_KC)
            pe.wait_ge(op_ready, op.at())
            with loop(pe, RET_HEADS - 1, (n, 8), (u, 20), (b, RET_BANKS), (op, TB + 1 + RET_VC + 2 * RET_KC),
                      (sq, RET_VC)):
                ret_body(False)
            ret_body(True)
            for c in range(2):
                sq.next(DC)
                mean_square()

            op.next(2 * DC)
            pe.wait_ge(op_ready, op.at())
            kv = (kv_hi, kv_lo)

            def sb_kq():
                w = slab()
                project(w, 0, kv)
                project(w, DC, x)

            def sb_out():
                pe.wait_ge(op_ready, op.at())
                w = slab()
                for c in range(DC):
                    project(w, SB_VC * c, (so_hi, so_lo), SB_VC)

            def sb_body(first, last):
                pe.wait_ge(acc_free, u.at(BANKS))
                for m in range(TB):
                    passes(side_bank()[:, 0:TRI[m]], (skq_hi[:, 0, plain[m]], skq_lo[:, 0, plain[m]]),
                           (skq_hi[:, 1, P * m:], skq_lo[:, 1, P * m:]), True, True).then_inc(att_full, 1)
                pair()
                if not first:
                    sb_out()
                op.next(TB)
                pe.wait_ge(op_ready, op.at())
                for m in range(TB):
                    dst = side_bank()
                    for k in range(m, TB):
                        cols = slice(TRI_AT[k], TRI_AT[k] + TRI[k])
                        still = tri_r if k == m else ones_r
                        mm(dst[:, P * (k - m):TRI[m]], still[:], sp_hi[:, cols], start=k == m, stop=False)
                        ins = mm(dst[:, P * (k - m):TRI[m]], still[:], sp_lo[:, cols], start=False, stop=k == TB - 1)
                    ins.then_inc(att_full, 1)
                if not last:
                    sb_kq()
                op.next(TB)
                pe.wait_ge(op_ready, op.at())
                for d in range(SB_VC):
                    dst = side_bank()
                    for m in range(TB):
                        cols = slice(TRI_AT[m], TRI_AT[m] + TRI[m])
                        ins = passes(dst[:, P * m:], (sv_hi[:, m, P * d:P * d + P], sv_lo[:, m, P * d:P * d + P]),
                                     (sp_hi[:, cols], sp_lo[:, cols]), m == 0, m == TB - 1)
                    ins.then_inc(att_full, 1)
                if not last:
                    values(kv, plain)
                op.next(SB_VC)

            sb_kq()
            values(kv, plain)
            sb_body(True, False)
            with loop(pe, SB_HEADS // 2 - 1, (n, 8), (u, 28), (b, 2 * (2 * TB + SB_VC)), (op, 2 * (2 * TB + SB_VC))):
                for j in range(2):
                    sb_body(False, False)
            sb_body(False, True)
            sb_out()
            sq.next(DC)
            mean_square()



def tiles(w):
    k, n = w.shape
    return w.reshape(k // P, P, n // P, P).transpose(2, 1, 0, 3)


def columns(w, first, width):
    return w[:, first:first + width].reshape(-1, P, width).transpose(1, 0, 2)


def lay_out(a):
    w = {}
    for f in ("ffn1", "ffn2"):
        up, lin = tiles(a[f + "_w1"][0]), tiles(a[f + "_w3"][0])
        w[f + "_up"] = np.stack([up, lin], 2).reshape(FC, P, SLAB)
        down = tiles(a[f + "_w2"][0]).reshape(DC, P, 2, FC // 2 * BLK)
        w[f + "_down"] = down.transpose(0, 2, 1, 3).reshape(2 * DC, P, FC // 2 * BLK)
    w_in = a["w_in"][0]
    heads = N_GROUPS * GROUP_HEADS * HEAD
    cols = tiles(w_in)
    qc = heads // P
    w["mix_qk"] = np.stack([np.stack([np.stack([cols[2 * g + c], cols[qc + 2 * g + c]], 1)
                                      for g in range(N_GROUPS)]) for c in range(2)]).reshape(2, N_GROUPS, P, SLAB)
    w["mix_v"] = np.stack([columns(w_in, 2 * heads + 256 * g, 256) for g in range(N_GROUPS)]).reshape(N_GROUPS, P, SLAB)
    pc, gc = 3 * qc, 3 * qc + len(POOL_WINDOWS)
    w["mix_pool"] = cols[pc:gc].reshape(2, 2, P, DC * BLK).transpose(0, 2, 1, 3).reshape(2, P, SLAB)
    w["pool_w"] = a["pool_w"][0].transpose(1, 0, 2).reshape(P, 4 * BLK)
    w["mix_branch"] = np.concatenate([tiles(a["w_branch_attn"][0]), tiles(a["w_branch_pool"][0])], 2).reshape(DC, P, 6 * BLK)
    w["mix_gate"] = np.stack([cols[gc:gc + DC], cols[gc + DC:gc + 2 * DC]], 2).reshape(DC, P, SLAB)

    def pairs(c):
        return c.reshape(-1, 2, P, DC * BLK).transpose(0, 2, 1, 3).reshape(-1, P, SLAB)

    w["mix_out"] = pairs(tiles(a["w_out"][0]))
    r = a["ret_w_in_2"][0]
    rp = pairs(tiles(r))
    keys = RET_HEADS * RET_KC * P
    vals = RET_HEADS * RET_VC * P
    gates = (2 * keys + vals) // 256
    w["ret_head"] = np.stack([np.stack(
        [rp[i], rp[RET_HEADS + i]]
        + [columns(r, 2 * keys + TOK * i + 256 * j, 256).reshape(P, SLAB) for j in range(2)]
        + [rp[gates + 2 * i + j] for j in range(2)]) for i in range(RET_HEADS)])
    ro = tiles(a["ret_w_out_2"][0])
    w["ret_out"] = np.stack([np.stack([ro[4 * j:4 * j + 4, :, RET_VC * i:RET_VC * (i + 1)].transpose(1, 0, 2, 3).reshape(P, SLAB)
                                       for j in range(2)]) for i in range(RET_HEADS)])
    kv, sbi, sbo = a["w_kv_2"], a["sb_w_in_2"][0], tiles(a["sb_w_out_2"][0])
    kt, st = tiles(kv), tiles(sbi)
    w["sb_kq"] = np.stack([kt[:SB_HEADS], st[:SB_HEADS]], 2).reshape(SB_HEADS, P, SLAB)
    w["sb_v"] = np.stack([columns(kv, SB_HEADS * P + 256 * i, 256) for i in range(SB_HEADS)]).reshape(SB_HEADS, P, SLAB)
    w["sb_g"] = pairs(st[SB_HEADS:])
    w["sb_out"] = np.stack([sbo[:, :, SB_VC * i:SB_VC * (i + 1)].transpose(1, 0, 2, 3).reshape(P, SLAB) for i in range(SB_HEADS)])
    w["x"] = a["x"][0].T.reshape(DC, P, TOK).transpose(1, 0, 2)
    w["gains"] = np.stack([a[g].reshape(DC, P).T for g in GAINS], 1)
    w["pool_scale"] = a["pool_scale"][0].reshape(-1, P).T
    return w


def constants():
    f = np.float32
    c = {"ident": np.eye(P, dtype=f), "mean_d": np.full((P, P), 1 / D, f), "mean_v": np.full((P, P), 1 / TOK, f)}
    i, j = np.arange(P)[:, None], np.arange(P)[None, :]
    c["diag_neg"] = np.where(i >= j, f(NEG), f(0))
    half = HEAD // 8
    rot = np.zeros((P, P), f)
    for m in range(P):
        d = m % HEAD
        if d < half:
            rot[m + half, m] = -1
        elif d < 2 * half:
            rot[m - half, m] = 1
    c["signs"] = np.stack([rot, (i >= j).astype(f), np.ones((P, P), f)], 1)
    pos = np.arange(TOK, dtype=f)
    inv = (f(500000.0) ** (-np.arange(0, 2 * half, 2, dtype=f) / f(2 * half))).astype(f)
    cos, sin = np.ones((P, TOK), f), np.zeros((P, TOK), f)
    for m in range(P):
        if m % HEAD < 2 * half:
            ang = pos * inv[m % HEAD % half]
            cos[m], sin[m] = np.cos(ang), np.sin(ang)
    c["rope_a"] = np.stack([cos, sin], 1)
    l, r, key = np.arange(P)[:, None, None], np.arange(DIL)[None, :, None], np.arange(TOK)[None, None, :]
    dist = DIL * l + r - key
    c["band"] = np.where((dist >= 0) & (dist <= 128), f(0), f(NEG)).astype(mybir.dt.np(mybir.dt.bfloat16))
    c["classes"] = np.stack([np.where(j <= i, f(0), f(NEG)),
                             np.where((j <= i) & ((i - j) % 4 == 0), f(0), f(NEG))], 1)
    first = np.arange(1, PAD + 1, dtype=f)
    c["rcount"] = np.broadcast_to(np.stack([f(1) / np.minimum(first, f(w)) for w in POOL_WINDOWS]), (P, 4, PAD)).astype(f)
    freq = (f(1) / (f(10000.0) ** (np.arange(P, dtype=f) / f(P)))).astype(f)
    ang = pos[None, :] * freq[:, None]
    c["rope_b"] = np.stack([np.cos(ang), np.sin(ang)], 1)
    lag = np.arange(TOK)[None, :] - np.arange(P)[:, None]
    gam = np.log1p(-np.exp2(-5.0 - np.arange(RET_HEADS)))
    dec = np.where(lag[:, None, :] >= 0, np.exp(gam[None, :, None] * np.maximum(lag, 0)[:, None, :]), 0)
    c["decay"] = (dec * (RET_KC * P) ** -0.5).astype(f)
    return c


def kernel(**inputs):
    import concourse.bacc as bacc
    from concourse.bass_utils import run_bass_kernel_spmd

    laid = lay_out({k: np.asarray(v) for k, v in inputs.items()})
    laid.update(constants())
    nc = bacc.Bacc("TRN2", target_bir_lowering=False, num_devices=1)
    arrays, dram = {}, {}
    for name, a in laid.items():
        a = np.ascontiguousarray(a)
        arrays[f"in_{name}"] = a
        dram[name] = nc.dram_tensor(f"in_{name}", a.shape, mybir.dt.from_np(a.dtype), kind="ExternalInput").ap()
    out = nc.dram_tensor("result", (P, DC, TOK), F32, kind="ExternalOutput").ap()
    block_kernel(nc, dram, out)
    got = run_bass_kernel_spmd(nc, [arrays], core_ids=[0]).results[0]["result"]
    return np.ascontiguousarray(got.transpose(1, 0, 2).reshape(D, TOK).T)[None]
```

```python
from contextlib import ExitStack, contextmanager

import numpy as np

import concourse.bass as bass
from concourse import mybir

F32 = mybir.dt.float32
F32R = mybir.dt.float32r
ALU = mybir.AluOpType
ACT = mybir.ActivationFunctionType
AX_X = mybir.AxisListType.X

P = 128
TOK = 512
D = 1024
DC = D // P
FF = 2816
FC = FF // P
BLK = P * P // P
SLAB = 16 * BLK
RING = 2
BANKS = 4
EPS = 1e-6
NEG = -1e30

N_GROUPS, GROUP_HEADS, HEAD = 3, 4, 64
DIL = 4
UNITS = 2 * DIL
KEYS = TOK + 2 * P
POOL_WINDOWS = (2, 4, 8, 16)
PAD = max(POOL_WINDOWS)
RET_HEADS, RET_KC, RET_VC = 4, 2, 4
SB_HEADS, SB_VC = 8, 2
TB = TOK // P
TRI = [TOK - P * m for m in range(TB)]
TRI_AT = [sum(TRI[:m]) for m in range(TB)]
TRI_COLS = sum(TRI)
RET_SKIP = -(TB + RET_VC + 2) % BANKS
RET_BANKS = TB + RET_VC + 2 + RET_SKIP

GAINS = ["ffn1_norm", "mix_norm", "ffn2_norm", "final_norm", "ret_norm_pre_2", "ret_norm_post_2",
         "kv_norm_2", "sb_norm_pre_2", "sb_norm_post_2"]


class Count:

    def __init__(self):
        self.k, self.turn, self.per = 0, None, 0

    def at(self, extra=0):
        return self.k + extra if self.turn is None else self.turn * self.per + (self.k + extra)

    def landed(self):
        first = 16 * (self.k // RING + 1)
        return first if self.turn is None else self.turn * (16 * self.per // RING) + first

    def next(self, by=1):
        self.k += by
        return self.at()


@contextmanager
def loop(eng, times, *steps):
    with eng.Fori(0, times) as i:
        begin = [c.k for c, _ in steps]
        for c, per in steps:
            c.turn, c.per = i, per
        yield i
        for (c, per), k in zip(steps, begin):
            assert c.k == k + per, (c.k - k, per)
            c.turn, c.k = None, k + per * times


def block_kernel(nc, dram, out):
    with ExitStack() as ctx:
        def sb(name, shape, dt=F32, scope=ctx):
            return scope.enter_context(nc.sbuf_tensor(name, shape, dt))

        def sem(name):
            return ctx.enter_context(nc.semaphore(name))

        h = sb("h", [P, DC, TOK])
        raw = sb("raw", [P, RING, SLAB])
        w_hi = sb("w_hi", [P, RING, SLAB], F32R)
        w_lo = sb("w_lo", [P, RING, SLAB], F32R)
        x_hi = sb("x_hi", [P, DC, TOK], F32R)
        x_lo = sb("x_lo", [P, DC, TOK], F32R)
        tmp = sb("tmp", [P, 6 * TOK])
        ssq = sb("ssq", [P, TOK])
        rstd = sb("rstd", [P, TOK])
        gains = sb("gains", [P, len(GAINS), DC])
        pool_scale = sb("pool_scale", [P, len(POOL_WINDOWS)])
        ident = sb("ident", [P, P])
        mean_d = sb("mean_d", [P, P])
        mean_v = sb("mean_v", [P, P])
        diag_neg = sb("diag_neg", [P, P])
        rot_r = sb("rot_r", [P, P], F32R)
        tri_r = sb("tri_r", [P, P], F32R)
        ones_r = sb("ones_r", [P, P], F32R)
        eps = sb("eps", [P, 1])

        signs = tmp[:, 4 * TOK:4 * TOK + 3 * P].rearrange("p (k c) -> p k c", k=3)
        o_tok = rstd[:].rearrange("p (k d) -> p k d", d=HEAD)

        def t(i, width=TOK):
            return tmp[:, i * TOK:i * TOK + width]

        with ExitStack() as scope:
            g_hi = sb("g_hi", [P, FC, TOK], F32R, scope)
            g_lo = sb("g_lo", [P, FC, TOK], F32R, scope)
            gsq = sb("gsq", [P, TOK], F32, scope)
            mean_eps = sb("mean_eps", [P, P], F32, scope)
            gain_sq = sb("gain_sq", [P, DC], F32, scope)
            gain_ret = sb("gain_ret", [P, DC], F32, scope)
            eps_sq = sb("eps_sq", [P, 1], F32, scope)
        with ExitStack() as scope:
            o_hi = sb("o_hi", [P, 2, TOK], F32R, scope)
            o_lo = sb("o_lo", [P, 2, TOK], F32R, scope)
            pool_hi = sb("pool_hi", [P, 4, TOK], F32R, scope)
            pool_lo = sb("pool_lo", [P, 4, TOK], F32R, scope)
            with ExitStack() as inner:
                qk_hi = sb("qk_hi", [P, 2, N_GROUPS, TOK], F32R, inner)
                qk_lo = sb("qk_lo", [P, 2, N_GROUPS, TOK], F32R, inner)
                va_hi = sb("va_hi", [P, TB, N_GROUPS, 256], F32R, inner)
                va_lo = sb("va_lo", [P, TB, N_GROUPS, 256], F32R, inner)
                stage_hi = sb("stage_hi", [P, 2 * KEYS], F32R, inner)
                stage_lo = sb("stage_lo", [P, 2 * KEYS], F32R, inner)
                rope_a = sb("rope_a", [P, 2, TOK], F32, inner)
                band = sb("band", [P, TOK + DIL - 1], mybir.dt.bfloat16, inner)
                classes = sb("classes", [P, 2, P], F32, inner)
                neg_max = sb("neg_max", [P, UNITS], F32, inner)
                den = sb("den", [P, UNITS], F32, inner)
                rden = sb("rden", [P, UNITS], F32, inner)
                rcount = sb("rcount", [P, 4, PAD], F32, inner)
            with ExitStack() as inner:
                m_hi = sb("m_hi", [P, DC, TOK], F32R, inner)
                m_lo = sb("m_lo", [P, DC, TOK], F32R, inner)
        with ExitStack() as scope:
            y_ret = sb("y_ret", [P, DC, TOK], F32, scope)
            rqk_hi = sb("rqk_hi", [P, 2, RET_KC, TOK], F32R, scope)
            rqk_lo = sb("rqk_lo", [P, 2, RET_KC, TOK], F32R, scope)
            rv_hi = sb("rv_hi", [P, TB, TOK], F32R, scope)
            rv_lo = sb("rv_lo", [P, TB, TOK], F32R, scope)
            rs_hi = sb("rs_hi", [P, TRI_COLS], F32R, scope)
            rs_lo = sb("rs_lo", [P, TRI_COLS], F32R, scope)
            r_gate = sb("r_gate", [P, RET_VC, TOK], F32, scope)
            r_out = sb("r_out", [P, RET_VC, TOK], F32, scope)
            rope_b = sb("rope_b", [P, 2, TOK], F32, scope)
            decay = sb("decay", [P, RET_HEADS, TOK], F32, scope)
        with ExitStack() as scope:
            y_sb = sb("y_sb", [P, DC, TOK], F32, scope)
            kv_hi = sb("kv_hi", [P, DC, TOK], F32R, scope)
            kv_lo = sb("kv_lo", [P, DC, TOK], F32R, scope)
            skq_hi = sb("skq_hi", [P, 2, TOK], F32R, scope)
            skq_lo = sb("skq_lo", [P, 2, TOK], F32R, scope)
            sv_hi = sb("sv_hi", [P, TB, 256], F32R, scope)
            sv_lo = sb("sv_lo", [P, TB, 256], F32R, scope)
            sp_hi = sb("sp_hi", [P, TRI_COLS], F32R, scope)
            sp_lo = sb("sp_lo", [P, TRI_COLS], F32R, scope)
            s_gate = sb("s_gate", [P, SB_VC, TOK], F32, scope)
            so_hi = sb("so_hi", [P, SB_VC, TOK], F32R, scope)
            so_lo = sb("so_lo", [P, SB_VC, TOK], F32R, scope)

        acc = ctx.enter_context(nc.psum_tensor("acc", [P, BANKS, TOK], F32))
        att = ctx.enter_context(nc.psum_tensor("att", [P, BANKS, TOK], F32))

        raw_landed = [sem(f"raw_landed{i}") for i in range(RING)]
        const_landed = sem("const_landed")
        x_landed = [sem(f"x_landed{c}") for c in range(DC)]
        mix_landed = sem("mix_landed")
        ret_landed = sem("ret_landed")
        out_landed = sem("out_landed")
        const_ready = sem("const_ready")
        w_hi_ready = sem("w_hi_ready")
        w_ready = sem("w_ready")
        seg_done = sem("seg_done")
        acc_free = sem("acc_free")
        att_full = sem("att_full")
        att_free = sem("att_free")
        fn_ready = sem("fn_ready")
        prob_ready = sem("prob_ready")
        turned = sem("turned")
        stage_ready = sem("stage_ready")
        mixed = sem("mixed")
        val_ready = sem("val_ready")
        hi_ready = sem("hi_ready")
        op_ready = sem("op_ready")
        sq_ready = sem("sq_ready")
        ssq_ready = sem("ssq_ready")
        dve_step = sem("dve_step")
        h_ready = sem("h_ready")

        block = ctx.enter_context(nc.Block())

        @block.sync
        def _(sp):
            n = Count()

            def fetch(src, cols=SLAB):
                sp.wait_ge(w_ready, n.at(1))
                slot = n.k % RING
                sp.dma_start(raw[:, slot, 0:cols], src).then_inc(raw_landed[slot], 16)
                n.next()

            def ffn(name):
                with loop(sp, FC // 2, (n, 2)) as i:
                    for j in range(2):
                        fetch(dram[name + "_up"][2 * i + j])
                with loop(sp, DC, (n, 2)) as i:
                    for j in range(2):
                        fetch(dram[name + "_down"][2 * i + j], FC // 2 * BLK)

            for c in range(DC):
                sp.dma_start(h[:, c, :], dram["x"][:, c, :]).then_inc(x_landed[c], 16)
            ffn("ffn1")
            for g in range(N_GROUPS):
                fetch(dram["mix_qk"][0, g])
            for i in range(2):
                fetch(dram["mix_pool"][i])
            for g in range(N_GROUPS):
                fetch(dram["mix_v"][g])
            fetch(dram["pool_w"], 4 * BLK)
            for g in range(N_GROUPS):
                fetch(dram["mix_qk"][1, g])
            with loop(sp, DC // 4, (n, 6)) as i:
                for j in range(2):
                    fetch(dram["mix_branch"][2 * i + j], 12 * BLK)
                    for k in range(2):
                        fetch(dram["mix_gate"][4 * i + (2 * j + k)])
            with loop(sp, DC // 4, (n, 2)) as i:
                for j in range(2):
                    fetch(dram["mix_out"][2 * i + j])
            ffn("ffn2")
            for j in range(2):
                fetch(dram["ret_head"][0, j])
            with loop(sp, RET_HEADS - 1, (n, 8)) as i:
                for j in range(2, 6):
                    fetch(dram["ret_head"][i, j])
                for j in range(2):
                    fetch(dram["ret_head"][i + 1, j])
                for j in range(2):
                    fetch(dram["ret_out"][i, j])
            for j in range(2, 6):
                fetch(dram["ret_head"][RET_HEADS - 1, j])
            for j in range(2):
                fetch(dram["ret_out"][RET_HEADS - 1, j])
            fetch(dram["sb_v"][0])
            fetch(dram["sb_kq"][0])
            fetch(dram["sb_g"][0])
            fetch(dram["sb_kq"][1])
            fetch(dram["sb_v"][1])
            with loop(sp, SB_HEADS // 2 - 1, (n, 8)) as i:
                for j in range(2):
                    fetch(dram["sb_g"][2 * i + (j + 1)])
                    fetch(dram["sb_out"][2 * i + j])
                    fetch(dram["sb_kq"][2 * i + (j + 2)])
                    fetch(dram["sb_v"][2 * i + (j + 2)])
            fetch(dram["sb_g"][SB_HEADS - 1])
            fetch(dram["sb_out"][SB_HEADS - 2])
            fetch(dram["sb_out"][SB_HEADS - 1])
            for c in range(DC):
                sp.wait_ge(h_ready, c + 1)
                sp.dma_start(out[:, c, :], h[:, c, :]).then_inc(out_landed, 16)
            sp.wait_ge(out_landed, 16 * DC)

        FFN_SEGS = FC * 2 + DC * 2
        MIX_SEGS = 3 * 2 + 3 * 2 + 2 * 2 + 4 + 3 * 2 + DC * 4 + DC

        @block.gpsimd
        def _(pool):
            for dst, name in ((gains, "gains"), (pool_scale, "pool_scale"), (ident, "ident"), (mean_d, "mean_d"),
                              (mean_v, "mean_v"), (diag_neg, "diag_neg"), (signs, "signs")):
                pool.dma_start(dst if name == "signs" else dst[:], dram[name]).then_inc(const_landed, 16)
            pool.wait_ge(seg_done, FFN_SEGS)
            for dst, name in ((rope_a, "rope_a"), (band, "band"), (classes, "classes"), (rcount, "rcount")):
                pool.dma_start(dst[:], dram[name]).then_inc(mix_landed, 16)
            pool.wait_ge(seg_done, 2 * FFN_SEGS + MIX_SEGS)
            for dst, name in ((rope_b, "rope_b"), (decay, "decay")):
                pool.dma_start(dst[:], dram[name]).then_inc(ret_landed, 16)

        @block.scalar
        def _(act):
            n, s, u, b = Count(), Count(), Count(), Count()
            val, turn = Count(), Count()

            def prep():
                slot = n.k % RING
                act.wait_ge(raw_landed[slot], n.landed())
                if s.k:
                    act.wait_ge(seg_done, s.at())
                nc.scalar.activation(w_hi[:, slot, :], raw[:, slot, :], ACT.Copy).then_inc(w_hi_ready, 1)
                n.next()

            def split_val(dst, src):
                act.wait_ge(val_ready, val.next())
                nc.scalar.activation(dst, src, ACT.Copy).then_inc(hi_ready, 1)

            def split_acc(dst, src, seg):
                act.wait_ge(seg_done, s.at(seg))
                nc.scalar.activation(dst, src, ACT.Copy).then_inc(hi_ready, 1)

            def std_of(skip=0, bias=eps):
                bank = b.k % BANKS
                act.wait_ge(att_full, b.next(1 + skip))
                nc.scalar.activation(t(5), att[:, bank, :], ACT.Sqrt, bias=bias[:]).then_inc(fn_ready, 1)

            def square(c, src):
                if c >= 4:
                    act.wait_ge(ssq_ready, sq.at(c - 3))
                nc.scalar.activation(t(c % 4), src, ACT.Square).then_inc(sq_ready, 1)

            def norm(dst):
                std_of()
                for c in range(DC):
                    split_val(dst[:, c, :], t(c % 4))

            def ffn():
                norm(x_hi)
                with loop(act, FC // 2, (n, 2), (s, 4), (u, 4)) as i:
                    for j in range(2):
                        prep()
                        act.wait_ge(seg_done, s.at(1))
                        nc.scalar.activation(t(j), acc[:, u.k % BANKS, :], ACT.Silu).then_inc(fn_ready, 1)
                        act.wait_ge(acc_free, u.at(BANKS + 2))
                        nc.scalar.activation(g_hi[:, 2 * i + j, :], t(2 + j), ACT.Copy).then_inc(hi_ready, 1)
                        s.next(2)
                        u.next(2)
                with loop(act, DC // 4, (n, 8), (s, 8), (u, 4)):
                    for j in range(8):
                        prep()
                        s.next()
                    u.next(4)

            sq = Count()
            for c in range(DC):
                act.wait_ge(x_landed[c], 16)
                square(c, h[:, c, :])
            sq.next(DC + 2 * (1 + DC) + 1 + DC + RET_HEADS * RET_VC + DC)
            prep()
            act.wait_ge(const_ready, 1)
            ffn()

            norm(x_hi)

            def rope_split(o):
                split_acc(stage_hi[:, o * TOK:(o + 1) * TOK], acc[:, u.k % BANKS, :], 1)
                s.next()
                u.next()

            def rope_done(g, o):
                b.next()
                split_val(qk_hi[:, o, g, :], t(o))

            def qk(last):
                for g in range(N_GROUPS):
                    for o in range(2):
                        if o == 0:
                            prep()
                        rope_split(o)
                        if (g, o) != (0, 0):
                            rope_done(g - 1 + o, 1 - o)
                if last:
                    rope_done(N_GROUPS - 1, 1)

            def attend(a):
                def exps(k):
                    at = KEYS * (k % 4)
                    b.next(2)
                    act.wait_ge(val_ready, val.next())
                    nc.scalar.activation(tmp[:, at:at + KEYS], tmp[:, at:at + KEYS], ACT.Exp,
                                         bias=neg_max[:, k:k + 1],
                                         accum_out=den[:, k:k + 1]).then_inc(prob_ready, 1)
                exps(0)
                exps(1)
                for k in range(UNITS):
                    at = KEYS * (k % 2)
                    act.wait_ge(turned, turn.next())
                    nc.scalar.activation(stage_hi[:, at:at + TOK], acc[:, u.k % BANKS, :], ACT.Copy)
                    nc.scalar.activation(stage_hi[:, at + TOK:at + KEYS], acc[:, (u.k + 1) % BANKS, 0:KEYS - TOK],
                                         ACT.Copy).then_inc(hi_ready, 1)
                    u.next(2)
                    if k + 2 < UNITS:
                        exps(k + 2)
                act.wait_ge(att_full, b.next())
                nc.scalar.activation(o_hi[:, a, :].rearrange("p (l r) -> p r l", r=DIL),
                                     att[:, (b.k - 1) % BANKS, :].rearrange("p (r l) -> p r l", r=DIL),
                                     ACT.Copy).then_inc(hi_ready, 1)

            qk(False)
            for i in range(4):
                if i % 2 == 0:
                    prep()
                s.next()
                u.next()
                if i == 0:
                    rope_done(N_GROUPS - 1, 1)
                split_val(pool_hi[:, i, :], tmp[:, 3 * (PAD + TOK):3 * (PAD + TOK) + TOK])
            for g in range(N_GROUPS):
                prep()
                for o in range(2):
                    split_acc(va_hi[:, 2 * o:2 * o + 2, g, :],
                              acc[:, u.k % BANKS, :].rearrange("p (k c) -> p k c", k=2), 1)
                    s.next()
                    u.next()
            prep()
            for i in range(4):
                s.next()
                act.wait_ge(acc_free, u.next() + BANKS)
                nc.scalar.activation(pool_hi[:, i, :], t(i), ACT.Copy).then_inc(hi_ready, 1)
            attend(0)
            qk(True)
            attend(1)
            with loop(act, DC // 4, (n, 6), (s, 16), (u, 16), (val, 4)) as i:
                for j in range(2):
                    prep()
                    s.next(4)
                    u.next(4)
                    for k in range(2):
                        prep()
                        for o in range(2):
                            act.wait_ge(seg_done, s.next())
                            nc.scalar.activation(t(4 + o), acc[:, u.k % BANKS, :], ACT.Sigmoid).then_inc(fn_ready, 1)
                            u.next()
                        split_val(m_hi[:, 4 * i + (2 * j + k), :], t(2 * k))
            with loop(act, DC // 4, (n, 2), (s, 4), (u, 4)):
                for j in range(2):
                    prep()
                    s.next(2)
                u.next(4)

            ffn()

            std_of(bias=eps_sq)
            for c in range(DC):
                split_val(x_hi[:, c, :], t(c % 4))
            std_of()

            def rope_split_b(o):
                for c in range(RET_KC):
                    split_val(rqk_hi[:, o, c, :], t(2 * c))

            def ret_rope(o):
                prep()
                rope_split_b(o)
                s.next(2)
                u.next(2)

            def ret_v(j):
                prep()
                for o in range(2):
                    split_acc(rv_hi[:, 2 * o:2 * o + 2, 256 * j:256 * j + 256],
                              acc[:, u.k % BANKS, :].rearrange("p (k c) -> p k c", k=2), 1)
                    s.next()
                    u.next()

            def gate(dst):
                prep()
                for o in range(2):
                    act.wait_ge(acc_free, u.next() + BANKS)
                    nc.scalar.activation(dst[:, o, :], dst[:, o, :], ACT.Silu).then_inc(fn_ready, 1)
                    s.next()

            def ret_body(last):
                ret_v(0)
                for m in range(TB):
                    act.wait_ge(att_free, b.next() + BANKS)
                    nc.scalar.activation(rs_hi[:, TRI_AT[m]:TRI_AT[m] + TRI[m]], t(m, TRI[m]),
                                         ACT.Copy).then_inc(hi_ready, 1)
                ret_v(1)
                gate(r_gate[:, 0:2, :])
                b.next(RET_VC)
                gate(r_gate[:, 2:4, :])
                b.next()
                if not last:
                    prep()
                    s.next(2)
                std_of(RET_SKIP)
                if not last:
                    prep()
                    s.next(2)
                    u.next(4)
                for c in range(RET_VC):
                    split_val(rv_hi[:, c, :], r_out[:, c, :])
                if not last:
                    for o in range(2):
                        rope_split_b(o)
                for j in range(2):
                    prep()
                    s.next(4)
                    u.next(4)

            for o in range(2):
                ret_rope(o)
            with loop(act, RET_HEADS - 1, (n, 8), (s, 20), (u, 20), (b, RET_BANKS), (val, 2 * RET_KC + RET_VC)):
                ret_body(False)
            ret_body(True)
            std_of()

            for c in range(DC):
                act.wait_ge(val_ready, val.next())
                nc.scalar.activation(y_ret[:, c, :], h[:, c, :], ACT.Square).then_inc(sq_ready, 1)

            norm(kv_hi)
            prep()
            for c in range(2):
                split_val(x_hi[:, c, :], t(c % 4))
            for k in range(TB):
                split_acc(sv_hi[:, k, :], acc[:, u.k % BANKS, 0:256], 1)
                s.next()
                u.next()
            for c in range(2, DC):
                split_val(x_hi[:, c, :], t(c % 4))

            def sb_kq():
                prep()
                for o in range(2):
                    split_acc(skq_hi[:, o, :], acc[:, u.k % BANKS, :], 1)
                    s.next()
                    u.next()

            def sb_v():
                prep()
                for o in range(2):
                    split_acc(sv_hi[:, 2 * o:2 * o + 2, :],
                              acc[:, u.k % BANKS, :].rearrange("p (k c) -> p k c", k=2), 1)
                    s.next()
                    u.next()

            z, e = tmp[:, 0:TRI_COLS], tmp[:, TRI_COLS:2 * TRI_COLS]

            def sb_soft():
                b.next(TB)
                act.wait_ge(val_ready, val.next())
                nc.scalar.activation(e, e, ACT.Exp).then_inc(act_step, 1)
                act.wait_ge(act_step, step.next())
                nc.scalar.activation(e, e, ACT.Ln, bias=1.0).then_inc(fn_ready, 1)
                split_val(sp_hi[:], e)

            def sb_weights():
                act.wait_ge(att_free, b.next(TB) + BANKS)
                nc.scalar.activation(e, z, ACT.Exp).then_inc(act_step, 1)
                act.wait_ge(act_step, step.next())
                nc.scalar.activation(sp_hi[:], e, ACT.Copy).then_inc(hi_ready, 1)

            def sb_gated():
                for d in range(SB_VC):
                    act.wait_ge(att_free, b.next() + BANKS)
                    nc.scalar.activation(so_hi[:, d, :], s_gate[:, d, :], ACT.Copy).then_inc(hi_ready, 1)

            def sb_body(first, last):
                prep()
                sb_soft()
                s.next(2)
                if not first:
                    prep()
                for o in range(2):
                    act.wait_ge(acc_free, u.next() + BANKS)
                    nc.scalar.activation(s_gate[:, o, :], s_gate[:, o, :], ACT.Silu).then_inc(fn_ready, 1)
                if not first:
                    s.next(DC)
                    u.next(DC)
                sb_weights()
                if not last:
                    sb_kq()
                sb_gated()
                if not last:
                    sb_v()

            act_step, step = sem("act_step"), Count()
            sb_kq()
            sb_body(True, False)
            with loop(act, SB_HEADS // 2 - 1, (n, 8), (s, 28), (u, 28), (b, 2 * (2 * TB + SB_VC)),
                      (val, 4), (step, 4)):
                for j in range(2):
                    sb_body(False, False)
            sb_body(False, True)
            for c in range(DC):
                act.wait_ge(acc_free, u.next() + BANKS)
                square(c, y_sb[:, c, :])
            std_of()

        @block.vector
        def _(dve):
            n, s, u, b = Count(), Count(), Count(), Count()
            fn, hi, step, sq, prob, mix, op, squared = (Count() for _ in range(8))
            tt = nc.vector.tensor_tensor
            stt = nc.vector.scalar_tensor_tensor

            def prep():
                slot = n.k % RING
                dve.wait_ge(w_hi_ready, n.at(1))
                tt(w_lo[:, slot, :], raw[:, slot, :], w_hi[:, slot, :].bitcast(F32), ALU.subtract).then_inc(w_ready, 1)
                n.next()

            def link(ins):
                ins.then_inc(dve_step, 1)
                dve.wait_ge(dve_step, step.next())

            def low(dst, src, hi_part, done=op_ready):
                dve.wait_ge(hi_ready, hi.next())
                tt(dst, src, hi_part.bitcast(F32), ALU.subtract).then_inc(done, 1)
                if done is op_ready:
                    op.next()

            def settle():
                dve.wait_ge(op_ready, op.at())

            def add_square(src, first, weight=None):
                if first:
                    tt(ssq[:], src, src, ALU.mult).then_inc(ssq_ready, 1)
                else:
                    dve.wait_ge(ssq_ready, sq.at())
                    link(tt(t(4), src, src, ALU.mult))
                    if weight is not None:
                        stt(gsq[:], t(4), weight, gsq[:], ALU.mult, ALU.add)
                    tt(ssq[:], ssq[:], t(4), ALU.add).then_inc(ssq_ready, 1)
                sq.next()

            def sum_square(c):
                dve.wait_ge(sq_ready, squared.next())
                if c == 0:
                    nc.vector.tensor_copy(ssq[:], t(0)).then_inc(ssq_ready, 1)
                else:
                    dve.wait_ge(ssq_ready, sq.at())
                    tt(ssq[:], ssq[:], t(c % 4), ALU.add).then_inc(ssq_ready, 1)
                sq.next()

            def rstd_of(skip=0):
                dve.wait_ge(fn_ready, fn.next())
                nc.vector.reciprocal(rstd[:], t(5)).then_inc(att_free, 1 + skip)
                dve.wait_ge(att_free, b.next(1 + skip) + BANKS)

            def norm_chunks(gain, dst_hi, dst_lo, first=0, last=DC):
                settle()
                for c in range(first, last + 1):
                    if c < last:
                        stt(t(c % 4), h[:, c, :], gain[:, c:c + 1], rstd[:], ALU.mult, ALU.mult).then_inc(val_ready, 1)
                    if c > first:
                        low(dst_lo[:, c - 1, :], t((c - 1) % 4), dst_hi[:, c - 1, :])

            def ffn(gain, final=False):
                rstd_of()
                norm_chunks(gains[:, gain, :], x_hi, x_lo)
                with loop(dve, FC // 2, (n, 2), (s, 4), (u, 4), (fn, 2), (hi, 2), (op, 2)) as i:
                    for j in range(2):
                        prep()
                        dve.wait_ge(fn_ready, fn.next())
                        dve.wait_ge(seg_done, s.next(2))
                        tt(t(2 + j), t(j), acc[:, (u.k + 1) % BANKS, :], ALU.mult).then_inc(acc_free, 2)
                        u.next(2)
                        low(g_lo[:, 2 * i + j, :], t(2 + j), g_hi[:, 2 * i + j, :])
                if final:
                    link(nc.vector.memset(gsq[:], 0.0))
                nc.vector.memset(ssq[:], 0.0).then_inc(ssq_ready, 1)
                sq.next()
                with loop(dve, DC // 4, (n, 8), (s, 8), (u, 4), (step, 4), (sq, 4)) as i:
                    for j in range(4):
                        prep()
                        prep()
                        dve.wait_ge(seg_done, s.next(2))
                        stt(h[:, 4 * i + j, :], acc[:, u.k % BANKS, :], 0.5, h[:, 4 * i + j, :],
                            ALU.mult, ALU.add).then_inc(acc_free, 1)
                        dve.wait_ge(acc_free, u.next() + BANKS)
                        add_square(h[:, 4 * i + j, :], False, gain_sq[:, bass.ds(4 * i + j, 1)] if final else None)

            nc.vector.memset(eps[:], EPS).then_inc(w_ready, RING)
            for c in range(DC):
                sum_square(c)
            dve.wait_ge(const_landed, 7 * 16)
            nc.vector.tensor_copy(rot_r[:], signs[:, 0, :]).then_inc(acc_free, BANKS)
            nc.vector.tensor_copy(tri_r[:], signs[:, 1, :]).then_inc(att_free, BANKS)
            nc.vector.tensor_copy(ones_r[:], signs[:, 2, :]).then_inc(const_ready, 1)
            dve.wait_ge(const_ready, 1)
            prep()
            ffn(0)

            rstd_of()
            norm_chunks(gains[:, 1, :], x_hi, x_lo)
            dve.wait_ge(mix_landed, 4 * 16)

            def rope_split(o):
                cols = slice(o * TOK, (o + 1) * TOK)
                settle()
                low(stage_lo[:, cols], acc[:, u.k % BANKS, :], stage_hi[:, cols])
                tt(t(o), acc[:, u.k % BANKS, :], rope_a[:, 0, :], ALU.mult).then_inc(acc_free, 1)
                s.next()
                u.next()

            def rope_done(g, o, split_after):
                dve.wait_ge(att_full, b.next())
                tt(t(2 + o), att[:, (b.k - 1) % BANKS, :], rope_a[:, 1, :], ALU.mult).then_inc(att_free, 1)
                dve.wait_ge(att_free, b.at(BANKS))
                dve.wait_ge(acc_free, u.at(BANKS - split_after))
                tt(t(o), t(o), t(2 + o), ALU.add).then_inc(val_ready, 1)
                low(qk_lo[:, o, g, :], t(o), qk_hi[:, o, g, :])

            def qk(last):
                for g in range(N_GROUPS):
                    for o in range(2):
                        if o == 0:
                            prep()
                        rope_split(o)
                        if (g, o) != (0, 0):
                            rope_done(g - 1 + o, 1 - o, 1)
                if last:
                    rope_done(N_GROUPS - 1, 1, 0)

            def attend(a):
                def scores(k):
                    at = KEYS * (k % 4)
                    dve.wait_ge(att_full, b.next(2))
                    stt(tmp[:, at:at + TOK], att[:, (b.k - 2) % BANKS, :], HEAD ** -0.5, band[:, DIL - 1 - k // 2:DIL - 1 - k // 2 + TOK],
                        ALU.mult, ALU.add)
                    stt(tmp[:, at + TOK:at + KEYS], att[:, (b.k - 1) % BANKS, 0:KEYS - TOK], HEAD ** -0.5,
                        classes[:].rearrange("p g c -> p (g c)"), ALU.mult, ALU.add).then_inc(att_free, 2)
                    dve.wait_ge(att_free, b.at(BANKS))
                    nc.vector.tensor_reduce(neg_max[:, k:k + 1], tmp[:, at:at + KEYS], AX_X, ALU.max,
                                            negate=True).then_inc(val_ready, 1)

                def stage(k):
                    at, bank = KEYS * (k % 2), u.k + 2 * k
                    dve.wait_ge(prob_ready, prob.next())
                    nc.vector.reciprocal(rden[:, k:k + 1], den[:, k:k + 1]).then_inc(dve_step, 1)
                    step.next()
                    dve.wait_ge(hi_ready, hi.next())
                    tt(stage_lo[:, at:at + TOK], acc[:, bank % BANKS, :], stage_hi[:, at:at + TOK].bitcast(F32),
                       ALU.subtract)
                    tt(stage_lo[:, at + TOK:at + KEYS], acc[:, (bank + 1) % BANKS, 0:KEYS - TOK],
                       stage_hi[:, at + TOK:at + KEYS].bitcast(F32), ALU.subtract).then_inc(stage_ready, 1)

                settle()
                scores(0)
                scores(1)
                stage(0)
                for k in range(UNITS):
                    if k + 2 < UNITS:
                        scores(k + 2)
                    done = step.at()
                    if k + 1 < UNITS:
                        stage(k + 1)
                    dve.wait_ge(mixed, mix.next())
                    dve.wait_ge(dve_step, done)
                    nc.vector.tensor_scalar(o_tok[:, k, :], acc[:, (u.k + 2 * k + 1) % BANKS, KEYS - TOK:KEYS - TOK + HEAD],
                                            rden[:, k:k + 1], None, ALU.mult).then_inc(acc_free, 2)
                u.next(2 * UNITS)
                dve.wait_ge(att_full, b.next())
                low(o_lo[:, a, :].rearrange("p (l r) -> p r l", r=DIL),
                    att[:, (b.k - 1) % BANKS, :].rearrange("p (r l) -> p r l", r=DIL),
                    o_hi[:, a, :].rearrange("p (l r) -> p r l", r=DIL), att_free)

            qk(False)
            for i, window in enumerate(POOL_WINDOWS):
                if i % 2 == 0:
                    prep()
                if i == 0:
                    rope_done(N_GROUPS - 1, 1, 0)
                width = PAD + TOK
                rows = [tmp[:, k * width:(k + 1) * width] for k in range(3)]
                settle()
                link(nc.vector.memset(tmp[:, 0:3 * width].rearrange("p (k c) -> p k c", k=3)[:, :, 0:PAD], 0.0))
                dve.wait_ge(seg_done, s.next())
                nc.vector.tensor_copy(rows[0][:, PAD:], acc[:, u.k % BANKS, :]).then_inc(acc_free, 1)
                dve.wait_ge(acc_free, u.next() + BANKS)
                src, reach = rows[0], 1
                while reach < window:
                    dst = rows[2] if src is rows[1] else rows[1]
                    link(tt(dst[:, PAD:], src[:, PAD:], src[:, PAD - reach:width - reach], ALU.add))
                    src, reach = dst, 2 * reach
                diff = tmp[:, 3 * width:3 * width + TOK]
                link(stt(diff, src[:, PAD:], 1.0 / window, rows[0][:, PAD:], ALU.mult, ALU.subtract))
                link(tt(diff[:, 0:PAD], src[:, PAD:2 * PAD], rcount[:, i, :], ALU.mult))
                tt(diff[:, 0:PAD], diff[:, 0:PAD], rows[0][:, PAD:2 * PAD], ALU.subtract).then_inc(val_ready, 1)
                low(pool_lo[:, i, :], diff, pool_hi[:, i, :])
            for g in range(N_GROUPS):
                prep()
                for o in range(2):
                    low(va_lo[:, 2 * o:2 * o + 2, g, :], acc[:, u.k % BANKS, :].rearrange("p (k c) -> p k c", k=2),
                        va_hi[:, 2 * o:2 * o + 2, g, :], acc_free)
                    s.next()
                    u.next()
            prep()
            settle()
            for i in range(4):
                dve.wait_ge(seg_done, s.next())
                nc.vector.tensor_scalar(t(i), acc[:, u.k % BANKS, :], pool_scale[:, i:i + 1], None,
                                        ALU.mult).then_inc(acc_free, 1)
                u.next()
                low(pool_lo[:, i, :], t(i), pool_hi[:, i, :])
            attend(0)
            qk(True)
            attend(1)
            with loop(dve, DC // 4, (n, 6), (s, 16), (u, 16), (fn, 8), (hi, 4), (op, 4)) as i:
                for j in range(2):
                    prep()
                    settle()
                    for o in range(4):
                        dve.wait_ge(seg_done, s.next())
                        nc.vector.tensor_copy(t(o), acc[:, u.k % BANKS, :]).then_inc(acc_free, 1)
                        u.next()
                    dve.wait_ge(acc_free, u.at(BANKS))
                    for k in range(2):
                        prep()
                        s.next(2)
                        for o in range(2):
                            dve.wait_ge(fn_ready, fn.next())
                            tt(t(2 * k + o), t(4 + o), t(2 * k + o), ALU.mult).then_inc(acc_free, 1)
                            u.next()
                        dve.wait_ge(acc_free, u.at(BANKS))
                        tt(t(2 * k), t(2 * k), t(2 * k + 1), ALU.add).then_inc(val_ready, 1)
                        low(m_lo[:, 4 * i + (2 * j + k), :], t(2 * k), m_hi[:, 4 * i + (2 * j + k), :])
            nc.vector.memset(ssq[:], 0.0).then_inc(ssq_ready, 1)
            sq.next()
            with loop(dve, DC // 4, (n, 2), (s, 4), (u, 4), (step, 4), (sq, 4)) as i:
                for j in range(2):
                    prep()
                    for o in range(2):
                        c = 4 * i + (2 * j + o)
                        dve.wait_ge(seg_done, s.next())
                        tt(h[:, c, :], acc[:, u.k % BANKS, :], h[:, c, :], ALU.add).then_inc(acc_free, 1)
                        dve.wait_ge(acc_free, u.next() + BANKS)
                        add_square(h[:, c, :], False)

            final, ret = gains[:, 3, :], gains[:, 4, :]
            tt(gain_sq[:], final, final, ALU.mult)
            tt(gain_ret[:], final, ret, ALU.mult)
            nc.vector.memset(eps_sq[:], EPS * EPS)
            link(nc.vector.tensor_scalar(mean_eps[:], mean_d[:], EPS, None, ALU.mult))
            ffn(2, True)

            rstd_of()
            norm_chunks(gain_ret[:], x_hi, x_lo)
            settle()
            rstd_of()
            for c in range(DC):
                ins = stt(h[:, c, :], h[:, c, :], final[:, c:c + 1], rstd[:], ALU.mult, ALU.mult)
            link(ins)

            dve.wait_ge(ret_landed, 2 * 16)

            def rope_products(o):
                dve.wait_ge(seg_done, s.next(2))
                settle()
                x1, x2 = acc[:, u.k % BANKS, :], acc[:, (u.k + 1) % BANKS, :]
                u.next(2)
                cos, sin = rope_b[:, 0, :], rope_b[:, 1, :]
                tt(t(0), x1, cos, ALU.mult)
                tt(t(1), x2, sin, ALU.mult)
                tt(t(2), x1, sin, ALU.mult)
                tt(t(3), x2, cos, ALU.mult).then_inc(acc_free, 2)

            def rope_sums(o, since=0):
                dve.wait_ge(acc_free, u.at(BANKS - since))
                tt(t(0), t(0), t(1), ALU.subtract).then_inc(val_ready, 1)
                tt(t(2), t(2), t(3), ALU.add).then_inc(val_ready, 1)
                for c in range(RET_KC):
                    low(rqk_lo[:, o, c, :], t(2 * c), rqk_hi[:, o, c, :])

            def ret_rope(o):
                prep()
                rope_products(o)
                rope_sums(o)

            def ret_v(j):
                prep()
                for o in range(2):
                    dst = slice(256 * j, 256 * j + 256)
                    low(rv_lo[:, 2 * o:2 * o + 2, dst], acc[:, u.k % BANKS, :].rearrange("p (k c) -> p k c", k=2),
                        rv_hi[:, 2 * o:2 * o + 2, dst], acc_free)
                    s.next()
                    u.next()

            def gate(dst):
                prep()
                for o in range(2):
                    dve.wait_ge(seg_done, s.next())
                    nc.vector.tensor_copy(dst[:, o, :], acc[:, u.k % BANKS, :]).then_inc(acc_free, 1)
                    u.next()

            def ret_body(head, last):
                ret_v(0)
                settle()
                for m in range(TB):
                    dve.wait_ge(att_full, b.next())
                    tt(t(m, TRI[m]), att[:, (b.k - 1) % BANKS, 0:TRI[m]], decay[:, head, 0:TRI[m]],
                       ALU.mult).then_inc(att_free, 1)
                for m in range(TB):
                    cols = slice(TRI_AT[m], TRI_AT[m] + TRI[m])
                    low(rs_lo[:, cols], t(m, TRI[m]), rs_hi[:, cols])
                ret_v(1)
                gate(r_gate[:, 0:2, :])
                for c in range(RET_VC):
                    dve.wait_ge(att_full, b.next())
                    nc.vector.tensor_copy(r_out[:, c, :], att[:, (b.k - 1) % BANKS, :]).then_inc(att_free, 1)
                dve.wait_ge(att_free, b.at(BANKS))
                link(tt(t(4), r_out[:, 0, :], r_out[:, 1, :], ALU.add))
                link(tt(t(4), t(4), r_out[:, 2, :], ALU.add))
                tt(t(4), t(4), r_out[:, 3, :], ALU.add).then_inc(op_ready, 1)
                op.next()
                gate(r_gate[:, 2:4, :])
                dve.wait_ge(att_full, b.next())
                for c in range(RET_VC):
                    ins = tt(r_out[:, c, :], r_out[:, c, :], att[:, (b.k - 1) % BANKS, :], ALU.subtract)
                ins.then_inc(att_free, 1)
                dve.wait_ge(att_free, b.at(BANKS))
                for c in range(RET_VC):
                    add_square(r_out[:, c, :], c == 0)
                if not last:
                    prep()
                for c in range(RET_VC):
                    dve.wait_ge(fn_ready, fn.next())
                    ins = tt(r_out[:, c, :], r_out[:, c, :], r_gate[:, c, :], ALU.mult)
                ins.then_inc(dve_step, 1)
                gated = step.next()
                if not last:
                    rope_products(0)
                rstd_of(RET_SKIP)
                dve.wait_ge(dve_step, gated)
                for c in range(RET_VC):
                    tt(r_out[:, c, :], r_out[:, c, :], rstd[:], ALU.mult).then_inc(val_ready, 1)
                if not last:
                    prep()
                for c in range(RET_VC):
                    low(rv_lo[:, c, :], r_out[:, c, :], rv_hi[:, c, :])
                if not last:
                    rope_sums(0)
                    rope_products(1)
                    rope_sums(1)
                for j in range(2):
                    prep()
                    for o in range(4):
                        c = 4 * j + o
                        dve.wait_ge(seg_done, s.next())
                        tt(y_ret[:, c, :], acc[:, u.k % BANKS, :], y_ret[:, c, :], ALU.add).then_inc(acc_free, 1)
                        u.next()
                        if last:
                            dve.wait_ge(acc_free, u.at(BANKS))
                            add_square(y_ret[:, c, :], c == 0)

            link(nc.vector.memset(y_ret[:], 0.0))
            for o in range(2):
                ret_rope(o)
            with loop(dve, RET_HEADS - 1, (n, 8), (s, 20), (u, 20), (b, RET_BANKS), (fn, RET_VC + 1),
                      (hi, 4 + TB + RET_VC + 2 * RET_KC), (step, 2 + 3 + 1), (sq, RET_VC),
                      (op, TB + 1 + RET_VC + 2 * RET_KC)) as head:
                ret_body(head, False)
            ret_body(RET_HEADS - 1, True)

            def post_norm(y, gain, done):
                rstd_of()
                for c in range(DC + 1):
                    if c < DC:
                        stt(t(c % 4), y[:, c, :], gains[:, gain, c:c + 1], rstd[:], ALU.mult, ALU.mult).then_inc(dve_step, 1)
                        step.next()
                    if c:
                        dve.wait_ge(dve_step, step.at(-1 if c < DC else 0))
                        tt(h[:, c - 1, :], h[:, c - 1, :], t((c - 1) % 4), ALU.add).then_inc(done, 1)

            settle()
            post_norm(y_ret, 5, val_ready)

            rstd_of()
            norm_chunks(gains[:, 6, :], kv_hi, kv_lo)
            prep()
            norm_chunks(gains[:, 7, :], x_hi, x_lo, 0, 2)
            for k in range(TB):
                low(sv_lo[:, k, :], acc[:, u.k % BANKS, 0:256], sv_hi[:, k, :], acc_free)
                s.next()
                u.next()
            norm_chunks(gains[:, 7, :], x_hi, x_lo, 2)
            link(nc.vector.memset(y_sb[:], 0.0))

            def sb_kq():
                prep()
                for o in range(2):
                    low(skq_lo[:, o, :], acc[:, u.k % BANKS, :], skq_hi[:, o, :], acc_free)
                    s.next()
                    u.next()

            def sb_v():
                prep()
                for o in range(2):
                    low(sv_lo[:, 2 * o:2 * o + 2, :], acc[:, u.k % BANKS, :].rearrange("p (k c) -> p k c", k=2),
                        sv_hi[:, 2 * o:2 * o + 2, :], acc_free)
                    s.next()
                    u.next()

            def sb_out(first, last):
                for c in range(first, last):
                    dve.wait_ge(seg_done, s.next())
                    tt(y_sb[:, c, :], acc[:, u.k % BANKS, :], y_sb[:, c, :], ALU.add).then_inc(acc_free, 1)
                    u.next()

            SCALE = float(P) ** -0.5

            z, e = tmp[:, 0:TRI_COLS], tmp[:, TRI_COLS:2 * TRI_COLS]

            def take_gate(o):
                dve.wait_ge(seg_done, s.next())
                nc.vector.tensor_copy(s_gate[:, o, :], acc[:, u.k % BANKS, :]).then_inc(acc_free, 1)
                u.next()

            def sb_body(first, last):
                prep()
                settle()
                for m in range(TB):
                    at, bank = TRI_AT[m], b.k % BANKS
                    dve.wait_ge(att_full, b.next())
                    if TRI[m] > P:
                        nc.vector.tensor_scalar(z[:, at + P:at + TRI[m]], att[:, bank, P:TRI[m]], SCALE, None, ALU.mult)
                    stt(z[:, at:at + P], att[:, bank, 0:P], SCALE, diag_neg[:], ALU.mult, ALU.add).then_inc(att_free, 1)
                dve.wait_ge(att_free, b.at(BANKS))
                stt(e, z, -1.0, z, ALU.mult, ALU.min).then_inc(val_ready, 1)
                take_gate(0)
                take_gate(1)
                dve.wait_ge(fn_ready, fn.next())
                stt(e, z, 0.0, e, ALU.max, ALU.add).then_inc(val_ready, 1)
                if not first:
                    sb_out(0, 2)
                low(sp_lo[:], e, sp_hi[:])
                if not first:
                    sb_out(2, 4)
                    prep()
                    sb_out(4, DC)
                settle()
                for m in range(TB):
                    zm = z[:, TRI_AT[m]:TRI_AT[m] + TRI[m]]
                    dve.wait_ge(att_full, b.next())
                    tt(zm, zm, att[:, (b.k - 1) % BANKS, 0:TRI[m]], ALU.subtract).then_inc(att_free, 1)
                low(sp_lo[:], e, sp_hi[:])
                if not last:
                    sb_kq()
                for d in range(SB_VC):
                    dve.wait_ge(att_full, b.next())
                    dve.wait_ge(fn_ready, fn.next())
                    tt(s_gate[:, d, :], s_gate[:, d, :], att[:, (b.k - 1) % BANKS, :], ALU.mult).then_inc(att_free, 1)
                for d in range(SB_VC):
                    low(so_lo[:, d, :], s_gate[:, d, :], so_hi[:, d, :])
                if not last:
                    sb_v()

            sb_kq()
            sb_body(True, False)
            with loop(dve, SB_HEADS // 2 - 1, (n, 8), (s, 28), (u, 28), (b, 2 * (2 * TB + SB_VC)),
                      (fn, 2 * (1 + SB_VC)), (hi, 2 * (2 + SB_VC + 4)), (op, 2 * (2 + SB_VC))):
                for j in range(2):
                    sb_body(False, False)
            sb_body(False, True)
            settle()
            squared.next(DC)
            for c in range(DC):
                sb_out(c, c + 1)
                if c:
                    sum_square(c - 1)
            sum_square(DC - 1)
            post_norm(y_sb, 8, h_ready)

        @block.tensor
        def _(pe):
            n, u, b = Count(), Count(), Count()
            op, sq, prob = Count(), Count(), Count()
            staged = Count()
            mm = nc.tensor.matmul

            def slab():
                pe.wait_ge(w_ready, n.at(RING + 1))
                slot = n.k % RING
                n.next()
                return lambda i, width=BLK: (w_hi[:, slot, i * width:(i + 1) * width],
                                             w_lo[:, slot, i * width:(i + 1) * width])

            def bank():
                pe.wait_ge(acc_free, u.at(1))
                u.next()
                return acc[:, (u.k - 1) % BANKS, :]

            def side_bank():
                pe.wait_ge(att_free, b.at(1))
                b.next()
                return att[:, (b.k - 1) % BANKS, :]

            def passes(dst, still, move, first, last):
                mm(dst, still[0], move[0], start=first, stop=False)
                mm(dst, still[0], move[1], start=False, stop=False)
                return mm(dst, still[1], move[0], start=False, stop=last)

            def project(w, first_block, x, chunks=DC, wait=None):
                dst = bank()
                for c in range(chunks):
                    if wait is not None:
                        pe.wait_ge(op_ready, op.at(wait - op.k + c + 1))
                    last = passes(dst, w(first_block + c), (x[0][:, c, :], x[1][:, c, :]), c == 0, c == chunks - 1)
                last.then_inc(seg_done, 1)

            def values(x, blocks):
                w = slab()
                for k in range(TB):
                    if k % 2 == 0:
                        dst = bank()
                    for c in range(DC):
                        last = passes(dst[:, 256 * (k % 2):256 * (k % 2) + 256],
                                      (x[0][:, c, blocks[k]], x[1][:, c, blocks[k]]), w(c, 256), c == 0, c == DC - 1)
                    if k % 2:
                        last.then_inc(seg_done, 1)

            def mean_square(skip=0, mean=mean_d):
                pe.wait_ge(ssq_ready, sq.at())
                dst = side_bank()
                b.next(skip)
                mm(dst, mean[:], ssq[:], start=True, stop=True).then_inc(att_full, 1 + skip)

            x = (x_hi, x_lo)

            def pair(wait=None):
                w = slab()
                dst = bank(), bank()
                for c in range(DC):
                    if wait is not None:
                        pe.wait_ge(op_ready, wait + c + 1)
                    for o in range(2):
                        last = passes(dst[o], w(o * DC + c), (x[0][:, c, :], x[1][:, c, :]), c == 0, c == DC - 1)
                        if c == DC - 1:
                            last.then_inc(seg_done, 1)

            def ffn(adds):
                sq.next(adds)
                mean_square()
                at = op.k
                op.next(DC)
                with loop(pe, FC // 2, (n, 2), (u, 4), (op, 2)):
                    for j in range(2):
                        pair(at if j == 0 else None)
                    op.next(2)
                with loop(pe, DC // 4, (n, 8), (u, 4)):
                    for j in range(4):
                        dst = bank()
                        for half in range(2):
                            w = slab()
                            k0 = half * FC // 2
                            if j == 0:
                                pe.wait_ge(op_ready, op.at(k0 + FC // 2 - FC))
                            for k in range(FC // 2):
                                last = passes(dst, w(k), (g_hi[:, k0 + k, :], g_lo[:, k0 + k, :]),
                                              k0 + k == 0, k0 + k == FC - 1)
                            last.then_inc(seg_done, 1)

            pe.wait_ge(const_ready, 1)
            ffn(DC)

            plain = [slice(P * k, P * k + P) for k in range(TB)]
            strided = [slice(r, None, DIL) for r in range(DIL)]
            sq.next(1 + DC)
            mean_square()
            normed = op.k
            op.next(DC)

            def rotate(o):
                dst = side_bank()
                cols = slice(o * TOK, (o + 1) * TOK)
                mm(dst, rot_r[:], stage_hi[:, cols], start=True, stop=False)
                mm(dst, rot_r[:], stage_lo[:, cols], start=False, stop=True).then_inc(att_full, 1)

            def qk(last):
                for g in range(N_GROUPS):
                    if g == 0 and not last:
                        pair(normed)
                    else:
                        w = slab()
                    for o in range(2):
                        if g or last:
                            project(w, o * DC, x)
                        if (g, o) != (0, 0):
                            pe.wait_ge(op_ready, op.next())
                            rotate(1 - o)
                            op.next()
                if last:
                    pe.wait_ge(op_ready, op.next())
                    rotate(1)
                    op.next()

            def attend(a):
                def scores(k):
                    r, rows = k // 2, slice(HEAD * (k % 2), HEAD * (k % 2) + HEAD)
                    for g in range(N_GROUPS):
                        if g < 2:
                            dst = side_bank()
                        keys = slice(None) if g == 0 else strided[r]
                        width = TOK if g == 0 else P
                        at = P if g == 2 else 0
                        last = passes(dst[:, at:at + width],
                                      (qk_hi[rows, 0, g, strided[r]], qk_lo[rows, 0, g, strided[r]]),
                                      (qk_hi[rows, 1, g, keys], qk_lo[rows, 1, g, keys]), True, True)
                    last.then_inc(att_full, 2)

                def turn(k):
                    pe.wait_ge(prob_ready, prob.next())
                    dst = bank(), bank()
                    for i in range(KEYS // P):
                        at = KEYS * (k % 4) + P * i
                        last = nc.tensor.transpose(dst[i // 4][:, P * (i % 4):P * (i % 4) + P], tmp[:, at:at + P], ident[:])
                    last.then_inc(turned, 1)

                first = u.k
                scores(0)
                scores(1)
                turn(0)
                for k in range(UNITS):
                    if k + 2 < UNITS:
                        scores(k + 2)
                    if k + 1 < UNITS:
                        turn(k + 1)
                    pe.wait_ge(stage_ready, staged.next())
                    dst = acc[:, (first + 2 * k + 1) % BANKS, KEYS - TOK:KEYS - TOK + HEAD]
                    head = slice(HEAD * (2 * a + k % 2), HEAD * (2 * a + k % 2) + HEAD)
                    for i in range(KEYS // P):
                        g, k_blk = (0, i) if i < TB else (i - TB + 1, k // 2)
                        at = KEYS * (k % 2) + P * i
                        last = passes(dst, (stage_hi[:, at:at + P], stage_lo[:, at:at + P]),
                                      (va_hi[:, k_blk, g, head], va_lo[:, k_blk, g, head]), i == 0, i == KEYS // P - 1)
                    last.then_inc(mixed, 1)
                pe.wait_ge(acc_free, u.at(BANKS))
                dst = side_bank()
                for r in range(DIL):
                    last = nc.tensor.transpose(dst[:, P * r:P * r + P], o_tok[:, 2 * r:2 * r + 2, :].rearrange("p k d -> p (k d)"),
                                               ident[:])
                last.then_inc(att_full, 1)

            qk(False)
            for i in range(4):
                if i % 2 == 0:
                    w = slab()
                project(w, DC * (i % 2), x)
                if i == 0:
                    pe.wait_ge(op_ready, op.next())
                    rotate(1)
                    op.next()
            for g in range(N_GROUPS):
                values(x, plain if g == 0 else strided)
            v_at = u.k
            w = slab()
            for i in range(4):
                pe.wait_ge(op_ready, op.next())
                passes(bank(), w(i), (pool_hi[:, i, :], pool_lo[:, i, :]), True, True).then_inc(seg_done, 1)
            op.next(4)
            pe.wait_ge(acc_free, v_at + BANKS)
            attend(0)
            qk(True)
            pe.wait_ge(op_ready, op.at())
            attend(1)
            pe.wait_ge(att_free, b.at(BANKS))
            with loop(pe, DC // 4, (n, 6), (u, 16)):
                for j in range(2):
                    w = slab()
                    for k in range(2):
                        project(w, 6 * k, (o_hi, o_lo), 2)
                        project(w, 6 * k + 2, (pool_hi, pool_lo), 4)
                    for k in range(2):
                        w = slab()
                        project(w, 0, x)
                        project(w, DC, x)
            at = op.k
            op.next(DC)
            with loop(pe, DC // 4, (n, 2), (u, 4)):
                for j in range(2):
                    w = slab()
                    project(w, 0, (m_hi, m_lo), wait=at if j == 0 else None)
                    project(w, DC, (m_hi, m_lo))

            ffn(1 + DC)

            sq.next(1 + DC)
            pe.wait_ge(ssq_ready, sq.at())
            dst = side_bank()
            mm(dst, mean_d[:], gsq[:], start=True, stop=False)
            mm(dst, mean_eps[:], ssq[:], start=False, stop=True).then_inc(att_full, 1)
            mean_square()

            normed = op.k
            op.next(DC)

            def ret_body(last):
                values(x, plain)
                pe.wait_ge(op_ready, op.at())
                for m in range(TB):
                    dst = side_bank()
                    for c in range(RET_KC):
                        ins = passes(dst[:, 0:TRI[m]], (rqk_hi[:, 1, c, plain[m]], rqk_lo[:, 1, c, plain[m]]),
                                     (rqk_hi[:, 0, c, P * m:], rqk_lo[:, 0, c, P * m:]), c == 0, c == RET_KC - 1)
                    ins.then_inc(att_full, 1)
                values(x, plain)
                pair()
                op.next(TB)
                pe.wait_ge(op_ready, op.at())
                pe.wait_ge(acc_free, u.at(BANKS - 2))
                for c in range(RET_VC):
                    dst = side_bank()
                    for m in range(TB):
                        cols = slice(TRI_AT[m], TRI_AT[m] + TRI[m])
                        ins = passes(dst[:, P * m:], (rv_hi[:, m, P * c:P * c + P], rv_lo[:, m, P * c:P * c + P]),
                                     (rs_hi[:, cols], rs_lo[:, cols]), m == 0, m == TB - 1)
                    ins.then_inc(att_full, 1)
                pair()
                pe.wait_ge(op_ready, op.next())
                mm(side_bank(), mean_v[:], t(4), start=True, stop=True).then_inc(att_full, 1)
                if not last:
                    pair()
                sq.next(RET_VC)
                mean_square(RET_SKIP, mean_v)
                if not last:
                    pair()
                normed = op.k
                op.next(RET_VC)
                if not last:
                    op.next(2 * RET_KC)
                for j in range(2):
                    w = slab()
                    for o in range(4):
                        project(w, 4 * o, (rv_hi, rv_lo), 4, wait=normed if j + o == 0 else None)

            for o in range(2):
                pair(normed if o == 0 else None)
                op.next(RET_KC)
            with loop(pe, RET_HEADS - 1, (n, 8), (u, 20), (b, RET_BANKS), (op, TB + 1 + RET_VC + 2 * RET_KC),
                      (sq, RET_VC)):
                ret_body(False)
            ret_body(True)
            sq.next(DC)
            mean_square()
            dst = side_bank()
            for c in range(DC):
                pe.wait_ge(sq_ready, DC + c + 1)
                ins = mm(dst, mean_d[:], y_ret[:, c, :], start=c == 0, stop=c == DC - 1)
            ins.then_inc(att_full, 1)

            kv = (kv_hi, kv_lo)

            def sb_kq():
                w = slab()
                project(w, 0, kv)
                project(w, DC, x)

            def sb_out():
                pe.wait_ge(op_ready, op.at())
                w = slab()
                for c in range(DC):
                    project(w, SB_VC * c, (so_hi, so_lo), SB_VC)

            def sb_body(first, last):
                pe.wait_ge(acc_free, u.at(BANKS - (0 if first else 2)))
                for m in range(TB):
                    passes(side_bank()[:, 0:TRI[m]], (skq_hi[:, 0, plain[m]], skq_lo[:, 0, plain[m]]),
                           (skq_hi[:, 1, P * m:], skq_lo[:, 1, P * m:]), True, True).then_inc(att_full, 1)
                pair()
                if not first:
                    sb_out()
                pe.wait_ge(op_ready, op.next())
                for m in range(TB):
                    dst = side_bank()
                    for k in range(m, TB):
                        cols = slice(TRI_AT[k], TRI_AT[k] + TRI[k])
                        still = tri_r if k == m else ones_r
                        mm(dst[:, P * (k - m):TRI[m]], still[:], sp_hi[:, cols], start=k == m, stop=False)
                        ins = mm(dst[:, P * (k - m):TRI[m]], still[:], sp_lo[:, cols], start=False, stop=k == TB - 1)
                    ins.then_inc(att_full, 1)
                if not last:
                    sb_kq()
                pe.wait_ge(op_ready, op.next())
                pe.wait_ge(acc_free, u.at(BANKS - 2 - (0 if first else DC) - (0 if last else 2)))
                for d in range(SB_VC):
                    dst = side_bank()
                    for m in range(TB):
                        cols = slice(TRI_AT[m], TRI_AT[m] + TRI[m])
                        ins = passes(dst[:, P * m:], (sv_hi[:, m, P * d:P * d + P], sv_lo[:, m, P * d:P * d + P]),
                                     (sp_hi[:, cols], sp_lo[:, cols]), m == 0, m == TB - 1)
                    ins.then_inc(att_full, 1)
                if not last:
                    values(kv, plain)
                op.next(SB_VC)

            w = slab()
            dst = [bank() for k in range(TB)]
            for c in range(DC):
                pe.wait_ge(op_ready, op.next())
                for k in range(TB):
                    last = passes(dst[k][:, 0:256], (kv_hi[:, c, plain[k]], kv_lo[:, c, plain[k]]), w(c, 256),
                                  c == 0, c == DC - 1)
                    if c == DC - 1:
                        last.then_inc(seg_done, 1)
            w = slab()
            project(w, 0, kv)
            project(w, DC, x, wait=op.k)
            op.next(DC)
            sb_body(True, False)
            with loop(pe, SB_HEADS // 2 - 1, (n, 8), (u, 28), (b, 2 * (2 * TB + SB_VC)), (op, 2 * (2 + SB_VC))):
                for j in range(2):
                    sb_body(False, False)
            sb_body(False, True)
            sb_out()
            sq.next(DC)
            mean_square()



def tiles(w):
    k, n = w.shape
    return w.reshape(k // P, P, n // P, P).transpose(2, 1, 0, 3)


def columns(w, first, width):
    return w[:, first:first + width].reshape(-1, P, width).transpose(1, 0, 2)


def lay_out(a):
    w = {}
    for f in ("ffn1", "ffn2"):
        up, lin = tiles(a[f + "_w1"][0]), tiles(a[f + "_w3"][0])
        w[f + "_up"] = np.stack([up, lin], 2).reshape(FC, P, SLAB)
        down = tiles(a[f + "_w2"][0]).reshape(DC, P, 2, FC // 2 * BLK)
        w[f + "_down"] = down.transpose(0, 2, 1, 3).reshape(2 * DC, P, FC // 2 * BLK)
    w_in = a["w_in"][0]
    heads = N_GROUPS * GROUP_HEADS * HEAD
    cols = tiles(w_in)
    qc = heads // P
    w["mix_qk"] = np.stack([np.stack([np.stack([cols[2 * g + c], cols[qc + 2 * g + c]], 1)
                                      for g in range(N_GROUPS)]) for c in range(2)]).reshape(2, N_GROUPS, P, SLAB)
    w["mix_v"] = np.stack([columns(w_in, 2 * heads + 256 * g, 256) for g in range(N_GROUPS)]).reshape(N_GROUPS, P, SLAB)
    pc, gc = 3 * qc, 3 * qc + len(POOL_WINDOWS)
    w["mix_pool"] = cols[pc:gc].reshape(2, 2, P, DC * BLK).transpose(0, 2, 1, 3).reshape(2, P, SLAB)
    w["pool_w"] = a["pool_w"][0].transpose(1, 0, 2).reshape(P, 4 * BLK)
    w["mix_branch"] = np.concatenate([tiles(a["w_branch_attn"][0]), tiles(a["w_branch_pool"][0])], 2)
    w["mix_branch"] = w["mix_branch"].reshape(DC // 2, 2, P, 6 * BLK).transpose(0, 2, 1, 3).reshape(DC // 2, P, 12 * BLK)
    w["mix_gate"] = np.stack([cols[gc:gc + DC], cols[gc + DC:gc + 2 * DC]], 2).reshape(DC, P, SLAB)

    def pairs(c):
        return c.reshape(-1, 2, P, DC * BLK).transpose(0, 2, 1, 3).reshape(-1, P, SLAB)

    w["mix_out"] = pairs(tiles(a["w_out"][0]))
    r = a["ret_w_in_2"][0]
    rp = pairs(tiles(r))
    keys = RET_HEADS * RET_KC * P
    vals = RET_HEADS * RET_VC * P
    gates = (2 * keys + vals) // 256
    w["ret_head"] = np.stack([np.stack(
        [rp[i], rp[RET_HEADS + i]]
        + [columns(r, 2 * keys + TOK * i + 256 * j, 256).reshape(P, SLAB) for j in range(2)]
        + [rp[gates + 2 * i + j] for j in range(2)]) for i in range(RET_HEADS)])
    ro = tiles(a["ret_w_out_2"][0])
    w["ret_out"] = np.stack([np.stack([ro[4 * j:4 * j + 4, :, RET_VC * i:RET_VC * (i + 1)].transpose(1, 0, 2, 3).reshape(P, SLAB)
                                       for j in range(2)]) for i in range(RET_HEADS)])
    kv, sbi, sbo = a["w_kv_2"], a["sb_w_in_2"][0], tiles(a["sb_w_out_2"][0])
    kt, st = tiles(kv), tiles(sbi)
    w["sb_kq"] = np.stack([kt[:SB_HEADS], st[:SB_HEADS]], 2).reshape(SB_HEADS, P, SLAB)
    w["sb_v"] = np.stack([columns(kv, SB_HEADS * P + 256 * i, 256) for i in range(SB_HEADS)]).reshape(SB_HEADS, P, SLAB)
    w["sb_g"] = pairs(st[SB_HEADS:])
    w["sb_out"] = np.stack([sbo[:, :, SB_VC * i:SB_VC * (i + 1)].transpose(1, 0, 2, 3).reshape(P, SLAB) for i in range(SB_HEADS)])
    w["x"] = a["x"][0].T.reshape(DC, P, TOK).transpose(1, 0, 2)
    w["gains"] = np.stack([a[g].reshape(DC, P).T for g in GAINS], 1)
    w["pool_scale"] = a["pool_scale"][0].reshape(-1, P).T
    return w


def constants():
    f = np.float32
    c = {"ident": np.eye(P, dtype=f), "mean_d": np.full((P, P), 1 / D, f), "mean_v": np.full((P, P), 1 / TOK, f)}
    i, j = np.arange(P)[:, None], np.arange(P)[None, :]
    c["diag_neg"] = np.where(i >= j, f(NEG), f(0))
    half = HEAD // 8
    rot = np.zeros((P, P), f)
    for m in range(P):
        d = m % HEAD
        if d < half:
            rot[m + half, m] = -1
        elif d < 2 * half:
            rot[m - half, m] = 1
    c["signs"] = np.stack([rot, (i >= j).astype(f), np.ones((P, P), f)], 1)
    pos = np.arange(TOK, dtype=f)
    inv = (f(500000.0) ** (-np.arange(0, 2 * half, 2, dtype=f) / f(2 * half))).astype(f)
    cos, sin = np.ones((P, TOK), f), np.zeros((P, TOK), f)
    for m in range(P):
        if m % HEAD < 2 * half:
            ang = pos * inv[m % HEAD % half]
            cos[m], sin[m] = np.cos(ang), np.sin(ang)
    c["rope_a"] = np.stack([cos, sin], 1)
    dist = DIL * np.arange(P)[:, None] + DIL - 1 - np.arange(TOK + DIL - 1)[None, :]
    c["band"] = np.where((dist >= 0) & (dist <= 128), f(0), f(NEG)).astype(mybir.dt.np(mybir.dt.bfloat16))
    c["classes"] = np.stack([np.where(j <= i, f(0), f(NEG)),
                             np.where((j <= i) & ((i - j) % 4 == 0), f(0), f(NEG))], 1)
    first = np.arange(1, PAD + 1, dtype=f)
    c["rcount"] = np.broadcast_to(np.stack([f(1) / np.minimum(first, f(w)) for w in POOL_WINDOWS]), (P, 4, PAD)).astype(f)
    freq = (f(1) / (f(10000.0) ** (np.arange(P, dtype=f) / f(P)))).astype(f)
    ang = pos[None, :] * freq[:, None]
    c["rope_b"] = np.stack([np.cos(ang), np.sin(ang)], 1)
    lag = np.arange(TOK)[None, :] - np.arange(P)[:, None]
    gam = np.log1p(-np.exp2(-5.0 - np.arange(RET_HEADS)))
    dec = np.where(lag[:, None, :] >= 0, np.exp(gam[None, :, None] * np.maximum(lag, 0)[:, None, :]), 0)
    c["decay"] = (dec * (RET_KC * P) ** -0.5).astype(f)
    return c


def kernel(**inputs):
    import concourse.bacc as bacc
    from concourse.bass_utils import run_bass_kernel_spmd

    laid = lay_out({k: np.asarray(v) for k, v in inputs.items()})
    laid.update(constants())
    nc = bacc.Bacc("TRN2", target_bir_lowering=False, num_devices=1)
    arrays, dram = {}, {}
    for name, a in laid.items():
        a = np.ascontiguousarray(a)
        arrays[f"in_{name}"] = a
        dram[name] = nc.dram_tensor(f"in_{name}", a.shape, mybir.dt.from_np(a.dtype), kind="ExternalInput").ap()
    out = nc.dram_tensor("result", (P, DC, TOK), F32, kind="ExternalOutput").ap()
    block_kernel(nc, dram, out)
    got = run_bass_kernel_spmd(nc, [arrays], core_ids=[0]).results[0]["result"]
    return np.ascontiguousarray(got.transpose(1, 0, 2).reshape(D, TOK).T)[None]
```

```python
from contextlib import ExitStack, contextmanager

import numpy as np

import concourse.bass as bass
from concourse import mybir

F32 = mybir.dt.float32
F32R = mybir.dt.float32r
ALU = mybir.AluOpType
ACT = mybir.ActivationFunctionType
AX_X = mybir.AxisListType.X

P = 128
TOK = 512
D = 1024
DC = D // P
FF = 2816
FC = FF // P
BLK = P * P // P
SLAB = 16 * BLK
RING = 2
BANKS = 4
EPS = 1e-6
NEG = -1e30

N_GROUPS, GROUP_HEADS, HEAD = 3, 4, 64
DIL = 4
UNITS = 2 * DIL
KEYS = TOK + 2 * P
POOL_WINDOWS = (2, 4, 8, 16)
PAD = max(POOL_WINDOWS)
RET_HEADS, RET_KC, RET_VC = 4, 2, 4
SB_HEADS, SB_VC = 8, 2
TB = TOK // P
TRI = [TOK - P * m for m in range(TB)]
TRI_AT = [sum(TRI[:m]) for m in range(TB)]
TRI_COLS = sum(TRI)
RET_SKIP = -(TB + RET_VC + 2) % BANKS
RET_BANKS = TB + RET_VC + 2 + RET_SKIP

GAINS = ["ffn1_norm", "mix_norm", "ffn2_norm", "final_norm", "ret_norm_pre_2", "ret_norm_post_2",
         "kv_norm_2", "sb_norm_pre_2", "sb_norm_post_2"]


class Count:

    def __init__(self):
        self.k, self.turn, self.per = 0, None, 0

    def at(self, extra=0):
        return self.k + extra if self.turn is None else self.turn * self.per + (self.k + extra)

    def landed(self):
        first = 16 * (self.k // RING + 1)
        return first if self.turn is None else self.turn * (16 * self.per // RING) + first

    def next(self, by=1):
        self.k += by
        return self.at()


@contextmanager
def loop(eng, times, *steps):
    with eng.Fori(0, times) as i:
        begin = [c.k for c, _ in steps]
        for c, per in steps:
            c.turn, c.per = i, per
        yield i
        for (c, per), k in zip(steps, begin):
            assert c.k == k + per, (c.k - k, per)
            c.turn, c.k = None, k + per * times


def block_kernel(nc, dram, out):
    with ExitStack() as ctx:
        def sb(name, shape, dt=F32, scope=ctx):
            return scope.enter_context(nc.sbuf_tensor(name, shape, dt))

        def sem(name):
            return ctx.enter_context(nc.semaphore(name))

        h = sb("h", [P, DC, TOK])
        raw = sb("raw", [P, RING, SLAB])
        w_hi = sb("w_hi", [P, RING, SLAB], F32R)
        w_lo = sb("w_lo", [P, RING, SLAB], F32R)
        x_hi = sb("x_hi", [P, DC, TOK], F32R)
        x_lo = sb("x_lo", [P, DC, TOK], F32R)
        tmp = sb("tmp", [P, 6 * TOK])
        ssq = sb("ssq", [P, TOK])
        rstd = sb("rstd", [P, TOK])
        r_tok = sb("r_tok", [P, 2 * TB])
        z_scale = sb("z_scale", [P, TB])
        gains = sb("gains", [P, len(GAINS), DC])
        pool_scale = sb("pool_scale", [P, len(POOL_WINDOWS)])
        ident = sb("ident", [P, P])
        mean_d = sb("mean_d", [P, P])
        mean_v = sb("mean_v", [P, P])
        diag_neg = sb("diag_neg", [P, P])
        rot_r = sb("rot_r", [P, P], F32R)
        tri_r = sb("tri_r", [P, P], F32R)
        ones_r = sb("ones_r", [P, P], F32R)
        eps = sb("eps", [P, 1])

        signs = tmp[:, 4 * TOK:4 * TOK + 3 * P].rearrange("p (k c) -> p k c", k=3)
        o_unit = tmp[:, 3 * TOK:5 * TOK].rearrange("p (k q) -> p k q", q=P)
        diag = tmp[:, 5 * TOK:5 * TOK + 2 * P].rearrange("p (k q) -> p k q", q=P)

        def t(i, width=TOK):
            return tmp[:, i * TOK:i * TOK + width]

        def by_blocks(v):
            return v.rearrange("p (i q) -> p i q", q=P)

        def by_heads(v):
            return v.rearrange("p (h d) -> p h d", d=HEAD)

        def value_slot(g, head):
            return head if g == 0 else GROUP_HEADS * (1 + head // 2) + 2 * (g - 1) + head % 2

        def whole_row(v):
            return v.unsqueeze(1)

        with ExitStack() as scope:
            g_hi = sb("g_hi", [P, FC, TOK], F32R, scope)
            g_lo = sb("g_lo", [P, FC, TOK], F32R, scope)
            gsq = sb("gsq", [P, TOK], F32, scope)
            mean_eps = sb("mean_eps", [P, P], F32, scope)
            gain_sq = sb("gain_sq", [P, DC], F32, scope)
            gain_ret = sb("gain_ret", [P, DC], F32, scope)
            eps_sq = sb("eps_sq", [P, 1], F32, scope)
        with ExitStack() as scope:
            o_hi = sb("o_hi", [P, 2, TOK], F32R, scope)
            o_lo = sb("o_lo", [P, 2, TOK], F32R, scope)
            pool_hi = sb("pool_hi", [P, 4, TOK], F32R, scope)
            pool_lo = sb("pool_lo", [P, 4, TOK], F32R, scope)
            with ExitStack() as inner:
                qk_hi = sb("qk_hi", [P, 2, N_GROUPS, TOK], F32R, inner)
                qk_lo = sb("qk_lo", [P, 2, N_GROUPS, TOK], F32R, inner)
                va = sb("va", [P, TB, N_GROUPS * GROUP_HEADS, 2, HEAD], F32R, inner)
                stage = sb("stage", [P, 4 * KEYS], F32R, inner)
                fold = sb("fold", [P, 3 * HEAD], F32, inner)
                rope_a = sb("rope_a", [P, 2, TOK], F32, inner)
                band = sb("band", [P, TOK + DIL - 1], mybir.dt.bfloat16, inner)
                classes = sb("classes", [P, 2, P], F32, inner)
                neg_max = sb("neg_max", [P, UNITS], F32, inner)
                den = sb("den", [P, UNITS], F32, inner)
                rden = sb("rden", [P, UNITS], F32, inner)
                rcount = sb("rcount", [P, 4, PAD], F32, inner)
            with ExitStack() as inner:
                m_hi = sb("m_hi", [P, DC, TOK], F32R, inner)
                m_lo = sb("m_lo", [P, DC, TOK], F32R, inner)
        with ExitStack() as scope:
            y_ret = sb("y_ret", [P, DC, TOK], F32, scope)
            rqk_hi = sb("rqk_hi", [P, 2, RET_KC, TOK], F32R, scope)
            rqk_lo = sb("rqk_lo", [P, 2, RET_KC, TOK], F32R, scope)
            rv_hi = sb("rv_hi", [P, TB, TOK], F32R, scope)
            rv_lo = sb("rv_lo", [P, TB, TOK], F32R, scope)
            rs_hi = sb("rs_hi", [P, TRI_COLS], F32R, scope)
            rs_lo = sb("rs_lo", [P, TRI_COLS], F32R, scope)
            r_gate = sb("r_gate", [P, RET_VC, TOK], F32, scope)
            r_out = sb("r_out", [P, RET_VC, TOK], F32, scope)
            rope_b = sb("rope_b", [P, 2, TOK], F32, scope)
            decay = sb("decay", [P, RET_HEADS, TOK], F32, scope)
            r_head = sb("r_head", [P, TOK], F32, scope)
            r_final = sb("r_final", [P, TOK], F32, scope)
        with ExitStack() as scope:
            y_sb = sb("y_sb", [P, DC, TOK], F32, scope)
            kv_hi = sb("kv_hi", [P, DC, TOK], F32R, scope)
            kv_lo = sb("kv_lo", [P, DC, TOK], F32R, scope)
            skq_hi = sb("skq_hi", [P, 2, TOK], F32R, scope)
            skq_lo = sb("skq_lo", [P, 2, TOK], F32R, scope)
            sv_hi = sb("sv_hi", [P, TB, 256], F32R, scope)
            sv_lo = sb("sv_lo", [P, TB, 256], F32R, scope)
            sp_hi = sb("sp_hi", [P, TRI_COLS], F32R, scope)
            sp_lo = sb("sp_lo", [P, TRI_COLS], F32R, scope)
            s_gate = sb("s_gate", [P, SB_VC, TOK], F32, scope)
            so_hi = sb("so_hi", [P, SB_VC, TOK], F32R, scope)
            so_lo = sb("so_lo", [P, SB_VC, TOK], F32R, scope)

        acc = ctx.enter_context(nc.psum_tensor("acc", [P, BANKS, TOK], F32))
        att = ctx.enter_context(nc.psum_tensor("att", [P, BANKS, TOK], F32))

        stage_hi, stage_lo = stage[:, 0:2 * KEYS], stage[:, 2 * KEYS:]
        turned_probs = stage[:].rearrange("p (u i s q) -> p u i s q", u=2, s=2, q=P)

        raw_landed = [sem(f"raw_landed{i}") for i in range(RING)]
        const_landed = sem("const_landed")
        x_landed = [sem(f"x_landed{c}") for c in range(DC)]
        mix_landed = sem("mix_landed")
        ret_landed = sem("ret_landed")
        out_landed = sem("out_landed")
        const_ready = sem("const_ready")
        w_hi_ready = sem("w_hi_ready")
        w_ready = sem("w_ready")
        seg_done = sem("seg_done")
        acc_free = sem("acc_free")
        att_full = sem("att_full")
        att_free = sem("att_free")
        fn_ready = sem("fn_ready")
        prob_ready = sem("prob_ready")
        rden_ready = sem("rden_ready")
        diag_ready = sem("diag_ready")
        turned = sem("turned")
        stage_ready = sem("stage_ready")
        mixed = sem("mixed")
        val_ready = sem("val_ready")
        hi_ready = sem("hi_ready")
        op_ready = sem("op_ready")
        sq_ready = sem("sq_ready")
        ssq_ready = sem("ssq_ready")
        dve_step = sem("dve_step")
        h_ready = sem("h_ready")
        gains_landed = sem("gains_landed")
        y_clear = sem("y_clear")

        block = ctx.enter_context(nc.Block())

        @block.sync
        def _(sp):
            n = Count()

            def fetch(src, cols=SLAB):
                sp.wait_ge(w_ready, n.at(1))
                slot = n.k % RING
                sp.dma_start(raw[:, slot, 0:cols], src).then_inc(raw_landed[slot], 16)
                n.next()

            def ffn(name):
                with loop(sp, FC // 2, (n, 2)) as i:
                    for j in range(2):
                        fetch(dram[name + "_up"][2 * i + j])
                with loop(sp, DC, (n, 2)) as i:
                    for j in range(2):
                        fetch(dram[name + "_down"][2 * i + j], FC // 2 * BLK)

            ffn("ffn1")
            for g in range(N_GROUPS):
                fetch(dram["mix_qk"][0, g])
            for i in range(2):
                fetch(dram["mix_pool"][i])
            for j in range(2):
                fetch(dram["mix_v"][j])
            fetch(dram["pool_w"], 4 * BLK)
            for g in range(N_GROUPS):
                fetch(dram["mix_qk"][1, g])
            fetch(dram["mix_v"][2])
            with loop(sp, DC // 4, (n, 6)) as i:
                for j in range(2):
                    fetch(dram["mix_branch"][2 * i + j], 12 * BLK)
                    for k in range(2):
                        fetch(dram["mix_gate"][4 * i + (2 * j + k)])
            with loop(sp, DC // 4, (n, 2)) as i:
                for j in range(2):
                    fetch(dram["mix_out"][2 * i + j])
            ffn("ffn2")
            for j in range(2):
                fetch(dram["ret_head"][0, j])
            with loop(sp, RET_HEADS - 1, (n, 8)) as i:
                for j in range(2, 6):
                    fetch(dram["ret_head"][i, j])
                for j in range(2):
                    fetch(dram["ret_head"][i + 1, j])
                for j in range(2):
                    fetch(dram["ret_out"][i, j])
            for j in range(2, 6):
                fetch(dram["ret_head"][RET_HEADS - 1, j])
            for j in range(2):
                fetch(dram["ret_out"][RET_HEADS - 1, j])
            fetch(dram["sb_kq"][0])
            fetch(dram["sb_v"][0])
            fetch(dram["sb_g"][0])
            fetch(dram["sb_kq"][1])
            fetch(dram["sb_v"][1])
            with loop(sp, SB_HEADS // 2 - 1, (n, 8)) as i:
                for j in range(2):
                    fetch(dram["sb_g"][2 * i + (j + 1)])
                    fetch(dram["sb_out"][2 * i + j])
                    fetch(dram["sb_kq"][2 * i + (j + 2)])
                    fetch(dram["sb_v"][2 * i + (j + 2)])
            fetch(dram["sb_g"][SB_HEADS - 1])
            fetch(dram["sb_out"][SB_HEADS - 2])
            fetch(dram["sb_out"][SB_HEADS - 1])
            for c in range(DC):
                sp.wait_ge(h_ready, 3 * DC + c + 1)
                sp.dma_start(out[:, c, :], h[:, c, :]).then_inc(out_landed, 16)
            sp.wait_ge(out_landed, 16 * DC)

        FFN_SEGS = FC * 2 + DC * 2
        MIX_SEGS = 3 * 2 + 3 * 2 + 2 * 2 + 4 + 3 * 2 + DC * 4 + DC

        @block.gpsimd
        def _(pool):
            pool.dma_start(gains[:], dram["gains"]).then_inc(gains_landed, 16)
            for dst, name in ((pool_scale, "pool_scale"), (ident, "ident"), (mean_d, "mean_d"),
                              (mean_v, "mean_v"), (diag_neg, "diag_neg"), (signs, "signs")):
                pool.dma_start(dst if name == "signs" else dst[:], dram[name]).then_inc(const_landed, 16)
            pool.wait_ge(seg_done, FFN_SEGS)
            for dst, name in ((rope_a, "rope_a"), (band, "band"), (classes, "classes"), (rcount, "rcount"), (fold, "fold")):
                pool.dma_start(dst[:], dram[name]).then_inc(mix_landed, 16)
            pool.wait_ge(seg_done, 2 * FFN_SEGS + MIX_SEGS)
            for dst, name in ((rope_b, "rope_b"), (decay, "decay")):
                pool.dma_start(dst[:], dram[name]).then_inc(ret_landed, 16)
            nc.gpsimd.memset(y_ret[:], 0.0).then_inc(y_clear, 1)

        @block.scalar
        def _(act):
            n, s, u, b = Count(), Count(), Count(), Count()
            val, turn, inv = Count(), Count(), Count()

            def prep(cols=SLAB):
                slot = n.k % RING
                act.wait_ge(raw_landed[slot], n.landed())
                if s.k:
                    act.wait_ge(seg_done, s.at())
                nc.scalar.activation(w_hi[:, slot, 0:cols], raw[:, slot, 0:cols], ACT.Copy).then_inc(w_hi_ready, 1)
                n.next()

            def split_val(dst, src):
                act.wait_ge(val_ready, val.next())
                nc.scalar.activation(dst, src, ACT.Copy).then_inc(hi_ready, 1)

            def split_acc(dst, src, seg):
                act.wait_ge(seg_done, s.at(seg))
                nc.scalar.activation(dst, src, ACT.Copy).then_inc(hi_ready, 1)

            def std_of(skip=0, bias=eps, dst=5):
                bank = b.k % BANKS
                act.wait_ge(att_full, b.next(1 + skip))
                nc.scalar.activation(t(dst), att[:, bank, :], ACT.Sqrt, bias=bias[:]).then_inc(fn_ready, 1)

            def square(c, src):
                if c >= 4:
                    act.wait_ge(ssq_ready, sq.at(c - 3))
                nc.scalar.activation(t(c % 4), src, ACT.Square).then_inc(sq_ready, 1)

            def weigh(dst, c, gain):
                c = bass.ds(c, 1)
                nc.scalar.activation(dst[:, c, :], h[:, c, :], ACT.Copy, scale=gain[:, c]).then_inc(hi_ready, 1)

            def ffn(next_gain):
                def up(place, first):
                    for j in range(2):
                        prep()
                        if first and j == 0:
                            std_of()
                        act.wait_ge(acc_free, u.at(BANKS + 1))
                        nc.scalar.activation(t(j), t(j), ACT.Silu).then_inc(fn_ready, 1)
                        act.wait_ge(acc_free, u.at(BANKS + 2))
                        nc.scalar.activation(g_hi[:, place(j), :], t(2 + j), ACT.Copy).then_inc(hi_ready, 1)
                        s.next(2)
                        u.next(2)

                up(lambda j: j, True)
                with loop(act, FC // 2 - 1, (n, 2), (s, 4), (u, 4)) as i:
                    up(lambda j: 2 * i + (j + 2), False)
                with loop(act, DC // 4, (n, 8), (s, 8), (u, 4), (hr, 4)) as i:
                    for j in range(4):
                        for half in range(2):
                            prep()
                            s.next()
                        u.next()
                        act.wait_ge(h_ready, hr.next())
                        weigh(x_hi, 4 * i + j, next_gain)

            hr = Count()
            sq = Count()
            for c in range(DC):
                act.dma_start(h[:, c, :], dram["x"][:, c, :]).then_inc(x_landed[c], 16)
            act.wait_ge(gains_landed, 16)
            for c in range(DC):
                act.wait_ge(x_landed[c], 16)
                square(c, h[:, c, :])
                weigh(x_hi, c, gains[:, 0, :])
                if c == 1:
                    prep()
            sq.next(DC + 3 * (1 + DC) + RET_HEADS * RET_VC)
            act.wait_ge(const_ready, 1)
            ffn(gains[:, 1, :])

            def rope_split(o):
                split_acc(stage_hi[:, o * TOK:(o + 1) * TOK], acc[:, u.k % BANKS, :], 1)
                s.next()
                u.next()

            def rope_done(g, o):
                b.next()
                split_val(qk_hi[:, o, g, :], t(o))

            def qk(last):
                for g in range(N_GROUPS):
                    for o in range(2):
                        if o == 0:
                            prep()
                            if g == 0 and not last:
                                std_of()
                                b.next()
                        rope_split(o)
                        if (g, o) != (0, 0):
                            rope_done(g - 1 + o, 1 - o)
                        elif last:
                            gather(0)

            def split_values(dst, o, row, view):
                act.wait_ge(seg_done, s.next())
                for j in range(2):
                    k = 2 * o + j
                    ins = nc.scalar.activation(dst(k), view(acc[:, u.k % BANKS, 256 * j:256 * j + 256]), ACT.Copy, scale=r_tok[:, row + k:row + k + 1])
                ins.then_inc(hi_ready, 1)
                u.next()

            def exps(k):
                at = KEYS * (k % 2)
                b.next(2)
                act.wait_ge(val_ready, val.next())
                nc.scalar.activation(tmp[:, at:at + KEYS], tmp[:, at:at + KEYS], ACT.Exp,
                                     bias=neg_max[:, k:k + 1],
                                     accum_out=den[:, k:k + 1]).then_inc(prob_ready, 1)

            def normalizer(k):
                act.wait_ge(rden_ready, inv.next())
                nc.scalar.activation(diag[:, k % 2, :], ident[:], ACT.Copy, scale=rden[:, k:k + 1]).then_inc(diag_ready, 1)

            def mix_values(j, o):
                heads = slice(GROUP_HEADS * j, GROUP_HEADS * (j + 1))
                split_values(lambda k: va[:, k, heads, 0, :], o, TB if j else 0, by_heads)

            def gather(a):
                act.wait_ge(att_full, b.next())
                nc.scalar.activation(o_hi[:, a, :].rearrange("p (l r) -> p r l", r=DIL),
                                     att[:, (b.k - 1) % BANKS, :].rearrange("p (r l) -> p r l", r=DIL),
                                     ACT.Copy).then_inc(hi_ready, 1)

            def attend(a, between=None):
                def stage(k):
                    probs = turned_probs[:, k % 2, :, 0, :]
                    act.wait_ge(turned, turn.next())
                    nc.scalar.activation(probs[:, 0:TB, :], by_blocks(acc[:, u.k % BANKS, :]), ACT.Copy).then_inc(hi_ready, 1)
                    act.wait_ge(turned, turn.next())
                    nc.scalar.activation(probs[:, TB:, :], by_blocks(acc[:, (u.k + 1) % BANKS, 0:KEYS - TOK]),
                                         ACT.Copy).then_inc(hi_ready, 1)
                    u.next(2)

                stage(0)
                for k in range(UNITS):
                    if k == UNITS - 3 and between is not None:
                        between()
                    if k + 1 < UNITS:
                        stage(k + 1)
                    if k + 2 < UNITS:
                        exps(k + 2)
                        normalizer(k + 2)

            tok_free = b.k + 2 + BANKS
            qk(False)
            act.wait_ge(att_free, tok_free)
            for i in range(4):
                if i % 2 == 0:
                    prep()
                s.next()
                u.next()
                if i == 0:
                    rope_done(N_GROUPS - 1, 1)
                split_val(pool_hi[:, i, :], tmp[:, 3 * (PAD + TOK):3 * (PAD + TOK) + TOK])
            prep()
            mix_values(0, 0)
            mix_values(0, 1)
            prep(4 * BLK)
            exps(0)
            exps(1)

            def pooled():
                for i in range(4):
                    s.next()
                    act.wait_ge(acc_free, u.next() + BANKS)
                    nc.scalar.activation(pool_hi[:, i, :], t(3 + i % 3), ACT.Copy).then_inc(hi_ready, 1)

            mix_values(1, 0)
            pooled()
            normalizer(0)
            normalizer(1)
            mix_values(1, 1)
            attend(0, prep)
            qk(True)
            rope_done(N_GROUPS - 1, 1)
            mix_values(2, 0)
            exps(0)
            normalizer(0)
            mix_values(2, 1)
            exps(1)
            normalizer(1)
            attend(1, prep)
            gather(1)
            with loop(act, DC // 4, (n, 6), (s, 16), (u, 16), (val, 4)) as i:
                for j in range(2):
                    prep()
                    s.next(4)
                    u.next(4)
                    for k in range(2):
                        prep()
                        for o in range(2):
                            act.wait_ge(acc_free, u.next() + BANKS)
                            nc.scalar.activation(t(4 + o), t(4 + o), ACT.Sigmoid).then_inc(fn_ready, 1)
                        s.next(2)
                        split_val(m_hi[:, 4 * i + (2 * j + k), :], t(2 * k))
            with loop(act, DC // 4, (n, 2), (s, 4), (u, 4)) as i:
                for j in range(2):
                    prep()
                    for o in range(2):
                        s.next()
                        act.wait_ge(acc_free, u.next() + BANKS)
                        weigh(x_hi, 4 * i + (2 * j + o), gains[:, 2, :])

            ffn(gain_ret)

            def rope_split_b(o):
                for c in range(RET_KC):
                    split_val(rqk_hi[:, o, c, :], t(2 * c))

            def ret_v(j):
                prep()
                for o in range(2):
                    split_values(lambda k: rv_hi[:, k:k + 1, 256 * j:256 * j + 256], o, 0, whole_row)

            def gate(dst):
                prep()
                for o in range(2):
                    act.wait_ge(acc_free, u.next() + BANKS)
                    nc.scalar.activation(dst[:, o, :], dst[:, o, :], ACT.Silu).then_inc(fn_ready, 1)
                    s.next()

            def outputs(first, end, last):
                for c in range(first, end):
                    val.next()
                    if last:
                        act.wait_ge(val_ready, val.at())
                        square(c, y_ret[:, c, :])

            def ret_body(last):
                ret_v(0)
                for m in range(TB):
                    act.wait_ge(att_free, b.next() + BANKS)
                    nc.scalar.activation(rs_hi[:, TRI_AT[m]:TRI_AT[m] + TRI[m]], t(m, TRI[m]),
                                         ACT.Copy).then_inc(hi_ready, 1)
                ret_v(1)
                gate(r_gate[:, 0:2, :])
                b.next(RET_VC)
                gate(r_gate[:, 2:4, :])
                b.next()
                if not last:
                    prep()
                    s.next(2)
                for c in range(RET_VC):
                    split_val(rv_hi[:, c, :], r_gate[:, c, :])
                if not last:
                    prep()
                    s.next(2)
                    u.next(4)
                    rope_split_b(0)
                prep()
                std_of(RET_SKIP)
                s.next(4)
                u.next(4)
                outputs(0, 2, last)
                if not last:
                    rope_split_b(1)
                outputs(2, 4, last)
                if not last:
                    prep()
                s.next(4)
                u.next(4)
                outputs(4, DC, last)
                if last:
                    prep()

            for o in range(2):
                prep()
                if o == 0:
                    std_of(bias=eps_sq)
                    std_of(dst=4)
                    act.wait_ge(att_free, b.next() + BANKS)
                rope_split_b(o)
                s.next(2)
                u.next(2)
            with loop(act, RET_HEADS - 1, (n, 8), (s, 20), (u, 20), (b, RET_BANKS), (val, 2 * RET_KC + RET_VC + DC)):
                ret_body(False)
            ret_body(True)
            sq.next(DC)
            std_of()

            for c in range(DC):
                act.wait_ge(h_ready, hr.next())
                weigh(kv_hi, c, gains[:, 6, :])
                nc.scalar.activation(y_ret[:, c, :], h[:, c, :], ACT.Square).then_inc(sq_ready, 1)

            for c in range(DC):
                weigh(x_hi, c, gains[:, 7, :])

            def sb_kq(first):
                prep()
                if first:
                    std_of()
                for o in range(2):
                    split_acc(skq_hi[:, o, :], acc[:, u.k % BANKS, :], 1)
                    s.next()
                    u.next()

            def sb_v(first):
                prep()
                if first:
                    act.wait_ge(att_free, b.next() + BANKS)
                for o in range(2):
                    split_values(lambda k: sv_hi[:, k:k + 1, :], o, 0, whole_row)

            z, e = tmp[:, 0:TRI_COLS], tmp[:, TRI_COLS:2 * TRI_COLS]

            def sb_soft():
                b.next(TB)
                act.wait_ge(val_ready, val.next())
                nc.scalar.activation(e, e, ACT.Exp).then_inc(act_step, 1)
                act.wait_ge(act_step, step.next())
                nc.scalar.activation(e, e, ACT.Ln, bias=1.0).then_inc(fn_ready, 1)
                split_val(sp_hi[:], e)

            def sb_weights():
                act.wait_ge(att_free, b.next(TB) + BANKS)
                nc.scalar.activation(e, z, ACT.Exp).then_inc(act_step, 1)
                act.wait_ge(act_step, step.next())
                nc.scalar.activation(sp_hi[:], e, ACT.Copy).then_inc(hi_ready, 1)

            def sb_gated():
                for d in range(SB_VC):
                    act.wait_ge(att_free, b.next() + BANKS)
                    nc.scalar.activation(so_hi[:, d, :], s_gate[:, d, :], ACT.Copy).then_inc(hi_ready, 1)

            def sb_body(first, last):
                prep()
                sb_soft()
                s.next(2)
                if not first:
                    prep()
                for o in range(2):
                    act.wait_ge(acc_free, u.next() + BANKS)
                    nc.scalar.activation(s_gate[:, o, :], s_gate[:, o, :], ACT.Silu).then_inc(fn_ready, 1)
                if not first:
                    s.next(DC)
                    u.next(DC)
                sb_weights()
                if not last:
                    sb_kq(False)
                sb_gated()
                if not last:
                    sb_v(False)

            act_step, step = sem("act_step"), Count()
            sb_kq(True)
            sb_v(True)
            sb_body(True, False)
            with loop(act, SB_HEADS // 2 - 1, (n, 8), (s, 28), (u, 28), (b, 2 * (2 * TB + SB_VC)),
                      (val, 4), (step, 4)):
                for j in range(2):
                    sb_body(False, False)
            sb_body(False, True)
            for c in range(DC):
                act.wait_ge(acc_free, u.next() + BANKS)
                square(c, y_sb[:, c, :])
            std_of()

        @block.vector
        def _(dve):
            n, s, u, b = Count(), Count(), Count(), Count()
            fn, hi, step, sq, prob, mix, op, squared = (Count() for _ in range(8))
            tt = nc.vector.tensor_tensor
            stt = nc.vector.scalar_tensor_tensor

            def prep(cols=SLAB):
                slot = n.k % RING
                dve.wait_ge(w_hi_ready, n.at(1))
                tt(w_lo[:, slot, 0:cols], raw[:, slot, 0:cols], w_hi[:, slot, 0:cols].bitcast(F32), ALU.subtract).then_inc(w_ready, 1)
                n.next()

            def link(ins):
                ins.then_inc(dve_step, 1)
                dve.wait_ge(dve_step, step.next())

            def low(dst, src, hi_part, done=op_ready):
                dve.wait_ge(hi_ready, hi.next())
                tt(dst, src, hi_part.bitcast(F32), ALU.subtract).then_inc(done, 1)
                if done is op_ready:
                    op.next()

            def settle():
                dve.wait_ge(op_ready, op.at())

            def add_square(src, first, weight=None):
                if first:
                    tt(ssq[:], src, src, ALU.mult).then_inc(ssq_ready, 1)
                else:
                    dve.wait_ge(ssq_ready, sq.at())
                    link(tt(t(4), src, src, ALU.mult))
                    if weight is not None:
                        stt(gsq[:], t(4), weight, gsq[:], ALU.mult, ALU.add)
                    tt(ssq[:], ssq[:], t(4), ALU.add).then_inc(ssq_ready, 1)
                sq.next()

            def sum_square(c):
                dve.wait_ge(sq_ready, squared.next())
                if c == 0:
                    nc.vector.tensor_copy(ssq[:], t(0)).then_inc(ssq_ready, 1)
                else:
                    dve.wait_ge(ssq_ready, sq.at())
                    tt(ssq[:], ssq[:], t(c % 4), ALU.add).then_inc(ssq_ready, 1)
                sq.next()

            def rstd_of(skip=0, dst=rstd, std=5):
                dve.wait_ge(fn_ready, fn.next())
                nc.vector.reciprocal(dst[:], t(std)).then_inc(att_free, 1 + skip)
                dve.wait_ge(att_free, b.next(1 + skip) + BANKS)

            def weigh(dst, c, gain, hi_part):
                c = bass.ds(c, 1)
                dve.wait_ge(hi_ready, hi.next())
                stt(dst[:, c, :], h[:, c, :], gain[:, c], hi_part[:, c, :].bitcast(F32), ALU.mult, ALU.subtract).then_inc(op_ready, 1)
                op.next()

            def turn_rstd(blocks):
                dve.wait_ge(att_full, b.next())
                nc.vector.tensor_copy(r_tok[:, 0:blocks], att[:, (b.k - 1) % BANKS, 0:blocks]).then_inc(att_free, 1)

            def split_values(dst, hi_part, o, row, view):
                dve.wait_ge(hi_ready, hi.next())
                for j in range(2):
                    k = 2 * o + j
                    ins = stt(dst(k), view(acc[:, u.k % BANKS, 256 * j:256 * j + 256]), r_tok[:, row + k:row + k + 1], hi_part(k).bitcast(F32), ALU.mult, ALU.subtract)
                ins.then_inc(acc_free, 1)
                s.next()
                u.next()

            def ffn(next_gain, weights=None):
                def up(place, first):
                    for j in range(2):
                        prep()
                        if first and j == 0:
                            rstd_of()
                        dve.wait_ge(seg_done, s.next())
                        tt(t(j), acc[:, u.k % BANKS, :], rstd[:], ALU.mult).then_inc(acc_free, 1)
                        u.next()
                        dve.wait_ge(seg_done, s.next())
                        dve.wait_ge(fn_ready, fn.next())
                        tt(t(2 + j), t(j), acc[:, u.k % BANKS, :], ALU.mult).then_inc(acc_free, 1)
                        u.next()
                        low(g_lo[:, place(j), :], t(2 + j), g_hi[:, place(j), :])

                up(lambda j: j, True)
                with loop(dve, FC // 2 - 1, (n, 2), (s, 4), (u, 4), (fn, 2), (hi, 2), (op, 2)) as i:
                    up(lambda j: 2 * i + (j + 2), False)
                if weights is not None:
                    link(nc.vector.memset(gsq[:], 0.0))
                nc.vector.memset(ssq[:], 0.0).then_inc(ssq_ready, 1)
                sq.next()
                with loop(dve, DC // 4, (n, 8), (s, 8), (u, 4), (step, 4), (sq, 4), (hr, 4), (hi, 4), (op, 4)) as i:
                    for j in range(4):
                        c = 4 * i + j
                        prep()
                        prep()
                        dve.wait_ge(seg_done, s.next(2))
                        stt(t(5), acc[:, u.k % BANKS, :], 0.5, rstd[:], ALU.mult, ALU.mult).then_inc(acc_free, 1)
                        dve.wait_ge(acc_free, u.next() + BANKS)
                        tt(h[:, c, :], h[:, c, :], t(5), ALU.add).then_inc(h_ready, 1)
                        dve.wait_ge(h_ready, hr.next())
                        add_square(h[:, c, :], False, None if weights is None else weights[:, bass.ds(c, 1)])
                        weigh(x_lo, c, next_gain, x_hi)

            hr = Count()

            nc.vector.memset(eps[:], EPS).then_inc(w_ready, RING)
            nc.vector.memset(r_tok[:], 0.0).then_inc(acc_free, BANKS)
            dve.wait_ge(gains_landed, 16)
            for c in range(DC):
                sum_square(c)
                weigh(x_lo, c, gains[:, 0, :], x_hi)
                if c == 1:
                    prep()
            dve.wait_ge(const_landed, 6 * 16)
            nc.vector.tensor_copy(rot_r[:], signs[:, 0, :])
            nc.vector.tensor_copy(tri_r[:], signs[:, 1, :]).then_inc(att_free, BANKS)
            nc.vector.tensor_copy(ones_r[:], signs[:, 2, :]).then_inc(const_ready, 1)
            dve.wait_ge(const_ready, 1)
            ffn(gains[:, 1, :])

            dve.wait_ge(mix_landed, 5 * 16)

            def rope_split(o):
                cols = slice(o * TOK, (o + 1) * TOK)
                settle()
                low(stage_lo[:, cols], acc[:, u.k % BANKS, :], stage_hi[:, cols])
                tt(t(o), acc[:, u.k % BANKS, :], rope_a[:, 0, :], ALU.mult).then_inc(acc_free, 1)
                s.next()
                u.next()

            def rope_done(g, o, split_after):
                dve.wait_ge(att_full, b.next())
                tt(t(2 + o), att[:, (b.k - 1) % BANKS, :], rope_a[:, 1, :], ALU.mult).then_inc(att_free, 1)
                dve.wait_ge(att_free, b.at(BANKS))
                dve.wait_ge(acc_free, u.at(BANKS - split_after))
                tt(t(o), t(o), t(2 + o), ALU.add).then_inc(val_ready, 1)
                low(qk_lo[:, o, g, :], t(o), qk_hi[:, o, g, :])

            def qk(last):
                for g in range(N_GROUPS):
                    for o in range(2):
                        if o == 0:
                            prep()
                            if g == 0 and not last:
                                rstd_of()
                                tt(rope_a[:, 0, :], rope_a[:, 0, :], rstd[:], ALU.mult)
                                link(tt(rope_a[:, 1, :], rope_a[:, 1, :], rstd[:], ALU.mult))
                                turn_rstd(2 * TB)
                        rope_split(o)
                        if (g, o) != (0, 0):
                            rope_done(g - 1 + o, 1 - o, 1)
                        elif last:
                            gather(0)

            def scores(k):
                at = KEYS * (k % 2)
                dve.wait_ge(att_full, b.next(2))
                stt(tmp[:, at:at + TOK], att[:, (b.k - 2) % BANKS, :], HEAD ** -0.5, band[:, DIL - 1 - k // 2:DIL - 1 - k // 2 + TOK],
                    ALU.mult, ALU.add)
                stt(tmp[:, at + TOK:at + KEYS], att[:, (b.k - 1) % BANKS, 0:KEYS - TOK], HEAD ** -0.5,
                    classes[:].rearrange("p g c -> p (g c)"), ALU.mult, ALU.add).then_inc(att_free, 2)
                dve.wait_ge(att_free, b.at(BANKS))
                nc.vector.tensor_reduce(neg_max[:, k:k + 1], tmp[:, at:at + KEYS], AX_X, ALU.max,
                                        negate=True).then_inc(val_ready, 1)

            def mix_values(j, o):
                heads = slice(GROUP_HEADS * j, GROUP_HEADS * (j + 1))
                split_values(lambda k: va[:, k, heads, 1, :], lambda k: va[:, k, heads, 0, :], o, TB if j else 0, by_heads)

            def gather(a):
                dve.wait_ge(att_full, b.next())
                low(o_lo[:, a, :].rearrange("p (l r) -> p r l", r=DIL),
                    att[:, (b.k - 1) % BANKS, :].rearrange("p (r l) -> p r l", r=DIL),
                    o_hi[:, a, :].rearrange("p (l r) -> p r l", r=DIL), att_free)

            def normalizer(k):
                dve.wait_ge(prob_ready, prob.next())
                nc.vector.reciprocal(rden[:, k:k + 1], den[:, k:k + 1]).then_inc(rden_ready, 1)

            def attend(a, between=None):
                def low_probs(k):
                    bank = u.k + 2 * k
                    high, rest = (turned_probs[:, k % 2, :, i, :] for i in range(2))
                    dve.wait_ge(hi_ready, hi.next())
                    tt(rest[:, 0:TB, :], by_blocks(acc[:, bank % BANKS, :]), high[:, 0:TB, :].bitcast(F32), ALU.subtract)
                    dve.wait_ge(hi_ready, hi.next())
                    tt(rest[:, TB:, :], by_blocks(acc[:, (bank + 1) % BANKS, 0:KEYS - TOK]),
                       high[:, TB:, :].bitcast(F32), ALU.subtract).then_inc(stage_ready, 1)

                low_probs(0)
                for k in range(UNITS):
                    if k == UNITS - 2 and between is not None:
                        between()
                    if k + 2 < UNITS:
                        scores(k + 2)
                    if k + 1 < UNITS:
                        low_probs(k + 1)
                    if k + 2 < UNITS:
                        normalizer(k + 2)
                    dve.wait_ge(mixed, mix.next())
                    by_part = acc[:, (u.k + 2 * k + 1) % BANKS, KEYS - TOK:]
                    nc.vector.tensor_reduce(o_unit[:, k, :], by_part.rearrange("p (s q) -> p q s", s=2), AX_X,
                                            ALU.add).then_inc(acc_free, 2)
                u.next(2 * UNITS)

            qk(False)
            for i, window in enumerate(POOL_WINDOWS):
                if i % 2 == 0:
                    prep()
                if i == 0:
                    rope_done(N_GROUPS - 1, 1, 0)
                width = PAD + TOK
                rows = [tmp[:, k * width:(k + 1) * width] for k in range(3)]
                settle()
                link(nc.vector.memset(tmp[:, 0:3 * width].rearrange("p (k c) -> p k c", k=3)[:, :, 0:PAD], 0.0))
                dve.wait_ge(seg_done, s.next())
                tt(rows[0][:, PAD:], acc[:, u.k % BANKS, :], rstd[:], ALU.mult).then_inc(acc_free, 1)
                dve.wait_ge(acc_free, u.next() + BANKS)
                src, reach = rows[0], 1
                while reach < window:
                    dst = rows[2] if src is rows[1] else rows[1]
                    link(tt(dst[:, PAD:], src[:, PAD:], src[:, PAD - reach:width - reach], ALU.add))
                    src, reach = dst, 2 * reach
                diff = tmp[:, 3 * width:3 * width + TOK]
                link(stt(diff, src[:, PAD:], 1.0 / window, rows[0][:, PAD:], ALU.mult, ALU.subtract))
                link(tt(diff[:, 0:PAD], src[:, PAD:2 * PAD], rcount[:, i, :], ALU.mult))
                tt(diff[:, 0:PAD], diff[:, 0:PAD], rows[0][:, PAD:2 * PAD], ALU.subtract).then_inc(val_ready, 1)
                low(pool_lo[:, i, :], diff, pool_hi[:, i, :])
            prep()
            mix_values(0, 0)
            mix_values(0, 1)
            prep(4 * BLK)
            settle()
            scores(0)
            scores(1)

            def pooled():
                def scaled(i):
                    dve.wait_ge(seg_done, s.next())
                    nc.vector.tensor_scalar(t(3 + i % 3), acc[:, u.k % BANKS, :], pool_scale[:, i:i + 1], None,
                                            ALU.mult).then_inc(acc_free, 1)
                    u.next()

                for i in range(4):
                    if i < 3:
                        scaled(i)
                    else:
                        settle()
                        scaled(i)
                    if i:
                        low(pool_lo[:, i - 1, :], t(3 + (i - 1) % 3), pool_hi[:, i - 1, :])
                low(pool_lo[:, 3, :], t(3), pool_hi[:, 3, :])

            mix_values(1, 0)
            pooled()
            settle()
            normalizer(0)
            normalizer(1)
            mix_values(1, 1)
            attend(0, prep)
            qk(True)
            rope_done(N_GROUPS - 1, 1, 0)
            mix_values(2, 0)
            settle()
            scores(0)
            scores(1)
            normalizer(0)
            mix_values(2, 1)
            normalizer(1)
            attend(1, prep)
            gather(1)
            with loop(dve, DC // 4, (n, 6), (s, 16), (u, 16), (fn, 8), (hi, 4), (op, 4), (step, 4)) as i:
                for j in range(2):
                    prep()
                    settle()
                    for o in range(4):
                        dve.wait_ge(seg_done, s.next())
                        nc.vector.tensor_copy(t(o), acc[:, u.k % BANKS, :]).then_inc(acc_free, 1)
                        u.next()
                    dve.wait_ge(acc_free, u.at(BANKS))
                    for k in range(2):
                        prep()
                        for o in range(2):
                            dve.wait_ge(seg_done, s.next())
                            tt(t(4 + o), acc[:, u.k % BANKS, :], rstd[:], ALU.mult).then_inc(acc_free, 1)
                            u.next()
                        for o in range(2):
                            dve.wait_ge(fn_ready, fn.next())
                            ins = tt(t(2 * k + o), t(4 + o), t(2 * k + o), ALU.mult)
                        link(ins)
                        tt(t(2 * k), t(2 * k), t(2 * k + 1), ALU.add).then_inc(val_ready, 1)
                        low(m_lo[:, 4 * i + (2 * j + k), :], t(2 * k), m_hi[:, 4 * i + (2 * j + k), :])
            nc.vector.memset(ssq[:], 0.0).then_inc(ssq_ready, 1)
            sq.next()
            with loop(dve, DC // 4, (n, 2), (s, 4), (u, 4), (step, 4), (sq, 4), (hi, 4), (op, 4)) as i:
                for j in range(2):
                    prep()
                    for o in range(2):
                        c = 4 * i + (2 * j + o)
                        dve.wait_ge(seg_done, s.next())
                        tt(h[:, c, :], acc[:, u.k % BANKS, :], h[:, c, :], ALU.add).then_inc(acc_free, 1)
                        dve.wait_ge(acc_free, u.next() + BANKS)
                        add_square(h[:, c, :], False)
                        weigh(x_lo, c, gains[:, 2, :], x_hi)

            final, ret = gains[:, 3, :], gains[:, 4, :]
            tt(gain_sq[:], final, final, ALU.mult)
            tt(gain_ret[:], final, ret, ALU.mult)
            nc.vector.memset(eps_sq[:], EPS * EPS)
            link(nc.vector.tensor_scalar(mean_eps[:], mean_d[:], EPS, None, ALU.mult))
            ffn(gain_ret, gain_sq)

            def rope_products(o):
                dve.wait_ge(seg_done, s.next(2))
                settle()
                x1, x2 = acc[:, u.k % BANKS, :], acc[:, (u.k + 1) % BANKS, :]
                u.next(2)
                cos, sin = rope_b[:, 0, :], rope_b[:, 1, :]
                tt(t(0), x1, cos, ALU.mult)
                tt(t(1), x2, sin, ALU.mult)
                tt(t(2), x1, sin, ALU.mult)
                tt(t(3), x2, cos, ALU.mult).then_inc(acc_free, 2)

            def rope_sums(o, since=0):
                dve.wait_ge(acc_free, u.at(BANKS - since))
                tt(t(0), t(0), t(1), ALU.subtract).then_inc(val_ready, 1)
                tt(t(2), t(2), t(3), ALU.add).then_inc(val_ready, 1)
                for c in range(RET_KC):
                    low(rqk_lo[:, o, c, :], t(2 * c), rqk_hi[:, o, c, :])

            def ret_v(j):
                prep()
                for o in range(2):
                    split_values(lambda k: rv_lo[:, k:k + 1, 256 * j:256 * j + 256],
                                 lambda k: rv_hi[:, k:k + 1, 256 * j:256 * j + 256], o, 0, whole_row)

            def gate(dst):
                prep()
                for o in range(2):
                    dve.wait_ge(seg_done, s.next())
                    tt(dst[:, o, :], acc[:, u.k % BANKS, :], rstd[:], ALU.mult).then_inc(acc_free, 1)
                    u.next()

            def square_head():
                for c in range(RET_VC):
                    add_square(r_out[:, c, :], c == 0)

            def gated(first, last):
                for c in range(first, last):
                    dve.wait_ge(fn_ready, fn.next())
                    tt(r_gate[:, c, :], r_out[:, c, :], r_gate[:, c, :], ALU.mult).then_inc(val_ready, 1)

            def outputs(first, end, last):
                for c in range(first, end):
                    part = t(4 + c % 2)
                    dve.wait_ge(seg_done, s.next())
                    tt(part, acc[:, u.k % BANKS, :], r_head[:], ALU.mult).then_inc(acc_free, 1)
                    dve.wait_ge(acc_free, u.next() + BANKS)
                    tt(y_ret[:, c, :], part, y_ret[:, c, :], ALU.add).then_inc(val_ready, 1)
                    if last and c:
                        sum_square(c - 1)

            def ret_body(head, last):
                ret_v(0)
                settle()
                for m in range(TB):
                    dve.wait_ge(att_full, b.next())
                    tt(t(m, TRI[m]), att[:, (b.k - 1) % BANKS, 0:TRI[m]], decay[:, head, 0:TRI[m]],
                       ALU.mult).then_inc(att_free, 1)
                for m in range(TB):
                    cols = slice(TRI_AT[m], TRI_AT[m] + TRI[m])
                    low(rs_lo[:, cols], t(m, TRI[m]), rs_hi[:, cols])
                ret_v(1)
                for j in range(DC // RET_HEADS):
                    c = bass.ds(DC // RET_HEADS * head + j, 1)
                    ins = stt(h[:, c, :], h[:, c, :], final[:, c], r_final[:].unsqueeze(1), ALU.mult, ALU.mult)
                link(ins)
                if not last:
                    gate(r_gate[:, 0:2, :])
                for c in range(RET_VC):
                    dve.wait_ge(att_full, b.next())
                    nc.vector.tensor_copy(r_out[:, c, :], att[:, (b.k - 1) % BANKS, :]).then_inc(att_free, 1)
                dve.wait_ge(att_free, b.at(BANKS))
                link(tt(t(4), r_out[:, 0, :], r_out[:, 1, :], ALU.add))
                link(tt(t(4), t(4), r_out[:, 2, :], ALU.add))
                tt(t(4), t(4), r_out[:, 3, :], ALU.add).then_inc(op_ready, 1)
                op.next()
                gate(r_gate[:, 0:2, :] if last else r_gate[:, 2:4, :])
                dve.wait_ge(att_full, b.next())
                for c in range(RET_VC):
                    ins = tt(r_out[:, c, :], r_out[:, c, :], att[:, (b.k - 1) % BANKS, :], ALU.subtract)
                ins.then_inc(att_free, 1)
                dve.wait_ge(att_free, b.at(BANKS))
                if last:
                    square_head()
                    gated(0, 2)
                    gate(r_gate[:, 2:4, :])
                    gated(2, 4)
                else:
                    gated(0, 4)
                    prep()
                    square_head()
                for c in range(RET_VC):
                    low(rv_lo[:, c, :], r_gate[:, c, :], rv_hi[:, c, :])
                if not last:
                    rope_products(0)
                    prep()
                    rope_sums(0)
                    rope_products(1)
                prep()
                rstd_of(RET_SKIP, r_head)
                outputs(0, 2, last)
                if not last:
                    rope_sums(1)
                outputs(2, 4, last)
                if not last:
                    prep()
                outputs(4, DC, last)
                if last:
                    sum_square(DC - 1)
                    prep()

            dve.wait_ge(ret_landed, 2 * 16)
            dve.wait_ge(y_clear, 1)
            for o in range(2):
                prep()
                if o == 0:
                    rstd_of()
                    rstd_of(dst=r_final, std=4)
                    tt(rope_b[:, 0, :], rope_b[:, 0, :], rstd[:], ALU.mult)
                    link(tt(rope_b[:, 1, :], rope_b[:, 1, :], rstd[:], ALU.mult))
                    turn_rstd(TB)
                rope_products(o)
                rope_sums(o)
            with loop(dve, RET_HEADS - 1, (n, 8), (s, 20), (u, 20), (b, RET_BANKS), (fn, RET_VC + 1),
                      (hi, 4 + TB + RET_VC + 2 * RET_KC), (step, 1 + 2 + 3), (sq, RET_VC),
                      (op, TB + 1 + RET_VC + 2 * RET_KC)) as head:
                ret_body(head, False)
            ret_body(RET_HEADS - 1, True)

            def post_norm(y, gain, last):
                rstd_of()
                for c in range(DC + 2):
                    if c < DC:
                        stt(t(c % 4), y[:, c, :], gains[:, gain, c:c + 1], rstd[:], ALU.mult, ALU.mult).then_inc(dve_step, 1)
                        step.next()
                    if 1 <= c <= DC:
                        dve.wait_ge(dve_step, step.at(-1 if c < DC else 0))
                        tt(h[:, c - 1, :], h[:, c - 1, :], t((c - 1) % 4), ALU.add).then_inc(h_ready, 1)
                        hr.next()
                    if c >= 2 and not last:
                        dve.wait_ge(h_ready, hr.at(-1 if c <= DC else 0))
                        weigh(kv_lo, c - 2, gains[:, 6, :], kv_hi)

            settle()
            post_norm(y_ret, 5, False)

            for c in range(DC):
                weigh(x_lo, c, gains[:, 7, :], x_hi)

            def sb_kq(first):
                prep()
                if first:
                    rstd_of()
                for o in range(2):
                    low(skq_lo[:, o, :], acc[:, u.k % BANKS, :], skq_hi[:, o, :], acc_free)
                    s.next()
                    u.next()

            def sb_v(first):
                prep()
                if first:
                    turn_rstd(TB)
                    dve.wait_ge(att_free, b.at(BANKS))
                    link(nc.vector.tensor_scalar(z_scale[:], r_tok[:, 0:TB], float(P) ** -0.5, None, ALU.mult))
                for o in range(2):
                    split_values(lambda k: sv_lo[:, k:k + 1, :], lambda k: sv_hi[:, k:k + 1, :], o, 0, whole_row)

            def sb_out(first, last):
                for c in range(first, last):
                    dve.wait_ge(seg_done, s.next())
                    tt(y_sb[:, c, :], acc[:, u.k % BANKS, :], y_sb[:, c, :], ALU.add).then_inc(acc_free, 1)
                    u.next()

            z, e = tmp[:, 0:TRI_COLS], tmp[:, TRI_COLS:2 * TRI_COLS]

            def take_gate(o):
                dve.wait_ge(seg_done, s.next())
                tt(s_gate[:, o, :], acc[:, u.k % BANKS, :], rstd[:], ALU.mult).then_inc(acc_free, 1)
                u.next()

            def sb_body(first, last):
                settle()
                for m in range(TB):
                    bank = b.k % BANKS
                    dve.wait_ge(att_full, b.next())
                    stt(z[:, TRI_AT[m]:TRI_AT[m] + TRI[m]], att[:, bank, 0:TRI[m]], z_scale[:, m:m + 1], rstd[:, P * m:],
                        ALU.mult, ALU.mult).then_inc(att_free, 1)
                dve.wait_ge(att_free, b.at(BANKS))
                for m in range(TB):
                    diag = z[:, TRI_AT[m]:TRI_AT[m] + P]
                    ins = tt(diag, diag, diag_neg[:], ALU.add)
                link(ins)
                stt(e, z, -1.0, z, ALU.mult, ALU.min).then_inc(val_ready, 1)
                prep()
                if not first:
                    take_gate(0)
                    take_gate(1)
                dve.wait_ge(fn_ready, fn.next())
                stt(e, z, 0.0, e, ALU.max, ALU.add).then_inc(val_ready, 1)
                if not first:
                    sb_out(0, 2)
                low(sp_lo[:], e, sp_hi[:])
                if first:
                    take_gate(0)
                    take_gate(1)
                if not first:
                    sb_out(2, 4)
                    prep()
                if not first and not last:
                    sb_out(4, DC)
                settle()
                for m in range(TB):
                    zm = z[:, TRI_AT[m]:TRI_AT[m] + TRI[m]]
                    dve.wait_ge(att_full, b.next())
                    tt(zm, zm, att[:, (b.k - 1) % BANKS, 0:TRI[m]], ALU.subtract).then_inc(att_free, 1)
                if last:
                    sb_out(DC // 2, DC)
                low(sp_lo[:], e, sp_hi[:])
                if not last:
                    sb_kq(False)
                for d in range(SB_VC):
                    dve.wait_ge(att_full, b.next())
                    dve.wait_ge(fn_ready, fn.next())
                    tt(s_gate[:, d, :], s_gate[:, d, :], att[:, (b.k - 1) % BANKS, :], ALU.mult).then_inc(att_free, 1)
                for d in range(SB_VC):
                    low(so_lo[:, d, :], s_gate[:, d, :], so_hi[:, d, :])
                if first:
                    link(nc.vector.memset(y_sb[:], 0.0))
                if not last:
                    sb_v(False)

            sb_kq(True)
            sb_v(True)
            sb_body(True, False)
            with loop(dve, SB_HEADS // 2 - 1, (n, 8), (s, 28), (u, 28), (b, 2 * (2 * TB + SB_VC)),
                      (fn, 2 * (1 + SB_VC)), (hi, 2 * (2 + SB_VC + 4)), (op, 2 * (2 + SB_VC)), (step, 2)):
                for j in range(2):
                    sb_body(False, False)
            sb_body(False, True)
            settle()
            squared.next(DC)
            for c in range(DC):
                sb_out(c, c + 1)
                if c:
                    sum_square(c - 1)
            sum_square(DC - 1)
            post_norm(y_sb, 8, True)

        @block.tensor
        def _(pe):
            n, u, b = Count(), Count(), Count()
            op, sq, prob = Count(), Count(), Count()
            staged = Count()
            mm = nc.tensor.matmul

            def slab():
                pe.wait_ge(w_ready, n.at(RING + 1))
                slot = n.k % RING
                n.next()
                return lambda i, width=BLK: (w_hi[:, slot, i * width:(i + 1) * width],
                                             w_lo[:, slot, i * width:(i + 1) * width])

            def bank():
                pe.wait_ge(acc_free, u.at(1))
                u.next()
                return acc[:, (u.k - 1) % BANKS, :]

            def side_bank():
                pe.wait_ge(att_free, b.at(1))
                b.next()
                return att[:, (b.k - 1) % BANKS, :]

            def passes(dst, still, move, first, last):
                mm(dst, still[0], move[0], start=first, stop=False)
                mm(dst, still[0], move[1], start=False, stop=False)
                return mm(dst, still[1], move[0], start=False, stop=last)

            def project(w, first_block, x, chunks=DC, wait=None):
                dst = bank()
                for c in range(chunks):
                    if wait is not None:
                        pe.wait_ge(op_ready, op.at(wait - op.k + c + 1))
                    last = passes(dst, w(first_block + c), (x[0][:, c, :], x[1][:, c, :]), c == 0, c == chunks - 1)
                last.then_inc(seg_done, 1)

            def values(x, blocks, between={}):
                w = slab()
                for k in range(TB):
                    if k % 2 == 0:
                        dst = bank()
                    for c in range(DC):
                        last = passes(dst[:, 256 * (k % 2):256 * (k % 2) + 256],
                                      (x[0][:, c, blocks[k]], x[1][:, c, blocks[k]]), w(c, 256), c == 0, c == DC - 1)
                    if k % 2:
                        last.then_inc(seg_done, 1)
                    if k in between:
                        between[k]()

            def mean_square(skip=0, mean=mean_d):
                pe.wait_ge(ssq_ready, sq.at())
                dst = side_bank()
                b.next(skip)
                mm(dst, mean[:], ssq[:], start=True, stop=True).then_inc(att_full, 1 + skip)

            x = (x_hi, x_lo)

            def pair(wait=None, between=None):
                w = slab()
                dst = bank(), bank()
                for c in range(DC):
                    if between is not None and c == 5:
                        between()
                    if wait is not None:
                        pe.wait_ge(op_ready, wait + c + 1)
                    for o in range(2):
                        last = passes(dst[o], w(o * DC + c), (x[0][:, c, :], x[1][:, c, :]), c == 0, c == DC - 1)
                        if c == DC - 1:
                            last.then_inc(seg_done, 1)

            def turn_rstd(blocks):
                dst = side_bank()
                for k, tokens in enumerate(blocks):
                    last = mm(dst[:, k:k + 1], rstd[:, tokens], ident[:, 0:1], start=True, stop=True)
                last.then_inc(att_full, 1)

            def ffn(adds, between):
                sq.next(adds)
                at = op.k
                op.next(DC)
                pair(at, between)
                pair()
                op.next(2)
                with loop(pe, FC // 2 - 1, (n, 2), (u, 4), (op, 2)):
                    for j in range(2):
                        pair()
                    op.next(2)
                with loop(pe, DC // 4, (n, 8), (u, 4)):
                    for j in range(4):
                        dst = bank()
                        for half in range(2):
                            w = slab()
                            k0 = half * FC // 2
                            if j == 0:
                                pe.wait_ge(op_ready, op.at(k0 + FC // 2 - FC))
                            for k in range(FC // 2):
                                last = passes(dst, w(k), (g_hi[:, k0 + k, :], g_lo[:, k0 + k, :]),
                                              k0 + k == 0, k0 + k == FC - 1)
                            last.then_inc(seg_done, 1)

            def first_mean():
                pe.wait_ge(const_ready, 1)
                mean_square()

            ffn(DC, first_mean)

            plain = [slice(P * k, P * k + P) for k in range(TB)]
            strided = [slice(r, None, DIL) for r in range(DIL)]
            sq.next(1 + DC)
            normed = op.k
            op.next(DC)

            def rotate(o):
                dst = side_bank()
                cols = slice(o * TOK, (o + 1) * TOK)
                mm(dst, rot_r[:], stage_hi[:, cols], start=True, stop=False)
                mm(dst, rot_r[:], stage_lo[:, cols], start=False, stop=True).then_inc(att_full, 1)

            def qk(last):
                for g in range(N_GROUPS):
                    if g == 0 and not last:
                        pair(normed, mean_square)
                        pe.wait_ge(att_free, b.at(BANKS))
                        turn_rstd(plain + strided)
                    else:
                        w = slab()
                    for o in range(2):
                        if g or last:
                            project(w, o * DC, x)
                        if (g, o) != (0, 0):
                            pe.wait_ge(op_ready, op.next())
                            rotate(1 - o)
                            op.next()
                        elif last:
                            gather(units_done)

            def rotate_last():
                pe.wait_ge(op_ready, op.next())
                rotate(1)
                op.next()

            def gather(done):
                pe.wait_ge(acc_free, done)
                dst = side_bank()
                for j in range(2):
                    last = mm(dst.rearrange("p (r l) -> p r l", r=DIL), fold[:, HEAD * (1 - j):HEAD * (1 - j) + P],
                              o_unit[:, j::2, :], start=j == 0, stop=j == 1)
                last.then_inc(att_full, 1)

            def scores(k):
                r, rows = k // 2, slice(HEAD * (k % 2), HEAD * (k % 2) + HEAD)
                for g in range(N_GROUPS):
                    if g < 2:
                        dst = side_bank()
                    keys = slice(None) if g == 0 else strided[r]
                    width = TOK if g == 0 else P
                    at = P if g == 2 else 0
                    last = passes(dst[:, at:at + width],
                                  (qk_hi[rows, 0, g, strided[r]], qk_lo[rows, 0, g, strided[r]]),
                                  (qk_hi[rows, 1, g, keys], qk_lo[rows, 1, g, keys]), True, True)
                last.then_inc(att_full, 2)

            def attend(a):
                def turn(k):
                    pe.wait_ge(diag_ready, prob.next())
                    dst = bank(), bank()
                    for i in range(KEYS // P):
                        at = KEYS * (k % 2) + P * i
                        last = mm(dst[i // TB][:, P * (i % TB):P * (i % TB) + P], tmp[:, at:at + P], diag[:, k % 2, :],
                                  start=True, stop=True)
                        if i % TB == TB - 1:
                            last.then_inc(turned, 1)
                    last.then_inc(turned, 1)

                first, values_in = u.k, u.at(BANKS)
                turn(0)
                for k in range(UNITS):
                    if k + 2 < UNITS:
                        scores(k + 2)
                    if k + 1 < UNITS:
                        turn(k + 1)
                    if k == 0:
                        pe.wait_ge(acc_free, values_in)
                    pe.wait_ge(stage_ready, staged.next())
                    dst = acc[:, (first + 2 * k + 1) % BANKS, KEYS - TOK:]
                    head = 2 * a + k % 2
                    for i in range(KEYS // P):
                        g, k_blk = (0, i) if i < TB else (i - TB + 1, k // 2)
                        last = mm(dst, va[:, k_blk, value_slot(g, head)].rearrange("p s d -> p (s d)"),
                                  turned_probs[:, k % 2, i].rearrange("p s q -> p (s q)"),
                                  start=i == 0, stop=i == KEYS // P - 1)
                    last.then_inc(mixed, 1)

            qk(False)
            for i in range(4):
                if i % 2 == 0:
                    w = slab()
                project(w, DC * (i % 2), x)
                if i == 0:
                    rotate_last()
            values(x, plain)

            def first_scores():
                pe.wait_ge(op_ready, op.at())
                scores(0)
                scores(1)

            first_scores()

            def pooled():
                w = slab()
                for i in range(4):
                    pe.wait_ge(op_ready, op.next())
                    passes(bank(), w(i), (pool_hi[:, i, :], pool_lo[:, i, :]), True, True).then_inc(seg_done, 1)
                op.next(4)

            values(x, strided, {1: pooled})
            attend(0)
            units_done = u.k + BANKS
            qk(True)
            values(x, strided, {1: rotate_last, 3: first_scores})
            attend(1)
            gather(u.at(BANKS))
            with loop(pe, DC // 4, (n, 6), (u, 16)):
                for j in range(2):
                    w = slab()
                    for k in range(2):
                        project(w, 6 * k + 2, (pool_hi, pool_lo), 4)
                        if j == 0 and k == 0:
                            pe.wait_ge(att_free, b.at(BANKS))
                        project(w, 6 * k, (o_hi, o_lo), 2)
                    for k in range(2):
                        w = slab()
                        project(w, DC, x)
                        project(w, 0, x)
            at = op.k
            op.next(DC)
            with loop(pe, DC // 4, (n, 2), (u, 4)):
                for j in range(2):
                    w = slab()
                    project(w, 0, (m_hi, m_lo), wait=at if j == 0 else None)
                    project(w, DC, (m_hi, m_lo))

            ffn(1 + DC, mean_square)

            sq.next(1 + DC)

            def both_norms():
                pe.wait_ge(ssq_ready, sq.at())
                dst = side_bank()
                mm(dst, mean_d[:], gsq[:], start=True, stop=False)
                mm(dst, mean_eps[:], ssq[:], start=False, stop=True).then_inc(att_full, 1)
                mean_square()

            normed = op.k
            op.next(DC)

            def ret_body(last):
                values(x, plain)
                pe.wait_ge(op_ready, op.at())
                for m in range(TB):
                    dst = side_bank()
                    for c in range(RET_KC):
                        ins = passes(dst[:, 0:TRI[m]], (rqk_hi[:, 1, c, plain[m]], rqk_lo[:, 1, c, plain[m]]),
                                     (rqk_hi[:, 0, c, P * m:], rqk_lo[:, 0, c, P * m:]), c == 0, c == RET_KC - 1)
                    ins.then_inc(att_full, 1)
                values(x, plain)
                if not last:
                    pair()
                op.next(TB)
                pe.wait_ge(op_ready, op.at())
                pe.wait_ge(acc_free, u.at(BANKS - (0 if last else 2)))
                for c in range(RET_VC):
                    dst = side_bank()
                    for m in range(TB):
                        cols = slice(TRI_AT[m], TRI_AT[m] + TRI[m])
                        ins = passes(dst[:, P * m:], (rv_hi[:, m, P * c:P * c + P], rv_lo[:, m, P * c:P * c + P]),
                                     (rs_hi[:, cols], rs_lo[:, cols]), m == 0, m == TB - 1)
                    ins.then_inc(att_full, 1)
                pair()
                pe.wait_ge(op_ready, op.next())
                mm(side_bank(), mean_v[:], t(4), start=True, stop=True).then_inc(att_full, 1)
                pair()
                if not last:
                    pair()
                sq.next(RET_VC)
                mean_square(RET_SKIP, mean_v)
                normed = op.k
                op.next(RET_VC)
                if not last:
                    op.next(2 * RET_KC)
                for j in range(2):
                    w = slab()
                    for o in range(4):
                        project(w, 4 * o, (rv_hi, rv_lo), 4, wait=normed if j + o == 0 else None)

            for o in range(2):
                if o == 0:
                    pair(normed, both_norms)
                    pe.wait_ge(att_free, b.at(BANKS - 1))
                    turn_rstd(plain)
                else:
                    pair()
                op.next(RET_KC)
            with loop(pe, RET_HEADS - 1, (n, 8), (u, 20), (b, RET_BANKS), (op, TB + 1 + RET_VC + 2 * RET_KC),
                      (sq, RET_VC)):
                ret_body(False)
            ret_body(True)
            sq.next(DC)
            mean_square()

            kv = (kv_hi, kv_lo)

            def sb_kq():
                w = slab()
                project(w, 0, kv)
                project(w, DC, x)

            def sb_out(w, first=0, last=DC):
                for c in range(first, last):
                    project(w, SB_VC * c, (so_hi, so_lo), SB_VC)

            def sb_body(first, last):
                pe.wait_ge(acc_free, u.at(BANKS - 2))
                for m in range(TB):
                    passes(side_bank()[:, 0:TRI[m]], (skq_hi[:, 0, plain[m]], skq_lo[:, 0, plain[m]]),
                           (skq_hi[:, 1, P * m:], skq_lo[:, 1, P * m:]), True, True).then_inc(att_full, 1)
                pair()
                if not first:
                    pe.wait_ge(op_ready, op.at())
                    w = slab()
                    sb_out(w, 0, DC // 2 if last else DC)
                pe.wait_ge(op_ready, op.next())
                for m in range(TB):
                    dst = side_bank()
                    for k in range(m, TB):
                        cols = slice(TRI_AT[k], TRI_AT[k] + TRI[k])
                        still = tri_r if k == m else ones_r
                        mm(dst[:, P * (k - m):TRI[m]], still[:], sp_hi[:, cols], start=k == m, stop=False)
                        ins = mm(dst[:, P * (k - m):TRI[m]], still[:], sp_lo[:, cols], start=False, stop=k == TB - 1)
                    ins.then_inc(att_full, 1)
                if last:
                    sb_out(w, DC // 2)
                else:
                    sb_kq()
                pe.wait_ge(op_ready, op.next())
                pe.wait_ge(acc_free, u.at(BANKS - 2 - (0 if first else DC) - (0 if last else 2)))
                for d in range(SB_VC):
                    dst = side_bank()
                    for m in range(TB):
                        cols = slice(TRI_AT[m], TRI_AT[m] + TRI[m])
                        ins = passes(dst[:, P * m:], (sv_hi[:, m, P * d:P * d + P], sv_lo[:, m, P * d:P * d + P]),
                                     (sp_hi[:, cols], sp_lo[:, cols]), m == 0, m == TB - 1)
                    ins.then_inc(att_full, 1)
                if not last:
                    values(kv, plain)
                op.next(SB_VC)

            w = slab()
            project(w, 0, kv, wait=op.k)
            op.next(DC)
            dst = side_bank()
            for c in range(DC):
                pe.wait_ge(sq_ready, 2 * DC + c + 1)
                ins = mm(dst, mean_d[:], y_ret[:, c, :], start=c == 0, stop=c == DC - 1)
            ins.then_inc(att_full, 1)
            project(w, DC, x, wait=op.k)
            op.next(DC)
            values(kv, plain)
            pe.wait_ge(att_free, b.at(BANKS))
            turn_rstd(plain)
            sb_body(True, False)
            with loop(pe, SB_HEADS // 2 - 1, (n, 8), (u, 28), (b, 2 * (2 * TB + SB_VC)), (op, 2 * (2 + SB_VC))):
                for j in range(2):
                    sb_body(False, False)
            sb_body(False, True)
            pe.wait_ge(op_ready, op.at())
            sb_out(slab())
            sq.next(DC)
            mean_square()



def tiles(w):
    k, n = w.shape
    return w.reshape(k // P, P, n // P, P).transpose(2, 1, 0, 3)


def columns(w, first, width):
    return w[:, first:first + width].reshape(-1, P, width).transpose(1, 0, 2)


def lay_out(a):
    w = {}
    for f in ("ffn1", "ffn2"):
        up, lin = tiles(a[f + "_w1"][0]), tiles(a[f + "_w3"][0])
        w[f + "_up"] = np.stack([up, lin], 2).reshape(FC, P, SLAB)
        down = tiles(a[f + "_w2"][0]).reshape(DC, P, 2, FC // 2 * BLK)
        w[f + "_down"] = down.transpose(0, 2, 1, 3).reshape(2 * DC, P, FC // 2 * BLK)
    w_in = a["w_in"][0]
    heads = N_GROUPS * GROUP_HEADS * HEAD
    cols = tiles(w_in)
    qc = heads // P
    w["mix_qk"] = np.stack([np.stack([np.stack([cols[2 * g + c], cols[qc + 2 * g + c]], 1)
                                      for g in range(N_GROUPS)]) for c in range(2)]).reshape(2, N_GROUPS, P, SLAB)
    v_cols = columns(w_in, 2 * heads, heads).reshape(P, DC, N_GROUPS, 2, 2 * HEAD)
    w["mix_v"] = np.stack([v_cols[:, :, 0], v_cols[:, :, 1:, 0], v_cols[:, :, 1:, 1]]).reshape(N_GROUPS, P, SLAB)
    pc, gc = 3 * qc, 3 * qc + len(POOL_WINDOWS)
    w["mix_pool"] = cols[pc:gc].reshape(2, 2, P, DC * BLK).transpose(0, 2, 1, 3).reshape(2, P, SLAB)
    w["pool_w"] = a["pool_w"][0].transpose(1, 0, 2).reshape(P, 4 * BLK)
    w["mix_branch"] = np.concatenate([tiles(a["w_branch_attn"][0]), tiles(a["w_branch_pool"][0])], 2)
    w["mix_branch"] = w["mix_branch"].reshape(DC // 2, 2, P, 6 * BLK).transpose(0, 2, 1, 3).reshape(DC // 2, P, 12 * BLK)
    w["mix_gate"] = np.stack([cols[gc:gc + DC], cols[gc + DC:gc + 2 * DC]], 2).reshape(DC, P, SLAB)

    def pairs(c):
        return c.reshape(-1, 2, P, DC * BLK).transpose(0, 2, 1, 3).reshape(-1, P, SLAB)

    w["mix_out"] = pairs(tiles(a["w_out"][0]))
    r = a["ret_w_in_2"][0]
    rp = pairs(tiles(r))
    keys = RET_HEADS * RET_KC * P
    vals = RET_HEADS * RET_VC * P
    gates = (2 * keys + vals) // 256
    w["ret_head"] = np.stack([np.stack(
        [rp[i], rp[RET_HEADS + i]]
        + [columns(r, 2 * keys + TOK * i + 256 * j, 256).reshape(P, SLAB) for j in range(2)]
        + [rp[gates + 2 * i + j] for j in range(2)]) for i in range(RET_HEADS)])
    ro = tiles(a["ret_w_out_2"][0])
    w["ret_out"] = np.stack([np.stack([ro[4 * j:4 * j + 4, :, RET_VC * i:RET_VC * (i + 1)].transpose(1, 0, 2, 3).reshape(P, SLAB)
                                       for j in range(2)]) for i in range(RET_HEADS)])
    kv, sbi, sbo = a["w_kv_2"], a["sb_w_in_2"][0], tiles(a["sb_w_out_2"][0])
    kt, st = tiles(kv), tiles(sbi)
    w["sb_kq"] = np.stack([kt[:SB_HEADS], st[:SB_HEADS]], 2).reshape(SB_HEADS, P, SLAB)
    w["sb_v"] = np.stack([columns(kv, SB_HEADS * P + 256 * i, 256) for i in range(SB_HEADS)]).reshape(SB_HEADS, P, SLAB)
    w["sb_g"] = pairs(st[SB_HEADS:])
    w["sb_out"] = np.stack([sbo[:, :, SB_VC * i:SB_VC * (i + 1)].transpose(1, 0, 2, 3).reshape(P, SLAB) for i in range(SB_HEADS)])
    w["x"] = a["x"][0].T.reshape(DC, P, TOK).transpose(1, 0, 2)
    w["gains"] = np.stack([a[g].reshape(DC, P).T for g in GAINS], 1)
    w["pool_scale"] = a["pool_scale"][0].reshape(-1, P).T
    return w


def constants():
    f = np.float32
    c = {"ident": np.eye(P, dtype=f), "mean_d": np.full((P, P), 1 / D, f), "mean_v": np.full((P, P), 1 / TOK, f)}
    i, j = np.arange(P)[:, None], np.arange(P)[None, :]
    c["diag_neg"] = np.where(i >= j, f(NEG), f(0))
    half = HEAD // 8
    rot = np.zeros((P, P), f)
    for m in range(P):
        d = m % HEAD
        if d < half:
            rot[m + half, m] = -1
        elif d < 2 * half:
            rot[m - half, m] = 1
    c["fold"] = np.hstack([np.zeros((P, HEAD), f), np.vstack([np.eye(HEAD, dtype=f)] * 2), np.zeros((P, HEAD), f)])
    c["signs"] = np.stack([rot, (i >= j).astype(f), np.ones((P, P), f)], 1)
    pos = np.arange(TOK, dtype=f)
    inv = (f(500000.0) ** (-np.arange(0, 2 * half, 2, dtype=f) / f(2 * half))).astype(f)
    cos, sin = np.ones((P, TOK), f), np.zeros((P, TOK), f)
    for m in range(P):
        if m % HEAD < 2 * half:
            ang = pos * inv[m % HEAD % half]
            cos[m], sin[m] = np.cos(ang), np.sin(ang)
    c["rope_a"] = np.stack([cos, sin], 1)
    dist = DIL * np.arange(P)[:, None] + DIL - 1 - np.arange(TOK + DIL - 1)[None, :]
    c["band"] = np.where((dist >= 0) & (dist <= 128), f(0), f(NEG)).astype(mybir.dt.np(mybir.dt.bfloat16))
    c["classes"] = np.stack([np.where(j <= i, f(0), f(NEG)),
                             np.where((j <= i) & ((i - j) % 4 == 0), f(0), f(NEG))], 1)
    first = np.arange(1, PAD + 1, dtype=f)
    c["rcount"] = np.broadcast_to(np.stack([f(1) / np.minimum(first, f(w)) for w in POOL_WINDOWS]), (P, 4, PAD)).astype(f)
    freq = (f(1) / (f(10000.0) ** (np.arange(P, dtype=f) / f(P)))).astype(f)
    ang = pos[None, :] * freq[:, None]
    c["rope_b"] = np.stack([np.cos(ang), np.sin(ang)], 1)
    lag = np.arange(TOK)[None, :] - np.arange(P)[:, None]
    gam = np.log1p(-np.exp2(-5.0 - np.arange(RET_HEADS)))
    dec = np.where(lag[:, None, :] >= 0, np.exp(gam[None, :, None] * np.maximum(lag, 0)[:, None, :]), 0)
    c["decay"] = (dec * (RET_KC * P) ** -0.5).astype(f)
    return c


def kernel(**inputs):
    import concourse.bacc as bacc
    from concourse.bass_utils import run_bass_kernel_spmd

    laid = lay_out({k: np.asarray(v) for k, v in inputs.items()})
    laid.update(constants())
    nc = bacc.Bacc("TRN2", target_bir_lowering=False, num_devices=1)
    arrays, dram = {}, {}
    for name, a in laid.items():
        a = np.ascontiguousarray(a)
        arrays[f"in_{name}"] = a
        dram[name] = nc.dram_tensor(f"in_{name}", a.shape, mybir.dt.from_np(a.dtype), kind="ExternalInput").ap()
    out = nc.dram_tensor("result", (P, DC, TOK), F32, kind="ExternalOutput").ap()
    block_kernel(nc, dram, out)
    got = run_bass_kernel_spmd(nc, [arrays], core_ids=[0]).results[0]["result"]
    return np.ascontiguousarray(got.transpose(1, 0, 2).reshape(D, TOK).T)[None]
```
